# Optimizing a Trainium2 kernel written in Bass

```python
import math
import jax, jax.numpy as jnp
from jax import lax
import numpy as np

D_MODEL = 1024
BATCH = 1
SEQ = 256
DEPTH = 2

N_MIXERS = 2
N_LAYERS_A = (DEPTH + 1) // 2
N_LAYERS_B = DEPTH // 2

A_HEADS = 4
A_QK_DIM = D_MODEL // (2 * A_HEADS)
A_V_DIM = D_MODEL // A_HEADS
A_CHUNK = 128
A_HQ = A_HEADS * A_QK_DIM
A_HV = A_HEADS * A_V_DIM
A_IN_COLS = 2 * A_HQ + 2 * A_HV + 2 * A_HEADS

B_HEADS = 8
B_HEAD_DIM = D_MODEL // (2 * B_HEADS)
B_V_DIM = 2 * B_HEAD_DIM
B_ROT_DIM = B_HEAD_DIM // 4
ROPE_THETA = 500000.0
Q_BLOCK = 128
B_IN_COLS = 3 * D_MODEL

N_EXPERTS = 16
N_GROUPS = 4
EXPERTS_PER_GROUP = N_EXPERTS // N_GROUPS
TOP_K = 2
D_EXPERT = 512
MOE_BLOCK = 128

EPS = 1e-6


def _rms(x, g):
    xf = x.astype(jnp.float32)
    y = xf * lax.rsqrt(jnp.mean(xf * xf, axis=-1, keepdims=True) + EPS)
    return y * g.astype(jnp.float32)

def _chunks(t):
    b_, h_, s_ = t.shape[:3]
    t = t.reshape(b_, h_, s_ // A_CHUNK, A_CHUNK, *t.shape[3:])
    return jnp.moveaxis(t, 2, 0)

def _mlstm_chunkwise(q, k, v, i_pre, log_f):
    b_, h_, s_, dk = q.shape
    dv = v.shape[-1]
    causal = jnp.tril(jnp.ones((A_CHUNK, A_CHUNK), dtype=bool))

    def step(carry, inp):
        C, n, m = carry
        qc, kc, vc, ic, fc = inp
        b = jnp.cumsum(fc, axis=-1)
        log_d = b[..., :, None] - b[..., None, :] + ic[..., None, :]
        log_d = jnp.where(causal, log_d, -jnp.inf)
        log_inter = b + m[..., None]
        m_t = jnp.maximum(jnp.max(log_d, axis=-1), log_inter)
        d = jnp.exp(log_d - m_t[..., None])
        inter = jnp.exp(log_inter - m_t)
        s = jnp.einsum('bhtd,bhsd->bhts', qc, kc) * d
        num = jnp.einsum('bhts,bhsv->bhtv', s, vc) + inter[..., None] * jnp.einsum('bhtd,bhdv->bhtv', qc, C)
        den = jnp.sum(s, axis=-1) + inter * jnp.einsum('bhtd,bhd->bht', qc, n)
        h = num / jnp.maximum(jnp.abs(den), jnp.exp(-m_t))[..., None]
        b_last = b[..., -1]
        log_w = b_last[..., None] - b + ic
        m_new = jnp.maximum(b_last + m, jnp.max(log_w, axis=-1))
        w = jnp.exp(log_w - m_new[..., None])
        decay = jnp.exp(b_last + m - m_new)
        kw = kc * w[..., None]
        C_new = decay[..., None, None] * C + jnp.einsum('bhsd,bhsv->bhdv', kw, vc)
        n_new = decay[..., None] * n + jnp.sum(kw, axis=2)
        return (C_new, n_new, m_new), h

    init = (jnp.zeros((b_, h_, dk, dv), jnp.float32), jnp.zeros((b_, h_, dk), jnp.float32),
            jnp.zeros((b_, h_), jnp.float32))
    _, hs = lax.scan(step, init, (_chunks(q), _chunks(k), _chunks(v), _chunks(i_pre), _chunks(log_f)))
    return jnp.moveaxis(hs, 0, 2).reshape(b_, h_, s_, dv)

def _mlstm_mixer(h, w_in, b_if, h_norm, w_out):
    b_, s_, _ = h.shape
    proj = h @ w_in.astype(h.dtype)
    q = proj[..., :A_HQ].reshape(b_, s_, A_HEADS, A_QK_DIM)
    k = proj[..., A_HQ:2 * A_HQ].reshape(b_, s_, A_HEADS, A_QK_DIM)
    v = proj[..., 2 * A_HQ:2 * A_HQ + A_HV].reshape(b_, s_, A_HEADS, A_V_DIM)
    o = proj[..., 2 * A_HQ + A_HV:2 * A_HQ + 2 * A_HV]
    gates = proj[..., 2 * A_HQ + 2 * A_HV:].astype(jnp.float32) + b_if.astype(jnp.float32)
    i_pre = jnp.transpose(gates[..., :A_HEADS], (0, 2, 1))
    log_f = jax.nn.log_sigmoid(jnp.transpose(gates[..., A_HEADS:], (0, 2, 1)))
    q = jnp.transpose(q, (0, 2, 1, 3)).astype(jnp.float32)
    k = jnp.transpose(k, (0, 2, 1, 3)).astype(jnp.float32) * (A_QK_DIM ** -0.5)
    v = jnp.transpose(v, (0, 2, 1, 3)).astype(jnp.float32)
    hout = _mlstm_chunkwise(q, k, v, i_pre, log_f)
    hout = _rms(jnp.transpose(hout, (0, 2, 1, 3)), h_norm.reshape(A_HEADS, A_V_DIM))
    hout = hout.reshape(b_, s_, A_HV) * jax.nn.sigmoid(o.astype(jnp.float32))
    return hout.astype(h.dtype) @ w_out.astype(h.dtype)

def _partial_rope(t, positions):
    half = B_ROT_DIM // 2
    inv_freq = ROPE_THETA ** (-jnp.arange(0, B_ROT_DIM, 2, dtype=jnp.float32) / B_ROT_DIM)
    ang = positions.astype(jnp.float32)[..., None] * inv_freq
    cos = jnp.cos(ang)[:, :, None, None, :]
    sin = jnp.sin(ang)[:, :, None, None, :]
    x1 = t[..., :half]
    x2 = t[..., half:B_ROT_DIM]
    return jnp.concatenate([x1 * cos - x2 * sin, x2 * cos + x1 * sin, t[..., B_ROT_DIM:]], axis=-1)

def _diff_attention(h, positions, w_in, q_norm, k_norm, lam_q1, lam_k1, lam_q2, lam_k2, o_norm, w_out, layer_idx):
    b_, s_, _ = h.shape
    proj = h @ w_in.astype(h.dtype)
    q = proj[..., :D_MODEL].reshape(b_, s_, B_HEADS, 2, B_HEAD_DIM)
    k = proj[..., D_MODEL:2 * D_MODEL].reshape(b_, s_, B_HEADS, 2, B_HEAD_DIM)
    v = proj[..., 2 * D_MODEL:].reshape(b_, s_, B_HEADS, B_V_DIM).astype(jnp.float32)
    q = _partial_rope(_rms(q, q_norm), positions)
    k = _partial_rope(_rms(k, k_norm), positions)
    q = jnp.transpose(q, (0, 2, 3, 1, 4)) * (B_HEAD_DIM ** -0.5)
    k = jnp.transpose(k, (0, 2, 3, 1, 4))
    v = jnp.transpose(v, (0, 2, 1, 3))
    lam_init = 0.8 - 0.6 * math.exp(-0.3 * layer_idx)
    lam = (jnp.exp(jnp.sum(lam_q1.astype(jnp.float32) * lam_k1.astype(jnp.float32)))
           - jnp.exp(jnp.sum(lam_q2.astype(jnp.float32) * lam_k2.astype(jnp.float32))) + lam_init)
    outs = []
    for j in range(s_ // Q_BLOCK):
        s0 = j * Q_BLOCK
        e = s0 + Q_BLOCK
        sc = jnp.einsum('bhcqd,bhckd->bhcqk', q[:, :, :, s0:e], k[:, :, :, :e])
        mask = (s0 + jnp.arange(Q_BLOCK))[:, None] >= jnp.arange(e)[None, :]
        p = jax.nn.softmax(jnp.where(mask, sc, -jnp.inf), axis=-1)
        a = p[:, :, 0] - lam * p[:, :, 1]
        outs.append(jnp.einsum('bhqk,bhkv->bhqv', a, v[:, :, :e]))
    o = jnp.concatenate(outs, axis=2)
    o = _rms(o, o_norm) * (1.0 - lam_init)
    o = jnp.transpose(o, (0, 2, 1, 3)).reshape(b_, s_, D_MODEL)
    return o.astype(h.dtype) @ w_out.astype(h.dtype)

def _grouped_moe(h, w_router, router_bias, w_gu, w_down):
    b_, s_, d_ = h.shape
    n_tok = b_ * s_
    xt = h.reshape(n_tok, d_)
    scores = jax.nn.sigmoid((xt @ w_router.astype(h.dtype)).astype(jnp.float32))
    biased = (scores + router_bias.astype(jnp.float32)).reshape(n_tok, N_GROUPS, EXPERTS_PER_GROUP)
    grp_score = jnp.sum(lax.top_k(biased, 2)[0], axis=-1)
    g_sel = jnp.argmax(grp_score, axis=-1)
    in_grp = jnp.take_along_axis(biased, g_sel[:, None, None], axis=1)[:, 0]
    _, local_idx = lax.top_k(in_grp, TOP_K)
    expert_idx = g_sel[:, None].astype(jnp.int32) * EXPERTS_PER_GROUP + local_idx.astype(jnp.int32)
    gate_w = jnp.take_along_axis(scores, expert_idx, axis=1)
    gate_w = gate_w / jnp.sum(gate_w, axis=-1, keepdims=True)
    n_assign = n_tok * TOP_K
    n_blocks = (n_assign + N_EXPERTS * (MOE_BLOCK - 1) + MOE_BLOCK - 1) // MOE_BLOCK
    cap = n_blocks * MOE_BLOCK
    flat_e = expert_idx.reshape(n_assign)
    flat_tok = jnp.repeat(jnp.arange(n_tok, dtype=jnp.int32), TOP_K)
    order = jnp.argsort(flat_e, stable=True)
    sorted_e = flat_e[order]
    sorted_tok = flat_tok[order]
    sorted_w = gate_w.reshape(n_assign)[order]
    counts = jnp.bincount(flat_e, length=N_EXPERTS).astype(jnp.int32)
    starts = jnp.cumsum(counts) - counts
    padded = ((counts + MOE_BLOCK - 1) // MOE_BLOCK) * MOE_BLOCK
    pad_ends = jnp.cumsum(padded)
    pad_starts = pad_ends - padded
    dest = pad_starts[sorted_e] + (jnp.arange(n_assign, dtype=jnp.int32) - starts[sorted_e])
    buf_tok = jnp.full((cap,), n_tok, jnp.int32).at[dest].set(sorted_tok)
    x_pad = jnp.concatenate([xt, jnp.zeros((1, d_), xt.dtype)], axis=0)
    xb = x_pad[buf_tok].reshape(n_blocks, MOE_BLOCK, d_)
    block_e = jnp.minimum(jnp.searchsorted(pad_ends, jnp.arange(n_blocks, dtype=jnp.int32) * MOE_BLOCK, side='right'),
                          N_EXPERTS - 1)

    def expert_block(args):
        xblk, e = args
        gu = xblk @ w_gu[e].astype(xblk.dtype)
        act = jax.nn.silu(gu[:, :D_EXPERT]) * gu[:, D_EXPERT:]
        return act @ w_down[e].astype(xblk.dtype)

    yb = lax.map(expert_block, (xb, block_e)).reshape(cap, d_)
    contrib = yb[dest].astype(jnp.float32) * sorted_w[:, None]
    y = jax.ops.segment_sum(contrib, sorted_tok, num_segments=n_tok)
    return y.reshape(b_, s_, d_).astype(h.dtype)

def first_inputs(seed: int = 0) -> dict:
    key = jax.random.key(seed)
    ks = jax.random.split(key, 24)
    f32 = jnp.float32
    nrm = lambda k, shape, s: jax.random.normal(k, shape, f32) * s
    offs = jax.random.randint(ks[2], (BATCH, 1), 0, 4096, dtype=jnp.int32)
    positions = offs + jnp.arange(SEQ, dtype=jnp.int32)[None, :]
    f_bias = jnp.linspace(3.0, 6.0, A_HEADS, dtype=f32)[None, :] + nrm(ks[8], (N_LAYERS_A, A_HEADS), 0.1)
    i_bias = nrm(ks[9], (N_LAYERS_A, A_HEADS), 0.1)
    return {
        "x": nrm(ks[0], (BATCH, SEQ, D_MODEL), 1.0),
        "c": nrm(ks[1], (BATCH, D_MODEL), 1.0),
        "positions": positions,
        "norm1": 1.0 + nrm(ks[3], (DEPTH, D_MODEL), 0.02),
        "norm2": 1.0 + nrm(ks[4], (DEPTH, D_MODEL), 0.02),
        "w_ada": nrm(ks[5], (DEPTH, D_MODEL, 6 * D_MODEL), 0.5 * D_MODEL ** -0.5),
        "b_ada": nrm(ks[6], (DEPTH, 6 * D_MODEL), 0.02),
        "a_w_in": nrm(ks[7], (N_LAYERS_A, D_MODEL, A_IN_COLS), D_MODEL ** -0.5),
        "a_b_if": jnp.concatenate([i_bias, f_bias], axis=-1),
        "a_h_norm": 1.0 + nrm(ks[10], (N_LAYERS_A, A_HV), 0.02),
        "a_w_out": nrm(ks[11], (N_LAYERS_A, A_HV, D_MODEL), A_HV ** -0.5),
        "b_w_in": nrm(ks[12], (N_LAYERS_B, D_MODEL, B_IN_COLS), D_MODEL ** -0.5),
        "b_q_norm": 1.0 + nrm(ks[13], (N_LAYERS_B, B_HEAD_DIM), 0.02),
        "b_k_norm": 1.0 + nrm(ks[14], (N_LAYERS_B, B_HEAD_DIM), 0.02),
        "b_lam_q1": nrm(ks[15], (N_LAYERS_B, B_HEAD_DIM), 0.1),
        "b_lam_k1": nrm(ks[16], (N_LAYERS_B, B_HEAD_DIM), 0.1),
        "b_lam_q2": nrm(ks[17], (N_LAYERS_B, B_HEAD_DIM), 0.1),
        "b_lam_k2": nrm(ks[18], (N_LAYERS_B, B_HEAD_DIM), 0.1),
        "b_o_norm": 1.0 + nrm(ks[19], (N_LAYERS_B, B_V_DIM), 0.02),
        "b_w_out": nrm(ks[20], (N_LAYERS_B, D_MODEL, D_MODEL), D_MODEL ** -0.5),
        "w_router": nrm(ks[21], (D_MODEL, N_EXPERTS), D_MODEL ** -0.5),
        "router_bias": nrm(ks[22], (N_EXPERTS,), 0.01),
        "moe_w_gu": nrm(ks[23], (DEPTH, N_EXPERTS, D_MODEL, 2 * D_EXPERT), D_MODEL ** -0.5),
        "moe_w_down": nrm(jax.random.fold_in(key, 99), (DEPTH, N_EXPERTS, D_EXPERT, D_MODEL), D_EXPERT ** -0.5),
    }

def first_block(x, c, positions, norm1, norm2, w_ada, b_ada, a_w_in, a_b_if, a_h_norm, a_w_out,
              b_w_in, b_q_norm, b_k_norm, b_lam_q1, b_lam_k1, b_lam_q2, b_lam_k2, b_o_norm, b_w_out,
              w_router, router_bias, moe_w_gu, moe_w_down):
    c_act = jax.nn.silu(c.astype(jnp.float32))
    for l in range(DEPTH):
        mod = (c_act @ w_ada[l].astype(jnp.float32) + b_ada[l].astype(jnp.float32))[:, None, :]
        sh1, sc1, g1, sh2, sc2, g2 = jnp.split(mod, 6, axis=-1)
        h = (_rms(x, norm1[l]) * (1.0 + sc1) + sh1).astype(x.dtype)
        j = l // N_MIXERS
        if l % N_MIXERS == 0:
            y = _mlstm_mixer(h, a_w_in[j], a_b_if[j], a_h_norm[j], a_w_out[j])
        else:
            y = _diff_attention(h, positions, b_w_in[j], b_q_norm[j], b_k_norm[j], b_lam_q1[j], b_lam_k1[j],
                                b_lam_q2[j], b_lam_k2[j], b_o_norm[j], b_w_out[j], l)
        x = (x.astype(jnp.float32) + g1 * y.astype(jnp.float32)).astype(x.dtype)
        h = (_rms(x, norm2[l]) * (1.0 + sc2) + sh2).astype(x.dtype)
        y = _grouped_moe(h, w_router, router_bias, moe_w_gu[l], moe_w_down[l])
        x = (x.astype(jnp.float32) + g2 * y.astype(jnp.float32)).astype(x.dtype)
    return x


GRID_W = 64
CTX_LEN = 256
HEAD_DIM = 64
A_Q_HEADS = 6
A_KV_HEADS = 2
B_HEADS_2 = 6
C_GROUPS = 4
C_WIDTH = C_GROUPS * HEAD_DIM
A_Q_W = A_Q_HEADS * HEAD_DIM
A_KV_W = A_KV_HEADS * HEAD_DIM
B_W = B_HEADS_2 * HEAD_DIM
Q_W = A_Q_W + B_W
KV_W = 2 * A_KV_W + 2 * B_W
MIX_W = A_Q_W + B_W + C_WIDTH
PROJ_W = Q_W + KV_W + 3 * C_WIDTH
PROJ_SPLIT = (A_Q_W, Q_W, Q_W + KV_W, Q_W + KV_W + C_WIDTH, Q_W + KV_W + 2 * C_WIDTH)
KV_SPLIT = (A_KV_W, 2 * A_KV_W, 2 * A_KV_W + B_W)
WIN_R = 8
WIN_C = 16
ROPE_FREQS = HEAD_DIM // 4
ROPE_THETA_2 = 10000.0
CONV_W = 3
FFN_DIM = 2816
N_MOD = 9


def rms_norm(x, g):
    xf = x.astype(jnp.float32)
    y = xf * lax.rsqrt(jnp.mean(xf * xf, axis=-1, keepdims=True) + EPS)
    return y.astype(x.dtype) * g

def heads(t, n):
    return t.reshape(t.shape[:-1] + (n, HEAD_DIM))

def axial_rope_tables(seq, dtype):
    pos = jnp.arange(seq, dtype=jnp.int32)
    row = (pos // GRID_W).astype(jnp.float32)
    col = (pos % GRID_W).astype(jnp.float32)
    freq = 1.0 / (ROPE_THETA_2 ** (jnp.arange(ROPE_FREQS, dtype=jnp.float32) / ROPE_FREQS))
    ang = jnp.stack([row[:, None] * freq, col[:, None] * freq], axis=1)
    return jnp.cos(ang).astype(dtype), jnp.sin(ang).astype(dtype)

def apply_axial_rope(x, cos, sin):
    xr = x.reshape(x.shape[:-1] + (2, 2, ROPE_FREQS))
    x1, x2 = xr[..., 0, :], xr[..., 1, :]
    cs, sn = cos[None, :, None], sin[None, :, None]
    return jnp.stack([x1 * cs - x2 * sn, x2 * cs + x1 * sn], axis=-2).reshape(x.shape)

def gqa_attention(q, k, v):
    bsz, s_len, hq, dh = q.shape
    hkv = k.shape[2]
    grp = hq // hkv
    nb = s_len // Q_BLOCK
    qb = q.reshape(bsz, nb, Q_BLOCK, hkv, grp, dh).transpose(1, 0, 2, 3, 4, 5)
    scale = dh ** -0.5

    def block(qi):
        s = jnp.einsum('bqhgd,bkhd->bhgqk', qi, k).astype(jnp.float32) * scale
        p = jax.nn.softmax(s, axis=-1).astype(v.dtype)
        return jnp.einsum('bhgqk,bkhd->bqhgd', p, v)

    o = lax.map(block, qb)
    return o.transpose(1, 0, 2, 3, 4, 5).reshape(bsz, s_len, hq * dh)

def neighbourhood_attention(q, k, v, k_ctx, v_ctx, rpb, rows):
    bsz, s_len, nh, dh = q.shape
    wr = min(WIN_R, rows)
    n_win = wr * WIN_C
    scale = dh ** -0.5
    qg = q.reshape(bsz, rows, GRID_W, nh, dh)
    kg = k.reshape(bsz, rows, GRID_W, nh, dh)
    vg = v.reshape(bsz, rows, GRID_W, nh, dh)
    col = jnp.arange(GRID_W)
    cs = jnp.clip(col - WIN_C // 2, 0, GRID_W - WIN_C)
    col_idx = cs[:, None] + jnp.arange(WIN_C)[None, :]
    dc_idx = col_idx - col[:, None] + (WIN_C - 1)

    def row_block(r):
        rs = jnp.clip(r - wr // 2, 0, rows - wr)
        qr = lax.dynamic_index_in_dim(qg, r, axis=1, keepdims=False)
        kw = lax.dynamic_slice_in_dim(kg, rs, wr, axis=1)[:, :, col_idx]
        vw = lax.dynamic_slice_in_dim(vg, rs, wr, axis=1)[:, :, col_idx]
        dr_idx = rs + jnp.arange(wr) - r + (WIN_R - 1)
        bias = rpb[:, dr_idx][:, :, dc_idx].transpose(0, 2, 1, 3)
        s_win = jnp.einsum('bqhd,brqjhd->bhqrj', qr, kw).astype(jnp.float32) * scale + bias.astype(jnp.float32)[None]
        s_ctx = jnp.einsum('bqhd,bkhd->bhqk', qr, k_ctx).astype(jnp.float32) * scale
        s = jnp.concatenate([s_win.reshape(bsz, nh, GRID_W, n_win), s_ctx], axis=-1)
        p = jax.nn.softmax(s, axis=-1).astype(v.dtype)
        p_win = p[..., :n_win].reshape(bsz, nh, GRID_W, wr, WIN_C)
        return (jnp.einsum('bhqrj,brqjhd->bqhd', p_win, vw)
                + jnp.einsum('bhqk,bkhd->bqhd', p[..., n_win:], v_ctx))

    o = lax.map(row_block, jnp.arange(rows, dtype=jnp.int32))
    return o.transpose(1, 0, 2, 3, 4).reshape(bsz, s_len, nh * dh)

def short_conv_mixer(xi, gate_b, gate_c, w):
    z = gate_c * xi
    y = lax.conv_general_dilated(z, w[:, None, :], window_strides=(1,),
                                 padding=((CONV_W // 2, CONV_W // 2),),
                                 dimension_numbers=('NWC', 'WIO', 'NWC'),
                                 feature_group_count=z.shape[-1])
    return gate_b * y

def swiglu(u, wi, wo):
    g, up = jnp.split(u @ wi, 2, axis=-1)
    return (jax.nn.silu(g) * up) @ wo

def split_kv(pkv, k_gain):
    ka, va, kb, vb = jnp.split(pkv, KV_SPLIT, axis=-1)
    return (rms_norm(heads(ka, A_KV_HEADS), k_gain), heads(va, A_KV_HEADS),
            heads(kb, B_HEADS_2), heads(vb, B_HEADS_2))

def context_mix(p, qk_g, conv_w):
    qa, qb, pkv, cx, cb, cc = jnp.split(p, PROJ_SPLIT, axis=-1)
    ka, va, kb, vb = split_kv(pkv, qk_g[1])
    o_a = gqa_attention(rms_norm(heads(qa, A_Q_HEADS), qk_g[0]), ka, va)
    o_b = gqa_attention(heads(qb, B_HEADS_2), kb, vb)
    o_c = short_conv_mixer(cx, cb, cc, conv_w)
    return jnp.concatenate([o_a, o_b, o_c], axis=-1), (ka, va, kb, vb)

def latent_mix(p, kv_ctx, cos, sin, qk_g, rpb, conv_w, rows):
    qa, qb, pkv, cx, cb, cc = jnp.split(p, PROJ_SPLIT, axis=-1)
    ka, va, kb, vb = split_kv(pkv, qk_g[1])
    ka_c, va_c, kb_c, vb_c = kv_ctx
    qa = apply_axial_rope(rms_norm(heads(qa, A_Q_HEADS), qk_g[0]), cos, sin)
    ka = apply_axial_rope(ka, cos, sin)
    o_a = gqa_attention(qa, jnp.concatenate([ka, ka_c], axis=1), jnp.concatenate([va, va_c], axis=1))
    o_b = neighbourhood_attention(heads(qb, B_HEADS_2), kb, vb, kb_c, vb_c, rpb, rows)
    o_c = short_conv_mixer(cx, cb, cc, conv_w)
    return jnp.concatenate([o_a, o_b, o_c], axis=-1)

def hybrid_layer(h, hc, c, c_ctx, w_ada, b_ada, g, w_in, qk_g, rpb, conv_w, w_o, ffn_wi, ffn_wo,
                 cos, sin, rows, last):
    m = (jax.nn.silu(c) @ w_ada + b_ada).reshape(c.shape[0], 1, N_MOD, D_MODEL)
    mc = (jax.nn.silu(c_ctx) @ w_ada + b_ada).reshape(1, 1, N_MOD, D_MODEL)

    def pre(t, mm, i, gi):
        return rms_norm(t, g[gi]) * (1 + mm[:, :, i + 1]) + mm[:, :, i]

    def post(t, y, mm, i, gi, wres):
        return t + wres * mm[:, :, i + 2] * rms_norm(y, g[gi])

    h = post(h, swiglu(pre(h, m, 0, 0), ffn_wi[0], ffn_wo[0]), m, 0, 1, 0.5)
    hc = post(hc, swiglu(pre(hc, mc, 0, 0), ffn_wi[0], ffn_wo[0]), mc, 0, 1, 0.5)
    u = pre(h, m, 3, 2)
    uc = pre(hc, mc, 3, 2)
    if last:
        kv_c = split_kv(uc @ w_in[:, Q_W:Q_W + KV_W], qk_g[1])
    else:
        oc, kv_c = context_mix(uc @ w_in, qk_g, conv_w)
        hc = post(hc, oc @ w_o, mc, 3, 3, 1.0)
    o = latent_mix(u @ w_in, kv_c, cos, sin, qk_g, rpb, conv_w, rows)
    h = post(h, o @ w_o, m, 3, 3, 1.0)
    h = post(h, swiglu(pre(h, m, 6, 4), ffn_wi[1], ffn_wo[1]), m, 6, 5, 0.5)
    if not last:
        hc = post(hc, swiglu(pre(hc, mc, 6, 4), ffn_wi[1], ffn_wo[1]), mc, 6, 5, 0.5)
    return h, hc

def second_inputs(seed: int = 0) -> dict:
    key = jax.random.key(seed)
    ks = jax.random.split(key, 14)
    nrm = jax.random.normal
    f32 = jnp.float32
    return {
        'x': nrm(ks[0], (BATCH, SEQ, D_MODEL), f32),
        'c': nrm(ks[1], (BATCH, D_MODEL), f32),
        'ctx': nrm(ks[2], (BATCH, CTX_LEN, D_MODEL), f32),
        'c_ctx': nrm(ks[3], (D_MODEL,), f32),
        'w_ada': nrm(ks[4], (DEPTH, D_MODEL, N_MOD * D_MODEL), f32) * (0.5 * D_MODEL ** -0.5),
        'b_ada': 0.01 * nrm(ks[5], (DEPTH, N_MOD * D_MODEL), f32),
        'norm_g': 1.0 + 0.05 * nrm(ks[6], (DEPTH, 6, D_MODEL), f32),
        'w_in': nrm(ks[7], (DEPTH, D_MODEL, PROJ_W), f32) * D_MODEL ** -0.5,
        'qk_g': 1.0 + 0.05 * nrm(ks[8], (DEPTH, 2, HEAD_DIM), f32),
        'rpb': 0.1 * nrm(ks[9], (DEPTH, B_HEADS_2, 2 * WIN_R - 1, 2 * WIN_C - 1), f32),
        'conv_w': nrm(ks[10], (DEPTH, CONV_W, C_WIDTH), f32) * CONV_W ** -0.5,
        'w_o': nrm(ks[11], (DEPTH, MIX_W, D_MODEL), f32) * MIX_W ** -0.5,
        'ffn_wi': nrm(ks[12], (DEPTH, 2, D_MODEL, 2 * FFN_DIM), f32) * D_MODEL ** -0.5,
        'ffn_wo': nrm(ks[13], (DEPTH, 2, FFN_DIM, D_MODEL), f32) * FFN_DIM ** -0.5,
    }

def second_block(x, c, ctx, c_ctx, w_ada, b_ada, norm_g, w_in, qk_g, rpb, conv_w, w_o, ffn_wi, ffn_wo):
    seq = x.shape[1]
    rows = seq // GRID_W
    cos, sin = axial_rope_tables(seq, x.dtype)
    h, hc = x, ctx
    for i in range(DEPTH):
        h, hc = hybrid_layer(h, hc, c, c_ctx, w_ada[i], b_ada[i], norm_g[i], w_in[i], qk_g[i], rpb[i],
                             conv_w[i], w_o[i], ffn_wi[i], ffn_wo[i], cos, sin, rows, i == DEPTH - 1)
    return h


def setup_inputs(seed=0):
    out = dict(first_inputs(seed))
    for name, value in second_inputs(seed + 1).items():
        if name != "x":
            out[name + "_2"] = value
    return out


def reference(
    x, c, positions, norm1, norm2, w_ada, b_ada, a_w_in, a_b_if, a_h_norm, a_w_out, b_w_in,
    b_q_norm, b_k_norm, b_lam_q1, b_lam_k1, b_lam_q2, b_lam_k2, b_o_norm, b_w_out, w_router,
    router_bias, moe_w_gu, moe_w_down, c_2, ctx_2, c_ctx_2, w_ada_2, b_ada_2, norm_g_2, w_in_2,
    qk_g_2, rpb_2, conv_w_2, w_o_2, ffn_wi_2, ffn_wo_2,
):
    x = first_block(
        x, c, positions, norm1, norm2, w_ada, b_ada, a_w_in, a_b_if, a_h_norm, a_w_out, b_w_in,
        b_q_norm, b_k_norm, b_lam_q1, b_lam_k1, b_lam_q2, b_lam_k2, b_o_norm, b_w_out, w_router,
        router_bias, moe_w_gu, moe_w_down,
    )
    return second_block(
        x, c_2, ctx_2, c_ctx_2, w_ada_2, b_ada_2, norm_g_2, w_in_2, qk_g_2, rpb_2, conv_w_2,
        w_o_2, ffn_wi_2, ffn_wo_2,
    )


_drawn_inputs = setup_inputs


def setup_inputs(seed=0):
    import zlib

    import numpy as np

    out = dict(_drawn_inputs(seed))
    spreads = {}
    factors = {'a_h_norm': 3.263,
     'b_q_norm': 8.0,
     'b_k_norm': 8.0,
     'b_lam_k1': 2.794,
     'b_lam_k2': 3.74,
     'b_o_norm': 3.922,
     'b_ada_2': 2.9,
     'qk_g_2': 8.0,
     'rpb_2': 31.209}
    for name, (base, spread) in spreads.items():
        noise = np.random.default_rng([zlib.crc32(name.encode()), seed]).standard_normal(out[name].shape)
        drawn = base * np.exp(spread * noise) if base else spread * noise
        out[name] = __import__('jax').numpy.asarray(drawn.astype(out[name].dtype))
    for name, factor in factors.items():
        out[name] = (out[name] * factor).astype(out[name].dtype)
    return out
```

```python
import math
from contextlib import ExitStack

import numpy as np

import concourse.bass as bass
from concourse import mybir

F32 = mybir.dt.float32
F32R = mybir.dt.float32r
I32 = mybir.dt.int32
U32 = mybir.dt.uint32
ALU = mybir.AluOpType
ACT = mybir.ActivationFunctionType
AX = mybir.AxisListType
ds = bass.ds

P = 128
D = 1024
KT = D // P
T1 = 256
T2 = 512
DEPTH = 2
EPS = 1e-6
A_HEADS, A_QK, A_V = 4, 128, 256
B_HEADS, B_HD = 8, 64
N_EXP, N_GRP, E_GRP = 16, 4, 4
D_EXP = 512
FFN = 2816
FFN_TILES = FFN // P
HALF = FFN_TILES // 2
NMOD2 = 9
HD = 64
LAT_HEADS = 12
SLOTS = 6
SLOT = 2048
LAM_INIT = 0.8 - 0.6 * math.exp(-0.3 * 1)
INVALID = -1e30

COLS = {}
_at = 0
for _name, _n in (("c1", 8), ("c2", 16), ("norm1", 16), ("norm2", 16), ("b_ada", 96), ("a_h_norm", 8),
                  ("b_q_norm", 1), ("b_k_norm", 1), ("b_o_norm", 1), ("b_ada_2", 144),
                  ("norm_g_2", 96), ("qk_g_2", 4), ("conv_w_2", 12), ("b_if", 8), ("router_bias", 16)):
    COLS[_name] = (_at, _n)
    _at += _n
NCOLS = _at

CONST = {}
_at = 0
for _name, _n in (("ident", 128), ("block_ones", 128), ("upper", 128), ("rope1", 128), ("causal", 128),
                  ("iota16", 16), ("iota8", 8), ("invfreq", 1)):
    CONST[_name] = (_at, _n)
    _at += _n
NCONST = _at
CONST2 = {"rope2": (0, 128), "dup0": (128, 128), "dup1": (256, 128), "cos2": (384, 256), "sin2": (640, 256)}
NCONST2 = 896


START = {"ada_col": 1, "gated": 4, "y_ready": KT}


class Log:

    def __init__(self, notes=None):
        self.notes = notes
        self.count, self.marks, self.loops = dict(START), {}, {}
        self.loop = None

    def enter(self, name, i, turns):
        self.loop, self.before = (name, i), dict(self.count)
        self.loops.setdefault(name, {"turns": turns, "per": {}})

    def leave(self):
        rec = self.loops[self.loop[0]]
        for k, v in self.count.items():
            if per := v - self.before.get(k, 0):
                rec["per"][k] = per
                self.count[k] = self.before.get(k, 0) + per * rec["turns"]
        self.loop = None

    def raised(self, sem, key, by):
        self.count[sem] = self.count.get(sem, 0) + by
        if key is not None:
            self.marks[(sem, key)] = (self.loop and self.loop[0], self.count[sem])

    def value(self, sem, key, loop, back):
        if self.notes is None:
            return 1
        at, v = self.notes.marks[(sem, key)]
        if at is None:
            return v
        rec = self.notes.loops[at]
        per = rec["per"][sem]
        if loop and loop[0] == at:
            return loop[1] * per + (v - back * per)
        return v + (rec["turns"] - 1) * per


def host_consts():
    c = np.zeros((P, NCONST), np.float32)
    p = np.arange(P)
    put = lambda n, a: c.__setitem__((slice(None), slice(CONST[n][0], CONST[n][0] + CONST[n][1])), a)
    put("ident", np.eye(P))
    put("block_ones", (p[:, None] // 64 == p[None, :] // 64))
    put("upper", (p[:, None] <= p[None, :]))
    put("causal", np.where(p[:, None] >= p[None, :], 0.0, INVALID))
    r = np.zeros((P, P))
    freq = np.zeros((P, 1))
    inv = (500000.0 ** (-np.arange(0, 16, 2, dtype=np.float32) / np.float32(16))).astype(np.float32)
    for h in range(2):
        for d in range(8):
            r[64 * h + d + 8, 64 * h + d] = -1
            r[64 * h + d, 64 * h + d + 8] = 1
            freq[64 * h + d] = freq[64 * h + d + 8] = inv[d]
    put("rope1", r)
    put("invfreq", freq)
    put("iota16", np.arange(16)[None, :])
    put("iota8", np.arange(8)[None, :])
    c2 = np.zeros((P, NCONST2), np.float32)
    r = np.zeros((P, P))
    cos, sin = np.zeros((P, T1), np.float32), np.zeros((P, T1), np.float32)
    f = (1.0 / (np.float32(10000.0) ** (np.arange(16, dtype=np.float32) / np.float32(16)))).astype(np.float32)
    pos = np.arange(T1)
    for q in range(P):
        axis, part, i = (q % 64) // 32, (q % 32) // 16, q % 16
        ang = ((pos // 64) if axis == 0 else (pos % 64)).astype(np.float32) * f[i]
        cos[q], sin[q] = np.cos(ang), np.sin(ang)
        if part == 0:
            r[q + 16, q] = -1
        else:
            r[q - 16, q] = 1
    c2[:, 0:128] = r
    c2[:, 128:256] = (p[:, None] == p[None, :] % 64)
    c2[:, 256:384] = (p[:, None] == 64 + p[None, :] % 64)
    c2[:, 384:640], c2[:, 640:896] = cos, sin
    return c, c2


def build(nc, A, out, notes=None):
    log = Log(notes)
    with ExitStack() as ctx:
        sems = {}

        def sem(name):
            if name not in sems:
                sems[name] = ctx.enter_context(nc.semaphore(name))
            return sems[name]

        stage = [""]

        def T(name, key=None, by=1):
            log.raised(name, (stage[0], key) if key is not None else None, by)
            return sem(name), by

        def W(name, key, at=None, back=0):
            return sem(name), log.value(name, (at or stage[0], key), log.loop, back)

        def T_at(name, key):
            log.raised(name, ("load", key), 1)
            return sem(name), 1

        top = [16544]

        def region(nbytes):
            at = top[0]
            top[0] += nbytes
            return at

        def sb(name, shape, dt, at):
            return nc.alloc_sbuf_tensor_at(name, shape, dt, offset=at)[:]

        def take(at):
            pos = [at]

            def f(name, shape, dt=F32):
                t = sb(name, shape, dt, pos[0])
                pos[0] += -(-4 * int(np.prod(shape[1:])) // 32) * 32
                return t
            f.pos = pos
            return f

        raw_at = region(SLOTS * SLOT * 4)
        raw = [sb(f"raw{s}", [P, SLOT], F32, raw_at + s * SLOT * 4) for s in range(SLOTS)]
        split_at = region(4 * SLOT * 4)
        w_hi = [sb(f"w_hi{b}", [P, SLOT], F32R, split_at + 2 * b * SLOT * 4) for b in range(2)]
        w_lo = [sb(f"w_lo{b}", [P, SLOT], F32R, split_at + (2 * b + 1) * SLOT * 4) for b in range(2)]
        X = sb("x_resid", [P, KT, T2], F32, region(KT * T2 * 4))
        h_at = region(2 * KT * T2 * 4)
        h_hi = sb("h_hi", [P, KT, T2], F32R, h_at)
        h_lo = sb("h_lo", [P, KT, T2], F32R, h_at + KT * T2 * 4)
        squares = sb("squares", [P, KT, T2], F32, h_at + KT * T2 * 4)
        a_at = region(2 * HALF * T2 * 4)
        y_at = region(KT * T2 * 4)
        Y = sb("y_out", [P, KT, T2], F32, y_at)
        act_hi = sb("act_hi", [P, HALF, T2], F32R, a_at)
        act_lo = sb("act_lo", [P, HALF, T2], F32R, a_at + HALF * T2 * 4)

        cst = take(region(0))
        consts_a = cst("consts_a", [P, 2 * P])
        b_at = cst.pos[0]
        consts_b = cst("consts_b", [P, NCONST - 2 * P])
        w_router = cst("w_router_sb", [P, KT, N_EXP])
        cst.pos[0] = max(cst.pos[0], b_at + 4 * NCONST2)
        consts2 = sb("consts2", [P, NCONST2], F32, b_at)
        C = {k: (consts_a[:, a:a + n] if a < 2 * P else consts_b[:, a - 2 * P:a - 2 * P + n]) for k, (a, n) in CONST.items()}
        C2 = {k: consts2[:, a:a + n] for k, (a, n) in CONST2.items()}
        cols_ = cst("cols", [P, NCOLS])
        V = {k: cols_[:, a:a + n] for k, (a, n) in COLS.items()}
        ones = cst("ones", [P, P])
        ident = C["ident"]
        epsc = cst("epsc", [P, 1])
        onec = cst("onec", [P, 1])
        mod1 = cst("mod1", [P, DEPTH, 48])
        pre1 = cst("pre1", [P, DEPTH, 2, KT])
        mod2 = cst("mod2", [P, DEPTH, NMOD2, KT, 2])
        pre2 = cst("pre2", [P, DEPTH, 3, KT, 2])
        post2 = cst("post2", [P, DEPTH, 3, KT, 2])
        cact1 = cst("cact1", [P, KT])
        cact2 = cst("cact2", [P, KT, 2])
        small = cst("small", [P, 16])
        tmp_at = cst.pos[0]
        tmp = [cst(f"tmp{i}", [P, T2]) for i in range(2)]
        full = [cst(f"full{i}", [P, T2]) for i in range(2)]
        rstd = cst("rstd", [P, T2])
        assert cst.pos[0] <= 229344, cst.pos[0]
        psum = [ctx.enter_context(nc.psum_tensor(f"bank{b}", [P, 512], F32)) for b in range(8)]

        at0 = take(a_at)
        xt = at0("x_tokens", [P, 4, D])
        ada_row = sb("ada_row", [2, 6 * 256], F32, h_at)
        m = take(a_at)
        m_q, m_k = m("m_q", [P, A_HEADS, T1]), m("m_k", [P, A_HEADS, T1])
        m_v, m_og = m("m_v", [P, 2, A_HEADS * A_V]), m("m_og", [P, KT, T1])
        w_gate = m("w_gate", [P, KT, 2 * A_HEADS])
        m_g, m_lf, m_u, m_b, m_a = (m(n, [P, 2, 2 * A_HEADS if n == "m_g" else A_HEADS])
                                    for n in ("m_g", "m_lf", "m_u", "m_b", "m_a"))
        m_rows, m_arow = m("m_rows", [A_HEADS, 512]), m("m_arow", [A_HEADS, T1])
        m_d, m_p, m_hh, m_em, m_dn = (m("m_d", [P, 384]), m("m_p", [P, 384]), m("m_hh", [P, 2, T1]),
                                      m("m_em", [P, T1]), m("m_dn", [P, T1]))
        m_full = m("m_full", [P, 2, T1])
        m_d2 = full[0]
        assert m.pos[0] <= y_at + KT * T2 * 4
        d = take(a_at)
        d_q, d_k = d("d_q", [P, B_HEADS, T1]), d("d_k", [P, B_HEADS, T1])
        d_v = d("d_v", [P, 2, D])
        d_cos, d_sin = d("d_cos", [P, T1]), d("d_sin", [P, T1])
        d_ang, d_n = d("d_ang", [P, T1]), d("d_n", [P, T1])
        d_pos = d("d_pos", [P, T1], I32)
        d_lam = d("d_lam", [P, 4, B_HD])
        d_ls = d("d_ls", [P, 8])
        d_raw = [d(f"d_raw{i}", [P, T1]) for i in range(2)]
        d_sq = [d(f"d_sq{i}", [P, T1]) for i in range(2)]
        d_rs = [d(f"d_rs{i}", [P, T1]) for i in range(2)]
        d_p = [d(f"d_p{i}", [P, 2, T1]) for i in range(2)]
        d_st = [d(f"d_st{i}", [P, 8]) for i in range(2)]
        d_at = [d(f"d_at{i}", [P, 2, T1]) for i in range(2)]
        assert d.pos[0] <= y_at + KT * T2 * 4
        e = take(a_at)
        e_hi, e_lo = e("e_hi", [P, 4, T1], F32R), e("e_lo", [P, 4, T1], F32R)
        e_gate = e("e_gate", [P, N_EXP, T1])
        e_s, e_b, e_m, e_w = (e(n, [P, 2, N_EXP]) for n in ("e_s", "e_b", "e_m", "e_w"))
        e_pair, e_g8, e_x8 = e("e_pair", [P, N_GRP, 6]), e("e_g8", [P, 8]), e("e_x8", [P, 8])
        e_i8 = e("e_i8", [P, 8], U32)
        e_f8, e_oh = e("e_f8", [P, 8]), e("e_oh", [P, 8])
        e_row = e("e_row", [N_EXP, T1])
        e_zero = e("e_zero", [P, T2], F32R)
        assert e.pos[0] <= y_at + KT * T2 * 4
        g = take(a_at)
        g_q, g_kb = g("g_q", [P, 6, T2]), g("g_kb", [P, 3, T2])
        g_ka, g_kd = g("g_ka", [P, T2]), g("g_kd", [P, 2, T2])
        g_v = g("g_v", [P, 4, 512])
        g_cx, g_cb, g_cc = (g(n, [P, 2, T2]) for n in ("g_cx", "g_cb", "g_cc"))
        assert g.pos[0] <= y_at
        g = take(y_at)
        g_bias = g("g_bias", [P, 2, 6, T1])
        g_p = [g(f"g_p{i}", [P, T2]) for i in range(2)]
        assert g.pos[0] <= y_at + KT * T2 * 4
        g_pt = [sb(f"g_pt{i}", [P, 4, T1], F32, tmp_at + i * 4096) for i in range(2)]
        xo = sb("x_out", [P, 2, D], F32, a_at)
        g_st = [small[:, 4 * i:4 * i + 4] for i in range(2)]

        block = ctx.enter_context(nc.Block())

        class Stream:

            def __init__(self):
                self.slot, self.all, self.loop = [0] * SLOTS, 0, None

            def enter(self, i, chunks):
                self.loop = (i, chunks, [len(range(s, chunks, SLOTS)) for s in range(SLOTS)])

            def leave(self, turns):
                _, chunks, per = self.loop
                self.loop = None
                self.all += (turns - 1) * chunks
                self.slot = [n + (turns - 1) * k for n, k in zip(self.slot, per)]

            def next(self, s):
                self.slot[s] += 1
                self.all += 1
                if self.loop is None:
                    return self.slot[s], self.all
                i, chunks, per = self.loop
                return i * per[s] + self.slot[s], i * chunks + self.all

        def w3(ap, k):
            return ap.rearrange("p (k n) -> p k n", k=k)

        def tt(*which, n):
            return [("T", P * x, n) for x in which]

        ITEMS = {"mlstm": [tt(0, 1, n=T1)] * 4 + [[("V", 0, 256, (0, 1))]] * 4 + [tt(0, 1, n=T1)] * 4,
                 "mlstm_out": [tt(0, 1, n=T1)] * 4,
                 "diff": [tt(0, 1, n=T1)] * 8 + [[("V", 0, 256, (0, 1))]] * 4,
                 "diff_out": [tt(0, 1, n=T1)] * 4}
        for l in range(DEPTH):
            n = T1 if l == DEPTH - 1 else T2
            ITEMS[f"in{l}"] = [tt(0, 1, n=n)] * 3 + [tt(0, n=T2) + [("V", 128, 128, (0, 1, 2, 3))], tt(0, 1, n=T2),
                               tt(0, n=T2) + [("V", 128, 128, (0, 1, 2, 3))],
                               [("V", 0, 256, (0, 1)), ("V", 0, 256, (2, 3))]] + [tt(0, 1, n=n)] * 3
            ITEMS[f"attn_out{l}"] = [tt(0, 1, n=n)] * 4

        def in_evac_by(c, n):
            return "evac_v" if (c, n) in ((3, 1), (5, 1)) or c == 6 else "evac_a"

        EVAC = {"mlstm": lambda c, n: "evac_v" if 4 <= c < 8 else "evac_a",
                "diff": lambda c, n: "evac_v" if c >= 8 else "evac_a",
                "mlstm_out": lambda c, n: "evac_v", "diff_out": lambda c, n: "evac_v",
                "in0": in_evac_by, "in1": in_evac_by,
                "attn_out0": lambda c, n: "evac_v", "attn_out1": lambda c, n: "evac_v"}
        ADA_CHUNKS = DEPTH * SLOTS * (4 + 6)

        def bank_of(name, c, n):
            return (sum(len(x) for x in ITEMS[name][:c]) + n) % 4

        def x_key(at, j):
            return ("evac_v", (j // 2, j % 2), at) if at.endswith("_out") else ("x_ready", j, at)

        def y_key(post, j):
            if post.endswith(".1"):
                return "evac_v", (j // 2, j % 2), f"attn_out{post[4]}"
            name = f"ffn{post[4]}a" if post.startswith("post") and post.endswith(".0") else post[4:]
            return "y_ready", ("g1" if name == LAST else "g", j), name

        EXP_CH, FFN_CH, FFN_UP = 6, HALF + KT, HALF
        DOWN = HALF * P
        LAST = f"ffn{DEPTH - 1}b"

        def last_item(name, c):
            return c, len(ITEMS[name][c]) - 1

        def units(l):
            return [(s, hd, qb) for s in range(1 if l == DEPTH - 1 else 2) for hd in range(LAT_HEADS)
                    for qb in range(2)]

        last_head = {"mix0": A_HEADS - 1, "mix1": B_HEADS - 1} | {f"mix2.{l}": len(units(l)) // 2 - 1 for l in range(DEPTH)}

        def keys_of(s):
            return (0, T2) if s == 0 else (T1, T2)

        def halves(l):
            return [(0, 0, T1), (1, T1, T2)][:1 if l == 2 else 2]

        @block.sync
        def _(sp):
            st = Stream()

            def load(c, src, k):
                s = c % SLOTS
                used, _ = st.next(s)
                dst = w3(raw[s], k) if k * (SLOT // k) == SLOT else w3(raw[s][:, 0:DOWN], k)
                sp.wait_ge(sem(f"raw_done{s}"), used)
                sp.dma_start(dst, src).then_inc(sem(f"raw_full{s}"), 16)

            def linear(name, W2d):
                v = W2d.rearrange("(k p) n -> p k n", p=P)
                for c in range(len(ITEMS[name])):
                    load(c, v[:, :, 256 * c:256 * c + 256], KT)

            def ada(W2d, turns):
                v = W2d.rearrange("(k p) n -> p k n", p=P)
                with sp.Fori(0, turns) as i:
                    st.enter(i, SLOTS)
                    for c in range(SLOTS):
                        load(c, v[:, :, ds(i * 1536 + c * 256, 256)], KT)
                st.leave(turns)

            def moe(l):
                gu = A["moe_w_gu"][l].rearrange("e (k p) (g c n) -> e p g k c n", p=P, g=2, c=4)
                dn = A["moe_w_down"][l].rearrange("e (k p) n -> e p k n", p=P)
                with sp.Fori(0, N_EXP) as i:
                    st.enter(i, EXP_CH)
                    for c in range(4):
                        s = c
                        used, _ = st.next(s)
                        dst = raw[s].rearrange("p (g k n) -> p g k n", g=2, k=KT)
                        sp.wait_ge(sem(f"raw_done{s}"), used)
                        sp.dma_start(dst, gu[i, :, :, :, c, :]).then_inc(sem(f"raw_full{s}"), 16)
                    for c in range(4, 6):
                        load(c, dn[i, :, :, 512 * (c - 4):512 * (c - 3)], 4)
                st.leave(N_EXP)

            def ffn(l, which):
                wi = A["ffn_wi_2"][l, which].rearrange("(k p) (g c n) -> p g k c n", p=P, g=2, c=FFN_TILES)
                wo = A["ffn_wo_2"][l, which].rearrange("(t f p) n -> p t f n", t=2, p=P)

                def group(t):
                    for c in range(FFN_UP):
                        s = c % SLOTS
                        used, _ = st.next(s)
                        dst = raw[s].rearrange("p (g k n) -> p g k n", g=2, k=KT)
                        sp.wait_ge(sem(f"raw_done{s}"), used)
                        sp.dma_start(dst, wi[:, :, :, t * HALF + c, :]).then_inc(sem(f"raw_full{s}"), 16)
                    for c in range(KT):
                        load(FFN_UP + c, wo[:, t, :, P * c:P * c + P], HALF)

                if (l, which) == (DEPTH - 1, 1):
                    group(0)
                    group(1)
                else:
                    with sp.Fori(0, 2) as t:
                        st.enter(t, FFN_CH)
                        group(t)
                    st.leave(2)

            stage[0] = "load"
            sp.dma_start(consts_a, A["consts"][:, 0:2 * P]).then_inc(*T("small_in", "ident", 16))
            sp.dma_start(consts_b, A["consts"][:, 2 * P:NCONST]).then_inc(*T("small_in", "consts", 16))
            sp.dma_start(cols_, A["columns"]).then_inc(*T("small_in", "cols", 16))
            sp.dma_start(w_router, A["w_router"].rearrange("(k p) n -> p k n", p=P)).then_inc(*T("small_in", "all", 16))
            for l in range(DEPTH):
                ada(A["w_ada"][l], 4)
            for l in range(DEPTH):
                ada(A["w_ada_2"][l], 6)
            linear("mlstm", A["a_w_in"][0])
            linear("mlstm_out", A["a_w_out"][0])
            moe(0)
            linear("diff", A["b_w_in"][0])
            linear("diff_out", A["b_w_out"][0])
            moe(1)
            for l in range(DEPTH):
                ffn(l, 0)
                linear(f"in{l}", A["w_in_2"][l])
                linear(f"attn_out{l}", A["w_o_2"][l])
                ffn(l, 1)

        @block.gpsimd
        def _(pool):
            stage[0] = "load"
            pool.dma_start(xt[:, 0:2, :], A["x"][0].rearrange("(t p) d -> p t d", p=P)).then_inc(*T("tokens_in", "x", 16))
            pool.dma_start(xt[:, 2:4, :], A["ctx_2"][0].rearrange("(t p) d -> p t d", p=P)).then_inc(*T("tokens_in", "all", 16))
            pool.wait_ge(*W("x_ready", KT - 1, at="turn_in"))
            pool.dma_start(w_gate, A["a_w_in"][0].rearrange("(k p) n -> p k n", p=P)[:, :, 3072:3080])\
                .then_inc(*T("gate_in", 0, 16))
            pool.wait_ge(*W("x_ready", KT - 1, at="moe0"))
            pool.dma_start(d_pos, A["positions"].broadcast_to([P, T1])).then_inc(*T("diff_in", "pos", 16))
            for n, name in enumerate(("b_lam_q1", "b_lam_k1", "b_lam_q2", "b_lam_k2")):
                pool.dma_start(d_lam[:, n, :], A[name].broadcast_to([P, B_HD])).then_inc(*T("diff_in", "all", 16))
            pool.wait_ge(*W("x_ready", KT - 1, at="moe1"))
            pool.dma_start(consts2, A["consts2"]).then_inc(*T("consts2_in", 0, 16))
            for l in range(DEPTH):
                pool.wait_ge(*W("x_ready", KT - 1, at=f"post{l}.0"))
                for r in range(4):
                    pool.dma_start(g_bias[64 * (r % 2):64 * (r % 2) + 64, r // 2, :, :],
                                   A["rpb_rows"][l, r]).then_inc(*T("bias_in", l, 16))
            stage[0] = "store"
            for t in range(2):
                pool.wait_ge(*W("out_tile", t))
                pool.dma_start(out[0, P * t:P * t + P, :], xo[:, t, :]).then_inc(*T("stored", t, 16))
            pool.wait_ge(*W("stored", 1))

        @block.tensor
        def _(pe):
            st = Stream()
            bank_user = {}

            def bank_ready(b):
                if b in bank_user:
                    pe.wait_ge(*W(*bank_user[b][0], **bank_user[b][1]))

            def ada(name, turns, cact, M):
                stage[0] = name
                with pe.Fori(0, turns) as i:
                    st.enter(i, SLOTS)
                    log.enter(name, i, turns)
                    for c in range(SLOTS):
                        used, _ = st.next(c)
                        w = w3(raw[c], KT)
                        pe.wait_ge(sem(f"raw_full{c}"), used * 16)
                        for k in range(KT):
                            mm = pe.matmul(psum[c // 2][0:M, 256 * (c % 2):256 * (c % 2) + 256],
                                           cact[:, k, 0:M] if M == 2 else cact[:, k:k + 1],
                                           w[:, k, :], start=(k == 0), stop=(k == KT - 1))
                        mm.then_inc(sem(f"raw_done{c}"), 1)
                    pe.wait_ge(*W("ada_row", "row"))
                    pe.wait_ge(*W("ada_col", "col", back=1))
                    for t in range(12):
                        mm = pe.matmul(psum[3][:, M * t:M * t + M], ada_row[0:M, P * t:P * t + P], ident[0:M, 0:M],
                                       start=True, stop=True)
                    mm.then_inc(*T("product", "cols"))
                    log.leave()
                st.leave(turns)

            def turn_in():
                stage[0] = "turn_in"
                pe.wait_ge(*W("tokens_in", "all", at="load"))
                pe.wait_ge(*W("ada_col", "col", at="ada2.1"))
                for j in range(KT):
                    for t in range(4):
                        mm = pe.transpose(psum[j][:, P * t:P * t + P], xt[:, t, P * j:P * j + P], ident)
                    mm.then_inc(*T("product", j))

            def sum_squares(name, n):
                stage[0] = name
                for j in range(KT):
                    pe.wait_ge(*W("squared", j))
                    mm = pe.matmul(psum[3][:, 0:n], ones, squares[:, j, 0:n], start=(j == 0), stop=(j == KT - 1))
                mm.then_inc(*T("product", "squares"))

            def linear(name, source, per_tile=True):
                stage[0] = name
                bank = 0
                for c, items in enumerate(ITEMS[name]):
                    used, _ = st.next(c % SLOTS)
                    pe.wait_ge(sem(f"raw_done{c % SLOTS}"), used + 1)
                    hi, lo = w3(w_hi[c % 2], KT), w3(w_lo[c % 2], KT)
                    for n, it in enumerate(items):
                        b = bank % 4
                        bank += 1
                        bank_ready(b)
                        if it[0] == "T":
                            jobs = [(slice(0, it[2]), None)]
                        else:
                            jobs = [(slice(it[2] * x, it[2] * x + it[2]), t) for x, t in enumerate(it[3])]
                        for where, t in jobs:
                            for k in range(KT):
                                if c == 0 and n == 0:
                                    pe.wait_ge(*W("h_ready", k if per_tile else last_head[source], at=source))
                                if t is None:
                                    cut = slice(it[1], it[1] + P)
                                    trio = [(hi[:, k, cut], h_hi[:, k, 0:it[2]]), (hi[:, k, cut], h_lo[:, k, 0:it[2]]),
                                            (lo[:, k, cut], h_hi[:, k, 0:it[2]])]
                                else:
                                    cut, tok = slice(it[1], it[1] + it[2]), slice(P * t, P * t + P)
                                    trio = [(h_hi[:, k, tok], hi[:, k, cut]), (h_hi[:, k, tok], lo[:, k, cut]),
                                            (h_lo[:, k, tok], hi[:, k, cut])]
                                for x, (l_, r_) in enumerate(trio):
                                    mm = pe.matmul(psum[b][:, where], l_, r_, start=(k == 0 and x == 0),
                                                   stop=(k == KT - 1 and x == 2))
                        mm.then_inc(*T("product", (c, n)))
                        bank_user[b] = ((EVAC[name](c, n), (c, n)), {"at": name})

            def moe(l):
                name = stage[0] = f"moe{l}"
                for t in range(2):
                    for k in range(KT):
                        if t == 0:
                            pe.wait_ge(*W("h_ready", k, at=f"norm{l}.1"))
                        for x, h in enumerate((h_hi, h_lo)):
                            mm = pe.matmul(psum[0][:, 16 * t:16 * t + 16], h[:, k, P * t:P * t + P].bitcast(F32),
                                           w_router[:, k, :], start=(k == 0 and x == 0), stop=(k == KT - 1 and x == 1))
                mm.then_inc(*T("product", "router"))
                pe.wait_ge(*W("gate_w", "tokens"))
                for t in range(2):
                    mm = pe.transpose(psum[0][0:N_EXP, 128 + P * t:256 + P * t], e_w[:, t, :], ident)
                mm.then_inc(*T("product", "gate_rows"))
                pe.wait_ge(*W("gate_w", "rows"))
                for x in range(N_EXP):
                    if x >= 4:
                        pe.wait_ge(*W("gate_bc", x - 4))
                    mm = pe.matmul(psum[x % 4][:, 0:T1], ident[0:N_EXP, x:x + 1].broadcast_to([N_EXP, P]), e_row,
                                   start=True, stop=True)
                    mm.then_inc(*T("product", ("bc", x)))
                pe.wait_ge(*W("gate_bc", N_EXP - 1))
                for b in range(4, 8):
                    pe.matmul(psum[b][:, :], e_zero[:, 0:P], e_zero, start=True, stop=False, skip_group_check=True)
                with pe.Fori(0, N_EXP) as i:
                    st.enter(i, EXP_CH)
                    log.enter(name, i, N_EXP)
                    for c in range(4):
                        used, _ = st.next(c)
                        hi, lo = w3(w_hi[c % 2], 2 * KT), w3(w_lo[c % 2], 2 * KT)
                        pe.wait_ge(sem(f"raw_done{c}"), used + 1)
                        pe.wait_ge(*W("gated", c, back=1))
                        for q in range(2):
                            o = psum[c][:, T1 * q:T1 * q + T1]
                            for k in range(KT):
                                f = q * KT + k
                                pe.matmul(o, hi[:, f, :], h_hi[:, k, 0:T1], start=(k == 0), stop=False)
                                pe.matmul(o, hi[:, f, :], h_lo[:, k, 0:T1], start=False, stop=False)
                                mm = pe.matmul(o, lo[:, f, :], h_hi[:, k, 0:T1], start=False, stop=(k == KT - 1))
                        mm.then_inc(*T("product", ("up", c)))
                    for c in range(4, 6):
                        used, _ = st.next(c)
                        hi, lo = w3(w_hi[c % 2], 4), w3(w_lo[c % 2], 4)
                        pe.wait_ge(sem(f"raw_done{c}"), used + 1)
                        for m_ in range(4):
                            j = 4 * (c - 4) + m_
                            o = psum[4 + j // 2][:, T1 * (j % 2):T1 * (j % 2) + T1]
                            for k in range(4):
                                if j == 0:
                                    pe.wait_ge(*W("act_ready", k))
                                cut = slice(P * m_, P * m_ + P)
                                pe.matmul(o, hi[:, k, cut], e_hi[:, k, :], start=False, stop=False, skip_group_check=True)
                                pe.matmul(o, hi[:, k, cut], e_lo[:, k, :], start=False, stop=False, skip_group_check=True)
                                mm = pe.matmul(o, lo[:, k, cut], e_hi[:, k, :], start=False, stop=False, skip_group_check=True)
                        mm.then_inc(*T("product", ("down", c)))
                    log.leave()
                st.leave(N_EXP)
                bank_user.clear()

            def ffn(l, which):
                name = stage[0] = f"ffn{l}{'ab'[which]}"
                n = T1 if name == LAST else T2

                def group(tag, back):
                    for c in range(FFN_UP):
                        used, _ = st.next(c % SLOTS)
                        hi, lo = w3(w_hi[c % 2], 2 * KT), w3(w_lo[c % 2], 2 * KT)
                        pe.wait_ge(sem(f"raw_done{c % SLOTS}"), used + 1)
                        if c >= 2:
                            pe.wait_ge(*W("gated", (tag, c - 2)))
                        elif back:
                            pe.wait_ge(*W("gated", (back, FFN_UP - 1 - c), back=1 if back == tag else 0))
                        for q in range(2):
                            o = psum[2 * (c % 2) + q][:, 0:n]
                            for k in range(KT):
                                if q == 0 and c == 0:
                                    pe.wait_ge(*W("h_ready", k, at=f"norm{name}"))
                                f = q * KT + k
                                pe.matmul(o, hi[:, f, :], h_hi[:, k, 0:n], start=(k == 0), stop=False)
                                pe.matmul(o, hi[:, f, :], h_lo[:, k, 0:n], start=False, stop=False)
                                mm = pe.matmul(o, lo[:, f, :], h_hi[:, k, 0:n], start=False, stop=(k == KT - 1))
                        mm.then_inc(*T("product", (tag, c)))
                    for j in range(KT):
                        c = FFN_UP + j
                        used, _ = st.next(c % SLOTS)
                        hi, lo = w3(w_hi[c % 2][:, 0:DOWN], HALF), w3(w_lo[c % 2][:, 0:DOWN], HALF)
                        pe.wait_ge(sem(f"raw_done{c % SLOTS}"), used + 1)
                        if j >= 4:
                            pe.wait_ge(*W("y_ready", (tag, j - 4)))
                        elif back:
                            pe.wait_ge(*W("y_ready", (back, 4 + j), back=1 if back == tag else 0))
                        o = psum[4 + j % 4][:, 0:n]
                        for k in range(HALF):
                            if j == 0:
                                pe.wait_ge(*W("act_ready", (tag, k)))
                            pe.matmul(o, hi[:, k, :], act_hi[:, k, 0:n], start=(k == 0), stop=False)
                            pe.matmul(o, hi[:, k, :], act_lo[:, k, 0:n], start=False, stop=False)
                            mm = pe.matmul(o, lo[:, k, :], act_hi[:, k, 0:n], start=False, stop=(k == HALF - 1))
                        mm.then_inc(*T("product", (tag, c)))

                if name == LAST:
                    group("g0", None)
                    group("g1", "g0")
                else:
                    with pe.Fori(0, 2) as t:
                        st.enter(t, FFN_CH)
                        log.enter(name, t, 2)
                        group("g", "g")
                        log.leave()
                    st.leave(2)
                bank_user.clear()

            def mlstm():
                stage[0] = "mix0"
                for b in range(4):
                    bank_ready(b)
                pe.wait_ge(*W("gate_in", 0, at="load"))
                for t in range(2):
                    for k in range(KT):
                        for x, h in enumerate((h_hi, h_lo)):
                            mm = pe.matmul(psum[4][:, 8 * t:8 * t + 8], h[:, k, P * t:P * t + P].bitcast(F32),
                                           w_gate[:, k, :], start=(k == 0 and x == 0), stop=(k == KT - 1 and x == 1))
                mm.then_inc(*T("product", "gates"))
                pe.wait_ge(*W("gate_v", "log_f"))
                pe.matmul(psum[4][:, 16:20], C["upper"], m_lf[:, 0, :], start=True, stop=True)
                pe.matmul(psum[4][:, 20:24], C["upper"], m_lf[:, 1, :], start=True, stop=False)
                mm = pe.matmul(psum[4][:, 20:24], ones, m_lf[:, 0, :], start=False, stop=True)
                mm.then_inc(*T("product", "cum"))
                pe.wait_ge(*W("gate_v", "a"))
                for n, v in enumerate((m_a, m_b)):
                    for t in range(2):
                        mm = pe.transpose(psum[5][0:A_HEADS, T1 * n + P * t:T1 * n + P * t + P], v[:, t, :], ident)
                mm.then_inc(*T("product", "rows"))
                pe.wait_ge(*W("gate_v", "rows"))
                for h in range(A_HEADS):
                    if h:
                        pe.wait_ge(*W("mix_v", ("masked", h - 1)))
                    pe.matmul(psum[0][:, :], ident[0:A_HEADS, h:h + 1].broadcast_to([A_HEADS, P]), m_rows[0:A_HEADS, :],
                              start=True, stop=True).then_inc(*T("product", ("bc", h)))
                    pe.matmul(psum[1][:, 0:T1], m_k[:, h, 0:P], m_q[:, h, :], start=True, stop=True)
                    pe.matmul(psum[1][:, T1:T1 + P], m_k[:, h, P:T1], m_q[:, h, P:T1], start=True, stop=True)\
                        .then_inc(*T("product", ("scores", h)))
                    pe.wait_ge(*W("mix_v", ("masked", h)))
                    if h:
                        pe.wait_ge(*W("mix_v", ("normed", h - 1)))
                    for o, lhs in ((psum[2][:, 0:T1], lambda s: ones),
                                   (psum[3][:, 0:T1], lambda s: m_v[:, s, A_V * h:A_V * h + P]),
                                   (psum[3][:, T1:T2], lambda s: m_v[:, s, A_V * h + P:A_V * h + A_V])):
                        pe.matmul(o, lhs(0), m_p[:, 0:T1], start=True, stop=False)
                        mm = pe.matmul(o[:, P:T1], lhs(1), m_p[:, T1:T1 + P], start=False, stop=True)
                    mm.then_inc(*T("product", ("sums", h)))
                    pe.wait_ge(*W("mix_a", ("squared", h)))
                    pe.matmul(psum[2][:, T1:T2], ones, m_d2[:, 0:T1], start=True, stop=False)
                    pe.matmul(psum[2][:, T1:T2], ones, m_d2[:, T1:T2], start=False, stop=True)\
                        .then_inc(*T("product", ("head_sq", h)))
                bank_user.clear()

            def diff():
                stage[0] = "mix1"
                for n in range(16):
                    b = 4 + n % 2
                    pe.wait_ge(*W("mix_a", ("sq", n)))
                    if n >= 2:
                        pe.wait_ge(*W("mix_v", ("roped", n - 2)))
                    pe.matmul(psum[b][:, 0:T1], C["block_ones"], d_sq[n % 2], start=True, stop=True)\
                        .then_inc(*T("product", ("sq", n)))
                    pe.wait_ge(*W("mix_v", ("normed", n)))
                    pe.matmul(psum[b][:, T1:T2], C["rope1"], (d_q if n < 8 else d_k)[:, n % 8, :], start=True, stop=True)\
                        .then_inc(*T("product", ("rot", n)))
                pe.wait_ge(*W("mix_v", ("roped", 15)))
                for b in range(4):
                    bank_ready(b)
                U = 2 * B_HEADS
                for u in range(U + 2):
                    if u < U:
                        h, qb = u // 2, u % 2
                        keys = P * (qb + 1)
                        if u >= 2:
                            pe.wait_ge(*W("mix_a", ("exp", u - 2)))
                        for x in range(2):
                            half = slice(64 * x, 64 * x + 64)
                            mm = pe.matmul(psum[4 * (u % 2) + x][:, 0:keys], d_q[half, h, P * qb:P * qb + P],
                                           d_k[half, h, 0:keys], start=True, stop=True)
                        mm.then_inc(*T("product", ("scores", u)))
                    if 1 <= u <= U:
                        v = u - 1
                        pe.wait_ge(*W("mix_v", ("probs", v)))
                        if v >= 2:
                            pe.wait_ge(*W("mix_a", ("turned", v - 2)))
                        for t in range(v % 2 + 1):
                            mm = pe.transpose(psum[2 + v % 2][:, P * t:P * t + P], d_p[v % 2][:, 0, P * t:P * t + P], ident)
                        mm.then_inc(*T("product", ("turn", v)))
                    if u >= 2 and (u - 2) % 2:
                        h = (u - 2) // 2
                        pe.wait_ge(*W("mix_a", ("turned", u - 2)))
                        if h >= 1:
                            pe.wait_ge(*W("h_ready", h - 1))
                        at = d_at[h % 2]
                        pe.matmul(psum[6][:, 0:T1], d_v[:, 0, P * h:P * h + P], at[:, 0, :], start=True, stop=False)
                        pe.matmul(psum[6][:, P:T1], d_v[:, 1, P * h:P * h + P], at[:, 1, P:T1], start=False, stop=True)\
                            .then_inc(*T("product", ("out", h)))
                        pe.wait_ge(*W("mix_a", ("osq", h)))
                        pe.matmul(psum[7][:, 0:T1], ones, d_sq[0], start=True, stop=True)\
                            .then_inc(*T("product", ("osum", h)))
                bank_user.clear()

            def attention(l):
                stage[0] = f"mix2.{l}"
                nq = T1 if l == DEPTH - 1 else T2
                pe.wait_ge(*W("consts2_in", 0, at="load"))
                for b in range(4):
                    bank_ready(b)
                for n in range(4):
                    w = T2 if n == 3 else nq
                    src = g_ka if n == 3 else g_q[:, n, :]
                    pe.wait_ge(*W("mix_a", ("sq", n)))
                    pe.matmul(psum[4][:, 0:w], C["block_ones"], g_p[n % 2][:, 0:w], start=True, stop=True)\
                        .then_inc(*T("product", ("sq", n)))
                    pe.wait_ge(*W("mix_v", ("normed", n)))
                    pe.matmul(psum[5][:, 0:T1], C2["rope2"], src[:, 0:T1], start=True, stop=True)\
                        .then_inc(*T("product", ("rot", n)))
                    pe.wait_ge(*W("mix_v", ("roped", n)))
                for n, dup in enumerate(("dup0", "dup1")):
                    pe.matmul(psum[4 + n][:, :], C2[dup], g_ka, start=True, stop=True)\
                        .then_inc(*T("product", ("dup", n)))
                pe.wait_ge(*W("mix_a", ("dup", 1)))
                pe.wait_ge(*W("mix_v", "conv"))
                us = units(l)
                for u in range(len(us) + 2):
                    if u < len(us):
                        s, hd, qb = us[u]
                        k0, k1 = keys_of(s)
                        tile, half = hd // 2, slice(64 * (hd % 2), 64 * (hd % 2) + 64)
                        k = g_kd[half, hd // 3, k0:k1] if hd < 6 else g_kb[half, tile - 3, k0:k1]
                        q0 = k0 * 0 + (T1 * s) + P * qb
                        if u >= 2:
                            pe.wait_ge(*W("mix_a", ("exp", u - 2)))
                        pe.matmul(psum[u % 2][:, 0:k1 - k0], g_q[half, tile, q0:q0 + P], k, start=True, stop=True)\
                            .then_inc(*T("product", ("scores", u)))
                    if 1 <= u <= len(us):
                        v = u - 1
                        s = us[v][0]
                        k0, k1 = keys_of(s)
                        pe.wait_ge(*W("mix_v", ("probs", v)))
                        if v >= 2:
                            pe.wait_ge(*W("mix_a", ("turned", v - 2)))
                        for t in range((k1 - k0) // P):
                            mm = pe.transpose(psum[2 + v % 2][:, P * t:P * t + P], g_p[v % 2][:, P * t:P * t + P], ident)
                        mm.then_inc(*T("product", ("turn", v)))
                    if u >= 2 and (u - 2) % 2:
                        v = u - 2
                        s, hd, _ = us[v]
                        k0, k1 = keys_of(s)
                        x = v // 2
                        half = slice(64 * (hd % 2), 64 * (hd % 2) + 64)
                        c0 = 64 * (hd // 3) if hd < 6 else P + 64 * (hd - 6)
                        pe.wait_ge(*W("mix_a", ("turned", v)))
                        if x >= 2:
                            pe.wait_ge(*W("h_ready", x - 2))
                        nt = (k1 - k0) // P
                        for t in range(nt):
                            mm = pe.matmul(psum[6 + x % 2][half, 0:T1], g_v[:, k0 // P + t, c0:c0 + 64],
                                           g_pt[x % 2][:, t, :], start=(t == 0), stop=(t == nt - 1))
                        mm.then_inc(*T("product", ("out", x)))
                bank_user.clear()

            def turn_out():
                stage[0] = "store"
                for t in range(2):
                    for j in range(KT):
                        if t == 0:
                            pe.wait_ge(*W("x_ready", j, at=f"post{LAST}"))
                        mm = pe.transpose(psum[2 * t + j // 4][:, P * (j % 4):P * (j % 4) + P], X[:, j, P * t:P * t + P], ident)
                        if j % 4 == 3:
                            mm.then_inc(*T("product", (t, j // 4)))

            pe.wait_ge(*W("small_in", "all", at="load"))
            pe.wait_ge(*W("setup", "act", at="load"))
            pe.wait_ge(*W("ones_set", 0, at="load"))
            for l in range(DEPTH):
                ada(f"ada1.{l}", 4, cact1, 1)
            for l in range(DEPTH):
                ada(f"ada2.{l}", 6, cact2, 2)
            turn_in()
            pe.wait_ge(*W("x_ready", KT - 1, at="turn_in"))
            sum_squares("norm0.0", T1)
            linear("mlstm", "norm0.0")
            mlstm()
            linear("mlstm_out", "mix0", per_tile=False)
            sum_squares("norm0.1", T1)
            moe(0)
            sum_squares("norm1.0", T1)
            linear("diff", "norm1.0")
            diff()
            linear("diff_out", "mix1", per_tile=False)
            sum_squares("norm1.1", T1)
            moe(1)
            for l in range(DEPTH):
                last = T1 if l == DEPTH - 1 else T2
                sum_squares(f"normffn{l}a", T2)
                ffn(l, 0)
                sum_squares(f"post{l}.0", T2)
                sum_squares(f"normin{l}", T2)
                linear(f"in{l}", f"normin{l}")
                attention(l)
                linear(f"attn_out{l}", f"mix2.{l}", per_tile=False)
                sum_squares(f"post{l}.1", last)
                sum_squares(f"normffn{l}b", last)
                ffn(l, 1)
                sum_squares(f"postffn{l}b", last)
            turn_out()

        @block.scalar
        def _(act):
            st = Stream()
            split_user = {}

            def step(ins, key=None):
                ins.then_inc(*T("act_step", ("n", log.count.get("act_step", 0))))
                act.wait_ge(sem("act_step"), log.count["act_step"])

            def split_hi(c, size, user, back=0):
                used, n = st.next(c % SLOTS)
                act.wait_ge(sem(f"raw_full{c % SLOTS}"), used * 16)
                if user:
                    act.wait_ge(*W("product", user[0], at=user[1], back=back))
                act.activation(w_hi[c % 2][:, 0:size], raw[c % SLOTS][:, 0:size], ACT.Copy).then_inc(sem("hi_ready"), 1)

            def ada(name, turns, M):
                stage[0] = name
                with act.Fori(0, turns) as i:
                    st.enter(i, SLOTS)
                    log.enter(name, i, turns)
                    for c in range(SLOTS):
                        used, _ = st.next(c)
                        if c % 2:
                            act.wait_ge(sem(f"raw_done{c}"), used + 1)
                            b = c // 2
                            ins = act.activation(ada_row[0:M, 512 * b:512 * b + 512], psum[b][0:M, :], ACT.Copy)
                    ins.then_inc(*T("ada_row", "row"))
                    log.leave()
                st.leave(turns)

            def norm(name, n, parts, x_at):
                stage[0] = name
                if x_at.endswith("_out"):
                    act.wait_ge(*W(*x_key(x_at, KT - 1)))
                for j in range(KT):
                    act.wait_ge(*W(*x_key(x_at, j)))
                    act.activation(squares[:, j, 0:n], X[:, j, 0:n], ACT.Square).then_inc(*T("squared", j))
                act.wait_ge(*W("product", "squares"))
                act.activation(rstd[:, 0:n], psum[3][:, 0:n], ACT.Sqrt, bias=epsc, scale=1.0 / D).then_inc(*T("rms", 0))
                for j in range(KT):
                    act.wait_ge(*W("scaled", j))
                    if j >= 2:
                        act.wait_ge(*W("h_ready", j - 2))
                    for a, b, sc, sh in parts:
                        ins = act.activation(full[j % 2][:, a:b], tmp[j % 2][:, a:b], ACT.Identity, bias=sh(j), scale=sc(j))
                    step(ins)
                    act.activation(h_hi[:, j, 0:n], full[j % 2][:, 0:n], ACT.Copy).then_inc(*T("h_upper", j))

            def post(name, n):
                stage[0] = name
                if name.endswith(".1"):
                    act.wait_ge(*W(*y_key(name, KT - 1)))
                for j in range(KT):
                    act.wait_ge(*W(*y_key(name, j)))
                    act.activation(squares[:, j, 0:n], Y[:, j, 0:n], ACT.Square).then_inc(*T("squared", j))
                act.wait_ge(*W("product", "squares"))
                act.activation(rstd[:, 0:n], psum[3][:, 0:n], ACT.Sqrt, bias=epsc, scale=1.0 / D).then_inc(*T("rms", 0))

            def linear(name, evac, following):
                stage[0] = name
                chunks = ITEMS[name]
                for c in range(len(chunks)):
                    if c + 1 < len(chunks):
                        split_hi(c + 1, SLOT, split_user.get((c + 1) % 2))
                    elif following:
                        split_hi(0, SLOT, split_user.get(0))
                    split_user[c % 2] = (last_item(name, c), name)
                    for n in range(len(chunks[c])):
                        if EVAC[name](c, n) == "evac_a":
                            act.wait_ge(*W("product", (c, n)))
                            evac(c, n).then_inc(*T("evac_a", (c, n)))

            def moe(l):
                name = stage[0] = f"moe{l}"
                act.wait_ge(*W("product", "router"))
                act.activation(e_s.rearrange("p t e -> p (t e)"), psum[0][:, 0:32], ACT.Sigmoid).then_inc(*T("scores", 0))
                with act.Fori(0, N_EXP) as i:
                    st.enter(i, EXP_CH)
                    log.enter(name, i, N_EXP)
                    for c in range(EXP_CH):
                        if c == 0:
                            split_hi(1, SLOT, (("down", 5), name), back=1)
                        elif c == EXP_CH - 1:
                            split_hi(0, SLOT, (("down", 4), name))
                        else:
                            split_hi(c + 1, SLOT, (("down" if c > 4 else "up", c - 1), name))
                        if c < 4:
                            act.wait_ge(*W("product", ("up", c)))
                            act.activation(tmp[c % 2][:, 0:T1], psum[c][:, 0:T1], ACT.Silu).then_inc(*T("silu", c))
                        if 1 <= c <= 4:
                            act.wait_ge(*W("gated", c - 1))
                            act.activation(e_hi[:, c - 1, :], full[(c - 1) % 2][:, 0:T1], ACT.Copy).then_inc(*T("act_upper", c - 1))
                    log.leave()
                st.leave(N_EXP)
                split_user[0], split_user[1] = (("down", 4), name), (("down", 5), name)

            def ffn(l, which, following):
                name = stage[0] = f"ffn{l}{'ab'[which]}"
                n = T1 if name == LAST else T2

                def group(tag, more):
                    for c in range(FFN_CH):
                        if c + 1 < FFN_CH:
                            user = ((tag, c - 1), name) if c else split_user.get(1)
                            split_hi(c + 1, SLOT if c + 1 < FFN_UP else DOWN, user)
                        if c < FFN_UP:
                            act.wait_ge(*W("product", (tag, c)))
                            act.activation(tmp[c % 2][:, 0:n], psum[2 * (c % 2)][:, 0:n], ACT.Silu).then_inc(*T("silu", (tag, c)))
                        if 1 <= c <= FFN_UP:
                            act.wait_ge(*W("gated", (tag, c - 1)))
                            act.activation(act_hi[:, c - 1, 0:n], full[(c - 1) % 2][:, 0:n], ACT.Copy)\
                                .then_inc(*T("act_upper", (tag, c - 1)))
                    if more:
                        split_hi(0, SLOT, ((tag, FFN_CH - 1), name))
                    split_user[0], split_user[1] = ((tag, FFN_CH - 1), name), ((tag, FFN_CH - 2), name)

                if name == LAST:
                    group("g0", True)
                    group("g1", following)
                else:
                    act.wait_ge(*W("product", split_user[1][0], at=split_user[1][1]))
                    split_user.pop(1)
                    with act.Fori(0, 2) as t:
                        st.enter(t, FFN_CH)
                        log.enter(name, t, 2)
                        group("g", True)
                        log.leave()
                    st.leave(2)

            def mlstm_evac(c, n):
                b = psum[bank_of("mlstm", c, n)][:, 0:T1]
                if c < 4:
                    j = 2 * (c % 2) + n
                    return act.activation((m_q if c < 2 else m_k)[:, j, :], b, ACT.Copy, scale=1.0 if c < 2 else A_QK ** -0.5)
                return act.activation(m_og[:, 2 * (c - 8) + n, :], b, ACT.Sigmoid)

            def mlstm():
                stage[0] = "mix0"
                act.wait_ge(*W("gate_v", "gates"))
                step(act.activation(m_u, m_g[:, :, A_HEADS:], ACT.Abs))
                step(act.activation(m_u, m_u, ACT.Exp, scale=-1.0))
                act.activation(m_u, m_u, ACT.Ln, bias=onec).then_inc(*T("mix_a", "log1p"))
                for h in range(A_HEADS):
                    act.wait_ge(*W("mix_v", ("gap", h)))
                    act.activation(m_d, m_d, ACT.Exp, scale=-1.0).then_inc(*T("mix_a", ("decay", h)))
                    act.activation(m_em, psum[0][:, T1:T2], ACT.Exp, scale=-1.0).then_inc(*T("mix_a", ("floor", h)))
                    act.wait_ge(*W("product", ("sums", h)))
                    act.activation(m_dn, psum[2][:, 0:T1], ACT.Abs).then_inc(*T("mix_a", ("den", h)))
                    act.wait_ge(*W("mix_v", ("normed", h)))
                    act.activation(m_d2, m_hh.rearrange("p a t -> p (a t)"), ACT.Square).then_inc(*T("mix_a", ("squared", h)))
                    act.wait_ge(*W("product", ("head_sq", h)))
                    act.activation(rstd[:, 0:T1], psum[2][:, T1:T2], ACT.Sqrt, bias=epsc, scale=1.0 / A_V).then_inc(*T("mix_a", ("rms", h)))
                    act.wait_ge(*W("mix_v", ("out", h)))
                    act.activation(h_hi[:, 2 * h:2 * h + 2, 0:T1], m_full, ACT.Copy).then_inc(*T("mix_a", ("upper", h)))

            def diff_evac(c, n):
                j = 2 * (c % 4) + n
                return act.activation((d_q if c < 4 else d_k)[:, j, :], psum[bank_of("diff", c, n)][:, 0:T1], ACT.Copy)

            def diff():
                stage[0] = "mix1"
                act.wait_ge(*W("mix_v", "angles"))
                act.activation(d_sin, d_ang, ACT.Sin)
                act.activation(d_n, d_n, ACT.Sin).then_inc(*T("mix_a", "sines"))
                act.wait_ge(*W("mix_v", "dots"))
                act.activation(d_ls[:, 2:4], d_ls[:, 0:2], ACT.Exp).then_inc(*T("mix_a", "lam"))
                for n in range(16):
                    if n == 0:
                        act.wait_ge(*W("evac_a", (7, 1), at="diff"))
                    if n >= 2:
                        act.wait_ge(*W("product", ("sq", n - 2)))
                    act.activation(d_sq[n % 2], (d_q if n < 8 else d_k)[:, n % 8, :], ACT.Square).then_inc(*T("mix_a", ("sq", n)))
                    act.wait_ge(*W("product", ("sq", n)))
                    if n >= 2:
                        act.wait_ge(*W("mix_v", ("normed", n - 2)))
                    act.activation(d_rs[n % 2], psum[4 + n % 2][:, 0:T1], ACT.Sqrt, bias=epsc, scale=1.0 / B_HD)\
                        .then_inc(*T("mix_a", ("rms", n)))
                U = 2 * B_HEADS
                for u in range(U + 2):
                    if u < U:
                        keys = P * (u % 2 + 1)
                        act.wait_ge(*W("mix_v", ("max", u)))
                        if u >= 2:
                            act.wait_ge(*W("product", ("turn", u - 2)))
                        for x in range(2):
                            ins = act.activation(d_p[u % 2][:, x, 0:keys], psum[4 * (u % 2) + x][:, 0:keys], ACT.Exp,
                                                 bias=d_st[u % 2][:, x:x + 1], accum_out=d_st[u % 2][:, 2 + x:3 + x])
                        ins.then_inc(*T("mix_a", ("exp", u)))
                    if 1 <= u <= U:
                        v = u - 1
                        act.wait_ge(*W("product", ("turn", v)))
                        if v >= 4:
                            act.wait_ge(*W("product", ("out", v // 2 - 2)))
                        t = v % 2 + 1
                        act.activation(d_at[(v // 2) % 2][:, 0:t, P * (v % 2):P * (v % 2) + P],
                                       psum[2 + v % 2][:, 0:P * t].rearrange("p (t n) -> p t n", t=t), ACT.Copy)\
                            .then_inc(*T("mix_a", ("turned", v)))
                    if u >= 2 and (u - 2) % 2:
                        h = (u - 2) // 2
                        act.wait_ge(*W("product", ("out", h)))
                        act.activation(d_sq[0], psum[6][:, 0:T1], ACT.Square).then_inc(*T("mix_a", ("osq", h)))
                        act.wait_ge(*W("product", ("osum", h)))
                        act.activation(d_rs[0], psum[7][:, 0:T1], ACT.Sqrt, bias=epsc, scale=1.0 / (2 * B_HD)).then_inc(*T("mix_a", ("orms", h)))
                        act.wait_ge(*W("mix_v", ("out", h)))
                        act.activation(h_hi[:, h, 0:T1], d_raw[0], ACT.Copy).then_inc(*T("mix_a", ("upper", h)))

            def in_evac(name, l):
                nq = T1 if l == DEPTH - 1 else T2

                def f(c, n):
                    bank = psum[bank_of(name, c, n)]
                    if c < 3:
                        j = 2 * c + n
                        return act.activation(g_q[:, j, 0:nq], bank[:, 0:nq], ACT.Copy, scale=1.0 if j < 3 else HD ** -0.5)
                    if c == 3:
                        return act.activation(g_ka, bank[:, :], ACT.Copy)
                    if c in (4, 5):
                        return act.activation(g_kb[:, 2 * (c - 4) + n, :], bank[:, :], ACT.Copy)
                    dst = (g_cx, g_cb, g_cc)[c - 7]
                    return act.activation(dst[:, n, 0:nq], bank[:, 0:nq], ACT.Copy)
                return f

            def attention(l):
                stage[0] = f"mix2.{l}"
                nq = T1 if l == DEPTH - 1 else T2
                for n in range(4):
                    w = T2 if n == 3 else nq
                    src = g_ka if n == 3 else g_q[:, n, :]
                    if n == 0:
                        act.wait_ge(*W("evac_a", (9, 1), at=f"in{l}"))
                    if n >= 2:
                        act.wait_ge(*W("product", ("sq", n - 2)))
                    act.activation(g_p[n % 2][:, 0:w], src[:, 0:w], ACT.Square).then_inc(*T("mix_a", ("sq", n)))
                    act.wait_ge(*W("product", ("sq", n)))
                    if n:
                        act.wait_ge(*W("mix_v", ("normed", n - 1)))
                    act.activation(rstd[:, 0:w], psum[4][:, 0:w], ACT.Sqrt, bias=epsc, scale=1.0 / HD).then_inc(*T("mix_a", ("rms", n)))
                for n in range(2):
                    act.wait_ge(*W("product", ("dup", n)))
                    act.activation(g_kd[:, n, :], psum[4 + n][:, :], ACT.Copy).then_inc(*T("mix_a", ("dup", n)))
                for n in range(2):
                    act.wait_ge(*W("mix_v", ("conv", n)))
                    act.activation(h_hi[:, 6 + n, 0:nq], full[0][:, 0:nq], ACT.Copy).then_inc(*T("mix_a", ("conv", n)))
                us = units(l)
                for u in range(len(us) + 2):
                    if u < len(us):
                        s = us[u][0]
                        k0, k1 = keys_of(s)
                        act.wait_ge(*W("mix_v", ("max", u)))
                        if u >= 2:
                            act.wait_ge(*W("product", ("turn", u - 2)))
                        act.activation(g_p[u % 2][:, 0:k1 - k0], psum[u % 2][:, 0:k1 - k0], ACT.Exp,
                                       bias=g_st[u % 2][:, 0:1], accum_out=g_st[u % 2][:, 1:2]).then_inc(*T("mix_a", ("exp", u)))
                    if 1 <= u <= len(us):
                        v = u - 1
                        s, hd, qb = us[v]
                        k0, k1 = keys_of(s)
                        nt = (k1 - k0) // P
                        act.wait_ge(*W("product", ("turn", v)))
                        if v >= 4:
                            act.wait_ge(*W("product", ("out", v // 2 - 2)))
                        if v == 0:
                            act.wait_ge(*W("mix_v", "conv"))
                        act.activation(g_pt[(v // 2) % 2][:, 0:nt, P * qb:P * qb + P],
                                       psum[2 + v % 2][:, 0:P * nt].rearrange("p (t n) -> p t n", t=nt), ACT.Copy)\
                            .then_inc(*T("mix_a", ("turned", v)))
                    if u >= 2 and (u - 2) % 2:
                        v = u - 2
                        s, hd, _ = us[v]
                        x = v // 2
                        half = slice(64 * (hd % 2), 64 * (hd % 2) + 64)
                        act.wait_ge(*W("product", ("out", x)))
                        act.activation(h_hi[half, hd // 2, T1 * s:T1 * s + T1], psum[6 + x % 2][half, 0:T1], ACT.Copy)\
                            .then_inc(*T("mix_a", ("upper", x)))

            act.wait_ge(*W("small_in", "all", at="load"))
            act.activation(cact1, V["c1"], ACT.Silu)
            act.activation(cact2.rearrange("p k s -> p (k s)"), V["c2"], ACT.Silu).then_inc(*T_at("setup", "act"))
            for l in range(DEPTH):
                ada(f"ada1.{l}", 4, 1)
            for l in range(DEPTH):
                ada(f"ada2.{l}", 6, 2)
            split_hi(0, SLOT, None)
            part1 = lambda l, w: [(0, T1, lambda j: pre1[:, l, w, j:j + 1], lambda j: mod1[:, l, 24 * w + j:24 * w + j + 1])]
            part2 = lambda l, i, both: [(T1 * s, T1 * s + T1, lambda j, s=s: pre2[:, l, i, j, s:s + 1],
                                         lambda j, s=s: mod2[:, l, 3 * i, j, s:s + 1]) for s in range(1 + both)]
            act.wait_ge(*W("mods", 0, at="load"))
            norm("norm0.0", T1, part1(0, 0), "turn_in")
            linear("mlstm", mlstm_evac, True)
            mlstm()
            linear("mlstm_out", None, True)
            norm("norm0.1", T1, part1(0, 1), "mlstm_out")
            moe(0)
            norm("norm1.0", T1, part1(1, 0), "moe0")
            linear("diff", diff_evac, True)
            diff()
            linear("diff_out", None, True)
            norm("norm1.1", T1, part1(1, 1), "diff_out")
            moe(1)
            for l in range(DEPTH):
                both = l < DEPTH - 1
                n = T2 if both else T1
                norm(f"normffn{l}a", T2, part2(l, 0, 1), "moe1" if l == 0 else f"postffn{l - 1}b")
                ffn(l, 0, True)
                post(f"post{l}.0", T2)
                norm(f"normin{l}", T2, part2(l, 1, 1), f"post{l}.0")
                linear(f"in{l}", in_evac(f"in{l}", l), True)
                attention(l)
                linear(f"attn_out{l}", None, True)
                post(f"post{l}.1", n)
                norm(f"normffn{l}b", n, part2(l, 2, both), f"post{l}.1")
                ffn(l, 1, both)
                post(f"postffn{l}b", n)

        @block.vector
        def _(dve):
            st = Stream()

            def step(ins):
                ins.then_inc(*T("vec_step"))
                dve.wait_ge(sem("vec_step"), log.count["vec_step"])

            def split_lo(c, size):
                _, n = st.next(c % SLOTS)
                dve.wait_ge(sem("hi_ready"), n - ADA_CHUNKS)
                dve.tensor_tensor(w_lo[c % 2][:, 0:size], raw[c % SLOTS][:, 0:size], w_hi[c % 2][:, 0:size].bitcast(F32),
                                  ALU.subtract).then_inc(sem(f"raw_done{c % SLOTS}"), 1)

            def ada(name, turns, dst, M):
                stage[0] = name
                with dve.Fori(0, turns) as i:
                    log.enter(name, i, turns)
                    dve.wait_ge(*W("product", "cols"))
                    dve.tensor_copy(dst[:, ds(i * 12 * M, 12 * M)], psum[3][:, 0:12 * M]).then_inc(*T("ada_col", "col"))
                    log.leave()
                st.all += SLOTS * turns
                for s in range(SLOTS):
                    st.slot[s] += turns

            def mods():
                dve.wait_ge(*W("ada_col", "col", at="ada2.1"))
                m1, m2 = mod1.rearrange("p l m -> p (l m)"), mod2.rearrange("p l m k s -> p (l m k) s")
                step(dve.tensor_tensor(m1, m1, V["b_ada"], ALU.add))
                for s in range(2):
                    ins = dve.tensor_tensor(m2[:, :, s], m2[:, :, s], V["b_ada_2"], ALU.add)
                step(ins)
                for l in range(DEPTH):
                    for w in range(2):
                        ins = dve.scalar_tensor_tensor(pre1[:, l, w, :], mod1[:, l, 24 * w + 8:24 * w + 16], 1.0,
                                                       V["norm1" if w == 0 else "norm2"][:, 8 * l:8 * l + 8], ALU.add, ALU.mult)
                    ng = V["norm_g_2"].rearrange("p (l g k) -> p l g k", l=DEPTH, g=6)
                    for i in range(3):
                        for s in range(2):
                            dve.scalar_tensor_tensor(pre2[:, l, i, :, s], mod2[:, l, 3 * i + 1, :, s], 1.0, ng[:, l, 2 * i, :],
                                                     ALU.add, ALU.mult)
                            ins = dve.scalar_tensor_tensor(post2[:, l, i, :, s], mod2[:, l, 3 * i + 2, :, s],
                                                           1.0 if i == 1 else 0.5, ng[:, l, 2 * i + 1, :], ALU.mult, ALU.mult)
                ins.then_inc(*T_at("mods", 0))
                dve.wait_ge(*W("mods", 0, at="load"))

            def turn_in():
                stage[0] = "turn_in"
                for j in range(KT):
                    dve.wait_ge(*W("product", j))
                    dve.tensor_copy(X[:, j, :], psum[j][:, :]).then_inc(*T("x_ready", j))

            def reciprocal_rms(n):
                dve.wait_ge(*W("rms", 0))
                step(dve.reciprocal(rstd[:, 0:n], rstd[:, 0:n]))

            def norm(name, n):
                stage[0] = name
                reciprocal_rms(n)
                for j in range(KT + 1):
                    if j < KT:
                        if j >= 2:
                            dve.wait_ge(*W("h_upper", j - 2))
                        dve.tensor_tensor(tmp[j % 2][:, 0:n], X[:, j, 0:n], rstd[:, 0:n], ALU.mult).then_inc(*T("scaled", j))
                    if j:
                        dve.wait_ge(*W("h_upper", j - 1))
                        dve.tensor_tensor(h_lo[:, j - 1, 0:n], full[(j - 1) % 2][:, 0:n], h_hi[:, j - 1, 0:n].bitcast(F32),
                                          ALU.subtract).then_inc(*T("h_ready", j - 1))

            def post(name, n, l, i):
                stage[0] = name
                reciprocal_rms(n)
                for j in range(KT + 1):
                    if j < KT:
                        if j >= 2:
                            dve.wait_ge(*W("x_ready", j - 2))
                        dve.tensor_tensor(tmp[j % 2][:, 0:n], Y[:, j, 0:n], rstd[:, 0:n], ALU.mult).then_inc(*T("scaled", j))
                    if j:
                        k = j - 1
                        dve.wait_ge(*W("scaled", k))
                        for s in range(n // T1):
                            cut = slice(T1 * s, T1 * s + T1)
                            ins = dve.scalar_tensor_tensor(X[:, k, cut], tmp[k % 2][:, cut], post2[:, l, i, k, s:s + 1],
                                                           X[:, k, cut], ALU.mult, ALU.add)
                        ins.then_inc(*T("x_ready", k))
                dve.wait_ge(*W("x_ready", KT - 1))

            def linear(name, evac, following):
                stage[0] = name
                chunks = ITEMS[name]
                for c in range(len(chunks)):
                    if c + 1 < len(chunks):
                        split_lo(c + 1, SLOT)
                    elif following:
                        split_lo(0, SLOT)
                    for n in range(len(chunks[c])):
                        if EVAC[name](c, n) == "evac_v":
                            dve.wait_ge(*W("product", (c, n)))
                            evac(c, n).then_inc(*T("evac_v", (c, n)))

            def residual(name, l, w):
                def f(c, n):
                    j = 2 * c + n
                    return dve.scalar_tensor_tensor(X[:, j, 0:T1], psum[bank_of(name, c, n)][:, 0:T1],
                                                    mod1[:, l, 24 * w + 16 + j:24 * w + 17 + j], X[:, j, 0:T1], ALU.mult, ALU.add)
                return f

            def moe(l):
                name = stage[0] = f"moe{l}"
                dve.memset(e_zero.bitcast(U32), 0)
                dve.wait_ge(*W("scores", 0))
                for t in range(2):
                    step(dve.tensor_tensor(e_b[:, t, :], e_s[:, t, :], V["router_bias"], ALU.add))
                for t in range(2):
                    b = e_b[:, t, :].rearrange("p (g e) -> p g e", g=N_GRP)
                    pairs = [(x, y) for x in range(E_GRP) for y in range(x + 1, E_GRP)]
                    for n, (x, y) in enumerate(pairs):
                        ins = dve.tensor_tensor(e_pair[:, :, n:n + 1], b[:, :, x:x + 1], b[:, :, y:y + 1], ALU.add)
                    step(ins)
                    step(dve.memset(e_g8, INVALID))
                    step(dve.tensor_reduce(e_g8[:, 0:N_GRP], e_pair, AX.X, ALU.max))
                    step(dve.max(e_x8, e_g8))
                    step(dve.max_index(e_i8, e_x8, e_g8))
                    step(dve.tensor_copy(e_f8, e_i8))
                    step(dve.tensor_scalar(e_oh, C["iota8"], e_f8[:, 0:1], None, ALU.is_equal))
                    for q in range(N_GRP):
                        ins = dve.tensor_scalar(e_m[:, t, 4 * q:4 * q + 4], e_b[:, t, 4 * q:4 * q + 4], e_oh[:, q:q + 1], None, ALU.mult)
                    step(ins)
                    step(dve.tensor_scalar(e_oh, e_oh, -1.0, -INVALID, ALU.add, ALU.mult))
                    for q in range(N_GRP):
                        ins = dve.tensor_scalar(e_m[:, t, 4 * q:4 * q + 4], e_m[:, t, 4 * q:4 * q + 4], e_oh[:, q:q + 1], None, ALU.add)
                    step(ins)
                    step(dve.max(e_x8, e_m[:, t, :]))
                    step(dve.max_index(e_i8, e_x8, e_m[:, t, :]))
                    step(dve.tensor_copy(e_f8, e_i8))
                    step(dve.tensor_scalar(e_w[:, t, :], C["iota16"], e_f8[:, 0:1], None, ALU.is_equal))
                    step(dve.scalar_tensor_tensor(e_w[:, t, :], C["iota16"], e_f8[:, 1:2], e_w[:, t, :], ALU.is_equal, ALU.add))
                    step(dve.tensor_tensor(e_w[:, t, :], e_w[:, t, :], e_s[:, t, :], ALU.mult))
                    step(dve.tensor_reduce(e_f8[:, 0:1], e_w[:, t, :], AX.X, ALU.add))
                    step(dve.reciprocal(e_f8[:, 1:2], e_f8[:, 0:1]))
                    ins = dve.tensor_scalar(e_w[:, t, :], e_w[:, t, :], e_f8[:, 1:2], None, ALU.mult)
                    if t == 0:
                        step(ins)
                ins.then_inc(*T("gate_w", "tokens"))
                dve.wait_ge(*W("product", "gate_rows"))
                dve.tensor_copy(e_row, psum[0][0:N_EXP, 128:128 + T1]).then_inc(*T("gate_w", "rows"))
                for x in range(N_EXP):
                    dve.wait_ge(*W("product", ("bc", x)))
                    dve.tensor_copy(e_gate[:, x, :], psum[x % 4][:, 0:T1]).then_inc(*T("gate_bc", x))
                dve.wait_ge(*W("gate_bc", N_EXP - 1))
                with dve.Fori(0, N_EXP) as i:
                    st.enter(i, EXP_CH)
                    log.enter(name, i, N_EXP)

                    def lower(c):
                        dve.wait_ge(*W("act_upper", c))
                        dve.tensor_tensor(e_lo[:, c, :], full[c % 2][:, 0:T1], e_hi[:, c, :].bitcast(F32), ALU.subtract)\
                            .then_inc(*T("act_ready", c))

                    for c in range(EXP_CH):
                        split_lo((c + 1) % EXP_CH, SLOT)
                        if c < 4:
                            dve.wait_ge(*W("silu", c))
                            dve.tensor_tensor(tmp[c % 2][:, T1:T2], tmp[c % 2][:, 0:T1], e_gate[:, ds(i, 1), :].rearrange("p e t -> p (e t)"), ALU.mult)\
                                .then_inc(*T("weighted", c))
                            dve.wait_ge(*W("weighted", c))
                            dve.tensor_tensor(full[c % 2][:, 0:T1], psum[c][:, T1:T2], tmp[c % 2][:, T1:T2], ALU.mult)\
                                .then_inc(*T("gated", c))
                        if 1 <= c <= 4:
                            lower(c - 1)
                    log.leave()
                st.leave(N_EXP)
                dve.wait_ge(*W("product", ("down", 5)))
                for j in range(KT):
                    dve.scalar_tensor_tensor(X[:, j, 0:T1], psum[4 + j // 2][:, T1 * (j % 2):T1 * (j % 2) + T1],
                                             mod1[:, l, 40 + j:41 + j], X[:, j, 0:T1], ALU.mult, ALU.add).then_inc(*T("x_ready", j))

            def ffn(l, which, following):
                name = stage[0] = f"ffn{l}{'ab'[which]}"
                n = T1 if name == LAST else T2
                step(dve.memset(Y, 0.0))

                def group(tag, more):
                    def lower(c):
                        dve.wait_ge(*W("act_upper", (tag, c)))
                        dve.tensor_tensor(act_lo[:, c, 0:n], full[c % 2][:, 0:n], act_hi[:, c, 0:n].bitcast(F32), ALU.subtract)\
                            .then_inc(*T("act_ready", (tag, c)))

                    for c in range(FFN_CH):
                        if c + 1 < FFN_CH:
                            split_lo(c + 1, SLOT if c + 1 < FFN_UP else DOWN)
                        if c < FFN_UP:
                            dve.wait_ge(*W("silu", (tag, c)))
                            if c >= 2:
                                dve.wait_ge(*W("act_ready", (tag, c - 2)))
                            dve.tensor_tensor(full[c % 2][:, 0:n], psum[2 * (c % 2) + 1][:, 0:n], tmp[c % 2][:, 0:n], ALU.mult)\
                                .then_inc(*T("gated", (tag, c)))
                        if 1 <= c <= FFN_UP:
                            lower(c - 1)
                            if c == FFN_UP:
                                dve.wait_ge(*W("act_ready", (tag, c - 1)))
                        if c >= FFN_UP:
                            j = c - FFN_UP
                            dve.wait_ge(*W("product", (tag, c)))
                            dve.tensor_tensor(Y[:, j, 0:n], Y[:, j, 0:n], psum[4 + j % 4][:, 0:n], ALU.add)\
                                .then_inc(*T("y_ready", (tag, j)))
                    if more:
                        split_lo(0, SLOT)

                if name == LAST:
                    group("g0", True)
                    group("g1", following)
                else:
                    with dve.Fori(0, 2) as t:
                        st.enter(t, FFN_CH)
                        log.enter(name, t, 2)
                        group("g", True)
                        log.leave()
                    st.leave(2)

            def mlstm_evac(c, n):
                return dve.tensor_copy(m_v[:, :, 256 * (c - 4):256 * (c - 4) + 256],
                                       psum[bank_of("mlstm", c, n)][:, :].rearrange("p (t n) -> p t n", t=2))

            def mlstm():
                stage[0] = "mix0"
                dve.wait_ge(*W("product", "gates"))
                for t in range(2):
                    ins = dve.tensor_tensor(m_g[:, t, :], psum[4][:, 8 * t:8 * t + 8], V["b_if"], ALU.add)
                ins.then_inc(*T("gate_v", "gates"))
                dve.wait_ge(*W("mix_a", "log1p"))
                dve.scalar_tensor_tensor(m_lf, m_g[:, :, A_HEADS:], 0.0, m_u, ALU.min, ALU.subtract).then_inc(*T("gate_v", "log_f"))
                dve.wait_ge(*W("product", "cum"))
                step(dve.tensor_copy(m_b.rearrange("p t h -> p (t h)"), psum[4][:, 16:24]))
                dve.tensor_tensor(m_a, m_g[:, :, 0:A_HEADS], m_b, ALU.subtract).then_inc(*T("gate_v", "a"))
                dve.wait_ge(*W("product", "rows"))
                step(dve.tensor_copy(m_arow[0:A_HEADS, :], psum[5][0:A_HEADS, 0:T1]))
                step(dve.tensor_tensor_scan(m_rows[0:A_HEADS, 0:T1], m_arow[0:A_HEADS, :], m_arow[0:A_HEADS, :], 0.0, ALU.max, ALU.max))
                dve.tensor_tensor(m_rows[0:A_HEADS, T1:T2], m_rows[0:A_HEADS, 0:T1], psum[5][0:A_HEADS, T1:T2], ALU.add)\
                    .then_inc(*T("gate_v", "rows"))
                for h in range(A_HEADS):
                    dve.wait_ge(*W("product", ("bc", h)))
                    dve.tensor_scalar(m_d[:, 0:T1], psum[0][:, 0:T1], m_a[:, 0, h:h + 1], 0.0, ALU.subtract, ALU.max)
                    dve.tensor_scalar(m_d[:, T1:T1 + P], psum[0][:, P:T1], m_a[:, 1, h:h + 1], 0.0, ALU.subtract, ALU.max)\
                        .then_inc(*T("mix_v", ("gap", h)))
                    dve.wait_ge(*W("mix_a", ("floor", h)))
                    dve.wait_ge(*W("product", ("scores", h)))
                    step(dve.tensor_tensor(m_p, psum[1][:, 0:384], m_d, ALU.mult))
                    dve.tensor_tensor(m_p[:, 0:P], m_p[:, 0:P], C["upper"], ALU.mult)
                    dve.tensor_tensor(m_p[:, T1:T1 + P], m_p[:, T1:T1 + P], C["upper"], ALU.mult).then_inc(*T("mix_v", ("masked", h)))
                    dve.wait_ge(*W("mix_a", ("den", h)))
                    step(dve.tensor_tensor(m_dn, m_dn, m_em, ALU.max))
                    step(dve.reciprocal(m_dn, m_dn))
                    for q in range(2):
                        ins = dve.tensor_tensor(m_hh[:, q, :], psum[3][:, T1 * q:T1 * q + T1], m_dn, ALU.mult)
                    ins.then_inc(*T("mix_v", ("normed", h)))
                    dve.wait_ge(*W("mix_v", ("normed", h)))
                    dve.wait_ge(*W("mix_a", ("rms", h)))
                    step(dve.reciprocal(rstd[:, 0:T1], rstd[:, 0:T1]))
                    for q in range(2):
                        j = 2 * h + q
                        ins = dve.scalar_tensor_tensor(m_full[:, q, :], m_hh[:, q, :], V["a_h_norm"][:, j:j + 1], rstd[:, 0:T1], ALU.mult, ALU.mult)
                    step(ins)
                    dve.tensor_tensor(m_full, m_full, m_og[:, 2 * h:2 * h + 2, :], ALU.mult).then_inc(*T("mix_v", ("out", h)))
                    dve.wait_ge(*W("mix_a", ("upper", h)))
                    ins = dve.tensor_tensor(h_lo[:, 2 * h:2 * h + 2, 0:T1], m_full, h_hi[:, 2 * h:2 * h + 2, 0:T1].bitcast(F32), ALU.subtract)
                    ins.then_inc(*T("h_ready", h))

            def diff_evac(c, n):
                return dve.tensor_copy(d_v[:, :, 256 * (c - 8):256 * (c - 8) + 256],
                                       psum[bank_of("diff", c, n)][:, :].rearrange("p (t n) -> p t n", t=2))

            def diff():
                stage[0] = "mix1"
                TWO_PI = 2 * math.pi
                c1 = 6.28125
                c2 = float(np.float32(np.round((TWO_PI - c1) * 2 ** 22) / 2 ** 22))
                c3 = float(np.float32(TWO_PI - c1 - c2))
                ROUND = 1.5 * 2 ** 23
                dve.wait_ge(*W("diff_in", "all", at="load"))
                step(dve.tensor_copy(d_ang, d_pos))
                step(dve.tensor_scalar(d_ang, d_ang, C["invfreq"], None, ALU.mult))
                step(dve.tensor_scalar(d_n, d_ang, 1.0 / TWO_PI, ROUND, ALU.mult, ALU.add))
                step(dve.tensor_scalar(d_n, d_n, ROUND, None, ALU.subtract))
                for cc in (c1, c2, c3):
                    step(dve.scalar_tensor_tensor(d_ang, d_n, -cc, d_ang, ALU.mult, ALU.add))
                step(dve.tensor_scalar(d_ang, d_ang, math.pi - 1e-6, -(math.pi - 1e-6), ALU.min, ALU.max))
                dve.tensor_scalar(d_n, d_ang, 0.5, None, ALU.mult).then_inc(*T("mix_v", "angles"))
                dve.wait_ge(*W("mix_a", "sines"))
                step(dve.tensor_tensor(d_cos, d_n, d_n, ALU.mult))
                step(dve.tensor_scalar(d_cos, d_cos, -2.0, 1.0, ALU.mult, ALU.add))
                for n in range(2):
                    step(dve.tensor_tensor(d_lam[:, 2 * n, :], d_lam[:, 2 * n, :], d_lam[:, 2 * n + 1, :], ALU.mult))
                    ins = dve.tensor_reduce(d_ls[:, n:n + 1], d_lam[:, 2 * n, :], AX.X, ALU.add)
                ins.then_inc(*T("mix_v", "dots"))
                dve.wait_ge(*W("mix_a", "lam"))
                step(dve.tensor_tensor(d_ls[:, 4:5], d_ls[:, 3:4], d_ls[:, 2:3], ALU.subtract))
                step(dve.tensor_scalar(d_ls[:, 5:6], d_ls[:, 4:5], LAM_INIT, None, ALU.subtract))
                for n in range(16):
                    x = (d_q if n < 8 else d_k)[:, n % 8, :]
                    gain = V["b_q_norm" if n < 8 else "b_k_norm"]
                    dve.wait_ge(*W("mix_a", ("rms", n)))
                    step(dve.reciprocal(d_rs[n % 2], d_rs[n % 2]))
                    if n < 8:
                        step(dve.tensor_scalar(d_rs[n % 2], d_rs[n % 2], B_HD ** -0.5, None, ALU.mult))
                    dve.scalar_tensor_tensor(x, x, gain, d_rs[n % 2], ALU.mult, ALU.mult).then_inc(*T("mix_v", ("normed", n)))
                    dve.wait_ge(*W("product", ("rot", n)))
                    step(dve.tensor_tensor(d_raw[n % 2], psum[4 + n % 2][:, T1:T2], d_sin, ALU.mult))
                    step(dve.tensor_tensor(x, x, d_cos, ALU.mult))
                    dve.tensor_tensor(x, x, d_raw[n % 2], ALU.add).then_inc(*T("mix_v", ("roped", n)))
                U = 2 * B_HEADS
                for u in range(U + 2):
                    if u < U:
                        keys = P * (u % 2 + 1)
                        dve.wait_ge(*W("product", ("scores", u)))
                        for x in range(2):
                            s = psum[4 * (u % 2) + x]
                            ins = dve.tensor_tensor(s[:, keys - P:keys], s[:, keys - P:keys], C["causal"], ALU.add)
                        step(ins)
                        for x in range(2):
                            ins = dve.tensor_reduce(d_st[u % 2][:, x:x + 1], psum[4 * (u % 2) + x][:, 0:keys], AX.X, ALU.max, negate=True)
                        ins.then_inc(*T("mix_v", ("max", u)))
                    if 1 <= u <= U:
                        v = u - 1
                        stt, p = d_st[v % 2], d_p[v % 2]
                        keys = P * (v % 2 + 1)
                        dve.wait_ge(*W("mix_a", ("exp", v)))
                        step(dve.reciprocal(stt[:, 4:6], stt[:, 2:4]))
                        step(dve.tensor_scalar(stt[:, 5:6], stt[:, 5:6], d_ls[:, 5:6], None, ALU.mult))
                        step(dve.tensor_scalar(p[:, 1, 0:keys], p[:, 1, 0:keys], stt[:, 5:6], None, ALU.mult))
                        dve.scalar_tensor_tensor(p[:, 0, 0:keys], p[:, 0, 0:keys], stt[:, 4:5], p[:, 1, 0:keys], ALU.mult, ALU.add)\
                            .then_inc(*T("mix_v", ("probs", v)))
                    if u >= 2 and (u - 2) % 2:
                        h = (u - 2) // 2
                        dve.wait_ge(*W("mix_a", ("orms", h)))
                        step(dve.reciprocal(d_rs[0], d_rs[0]))
                        step(dve.scalar_tensor_tensor(d_raw[0], psum[6][:, 0:T1], V["b_o_norm"], d_rs[0], ALU.mult, ALU.mult))
                        dve.tensor_scalar(d_raw[0], d_raw[0], 1.0 - LAM_INIT, None, ALU.mult).then_inc(*T("mix_v", ("out", h)))
                        dve.wait_ge(*W("mix_a", ("upper", h)))
                        dve.tensor_tensor(h_lo[:, h, 0:T1], d_raw[0], h_hi[:, h, 0:T1].bitcast(F32), ALU.subtract).then_inc(*T("h_ready", h))

            def in_evac(name, l):
                def f(c, n):
                    bank = psum[bank_of(name, c, n)]
                    if c in (3, 5):
                        at = 0 if c == 3 else P
                        return dve.tensor_copy(g_v[:, :, at:at + P], bank[:, :].rearrange("p (t n) -> p t n", t=4))
                    return dve.tensor_copy(g_v[:, 2 * n:2 * n + 2, 256:512], bank[:, :].rearrange("p (t n) -> p t n", t=2))
                return f

            def y_evac(name, n_tok):
                def f(c, n):
                    return dve.tensor_copy(Y[:, 2 * c + n, 0:n_tok], psum[bank_of(name, c, n)][:, 0:n_tok])
                return f

            def attention(l):
                stage[0] = f"mix2.{l}"
                nq = T1 if l == DEPTH - 1 else T2
                qk = V["qk_g_2"]
                dve.wait_ge(*W("consts2_in", 0, at="load"))
                for n in range(4):
                    w = T2 if n == 3 else nq
                    src = g_ka if n == 3 else g_q[:, n, :]
                    dve.wait_ge(*W("mix_a", ("rms", n)))
                    step(dve.reciprocal(rstd[:, 0:w], rstd[:, 0:w]))
                    if n < 3:
                        step(dve.tensor_scalar(rstd[:, 0:w], rstd[:, 0:w], HD ** -0.5, None, ALU.mult))
                    dve.scalar_tensor_tensor(src[:, 0:w], src[:, 0:w], qk[:, 2 * l + n // 3:2 * l + n // 3 + 1], rstd[:, 0:w],
                                             ALU.mult, ALU.mult).then_inc(*T("mix_v", ("normed", n)))
                    dve.wait_ge(*W("product", ("rot", n)))
                    step(dve.tensor_tensor(full[0][:, 0:T1], psum[5][:, 0:T1], C2["sin2"], ALU.mult))
                    step(dve.tensor_tensor(src[:, 0:T1], src[:, 0:T1], C2["cos2"], ALU.mult))
                    dve.tensor_tensor(src[:, 0:T1], src[:, 0:T1], full[0][:, 0:T1], ALU.add).then_inc(*T("mix_v", ("roped", n)))
                dve.wait_ge(*W("evac_a", (9, 1), at=f"in{l}"))
                w = V["conv_w_2"].rearrange("p (l t n) -> p l t n", l=DEPTH, t=3)
                for n in range(2):
                    step(dve.tensor_tensor(g_cx[:, n, 0:nq], g_cx[:, n, 0:nq], g_cc[:, n, 0:nq], ALU.mult))
                    step(dve.tensor_scalar(tmp[0][:, 0:nq], g_cx[:, n, 0:nq], w[:, l, 1, n:n + 1], None, ALU.mult))
                    for s in range(nq // T1):
                        a, b = T1 * s, T1 * s + T1
                        step(dve.scalar_tensor_tensor(tmp[0][:, a + 1:b], g_cx[:, n, a:b - 1], w[:, l, 0, n:n + 1], tmp[0][:, a + 1:b], ALU.mult, ALU.add))
                        step(dve.scalar_tensor_tensor(tmp[0][:, a:b - 1], g_cx[:, n, a + 1:b], w[:, l, 2, n:n + 1], tmp[0][:, a:b - 1], ALU.mult, ALU.add))
                    dve.tensor_tensor(full[0][:, 0:nq], tmp[0][:, 0:nq], g_cb[:, n, 0:nq], ALU.mult).then_inc(*T("mix_v", ("conv", n)))
                    dve.wait_ge(*W("mix_a", ("conv", n)))
                    ins = dve.tensor_tensor(h_lo[:, 6 + n, 0:nq], full[0][:, 0:nq], h_hi[:, 6 + n, 0:nq].bitcast(F32), ALU.subtract)
                    if n == 0:
                        step(ins)
                ins.then_inc(*T("mix_v", "conv"))
                dve.wait_ge(*W("mix_v", "conv"))
                dve.wait_ge(*W("bias_in", l, at="load"))
                us = units(l)
                for u in range(len(us) + 2):
                    if u < len(us):
                        s, hd, qb = us[u]
                        k0, k1 = keys_of(s)
                        sc = psum[u % 2][:, 0:k1 - k0]
                        dve.wait_ge(*W("product", ("scores", u)))
                        if s == 0 and hd >= 6:
                            step(dve.tensor_tensor(sc[:, 0:T1], sc[:, 0:T1], g_bias[:, qb, hd - 6, :], ALU.add))
                        dve.tensor_reduce(g_st[u % 2][:, 0:1], sc, AX.X, ALU.max, negate=True).then_inc(*T("mix_v", ("max", u)))
                    if 1 <= u <= len(us):
                        v = u - 1
                        k0, k1 = keys_of(us[v][0])
                        dve.wait_ge(*W("mix_a", ("exp", v)))
                        step(dve.reciprocal(g_st[v % 2][:, 2:3], g_st[v % 2][:, 1:2]))
                        dve.tensor_scalar(g_p[v % 2][:, 0:k1 - k0], g_p[v % 2][:, 0:k1 - k0], g_st[v % 2][:, 2:3], None, ALU.mult)\
                            .then_inc(*T("mix_v", ("probs", v)))
                    if u >= 2 and (u - 2) % 2:
                        v = u - 2
                        s, hd, _ = us[v]
                        x = v // 2
                        half = slice(64 * (hd % 2), 64 * (hd % 2) + 64)
                        cut = slice(T1 * s, T1 * s + T1)
                        dve.wait_ge(*W("mix_a", ("upper", x)))
                        dve.tensor_tensor(h_lo[half, hd // 2, cut], psum[6 + x % 2][half, 0:T1], h_hi[half, hd // 2, cut].bitcast(F32),
                                          ALU.subtract).then_inc(*T("h_ready", x))

            def turn_out():
                stage[0] = "store"
                for t in range(2):
                    for q in range(2):
                        dve.wait_ge(*W("product", (t, q)))
                        ins = dve.tensor_copy(xo[:, t, 512 * q:512 * q + 512], psum[2 * t + q][:, :])
                    ins.then_inc(*T("out_tile", t))

            for s in range(SLOTS):
                dve.sem_inc(sem(f"raw_done{s}"), 1)
            for name, start in START.items():
                dve.sem_inc(sem(name), start)
            dve.memset(epsc, EPS)
            dve.memset(onec, 1.0)
            dve.memset(ones, 1.0).then_inc(*T_at("ones_set", 0))
            for l in range(DEPTH):
                ada(f"ada1.{l}", 4, mod1[:, l, :], 1)
            for l in range(DEPTH):
                ada(f"ada2.{l}", 6, mod2[:, l].rearrange("p m k s -> p (m k s)"), 2)
            turn_in()
            dve.wait_ge(*W("small_in", "all", at="load"))
            mods()
            split_lo(0, SLOT)
            norm("norm0.0", T1)
            linear("mlstm", mlstm_evac, True)
            mlstm()
            linear("mlstm_out", residual("mlstm_out", 0, 0), True)
            norm("norm0.1", T1)
            moe(0)
            norm("norm1.0", T1)
            linear("diff", diff_evac, True)
            diff()
            linear("diff_out", residual("diff_out", 1, 0), True)
            norm("norm1.1", T1)
            moe(1)
            for l in range(DEPTH):
                both = l < DEPTH - 1
                n = T2 if both else T1
                norm(f"normffn{l}a", T2)
                ffn(l, 0, True)
                post(f"post{l}.0", T2, l, 0)
                norm(f"normin{l}", T2)
                linear(f"in{l}", in_evac(f"in{l}", l), True)
                attention(l)
                linear(f"attn_out{l}", y_evac(f"attn_out{l}", n), True)
                post(f"post{l}.1", n, l, 1)
                norm(f"normffn{l}b", n)
                ffn(l, 1, both)
                post(f"postffn{l}b", n, l, 2)
            turn_out()
    return log


def pack_columns(x):
    col = lambda v: np.asarray(v, np.float32).reshape(-1, P).T
    twice = lambda v: np.concatenate([np.asarray(v).reshape(-1, HD)] * 2, axis=1).T
    rows = lambda v: np.repeat(np.asarray(v).reshape(1, -1), P, axis=0)
    both = np.stack([np.asarray(x["c_2"]).reshape(KT, P), np.asarray(x["c_ctx_2"]).reshape(KT, P)], axis=1)
    parts = {"c1": col(x["c"]), "c2": both.reshape(2 * KT, P).T, "norm1": col(x["norm1"]), "norm2": col(x["norm2"]),
             "b_ada": col(x["b_ada"]), "a_h_norm": col(x["a_h_norm"]), "b_q_norm": twice(x["b_q_norm"]),
             "b_k_norm": twice(x["b_k_norm"]), "b_o_norm": col(x["b_o_norm"]), "b_ada_2": col(x["b_ada_2"]),
             "norm_g_2": col(x["norm_g_2"]), "qk_g_2": twice(x["qk_g_2"]), "conv_w_2": col(x["conv_w_2"]),
             "b_if": rows(x["a_b_if"]), "router_bias": rows(x["router_bias"])}
    return np.concatenate([parts[k] for k in COLS], axis=1)


def rpb_rows(rpb):
    out = np.full((DEPTH, 4, 64, 6, 4, 64), INVALID, np.float32)
    for r in range(4):
        for c in range(64):
            first = min(max(c - 8, 0), 48)
            for kr in range(4):
                out[:, r, c, :, kr, first:first + 16] = rpb[:, :, kr - r + 7, first - c + 15:first - c + 31]
    return out.reshape(DEPTH, 4, 64, 6, T1)


DIRECT = ["x", "ctx_2", "positions", "w_ada", "w_ada_2", "a_w_in", "a_w_out", "b_w_in", "b_w_out", "w_router",
          "b_lam_q1", "b_lam_k1", "b_lam_q2", "b_lam_k2", "moe_w_gu", "moe_w_down", "w_in_2", "w_o_2",
          "ffn_wi_2", "ffn_wo_2"]


def kernel(**inputs):
    import concourse.bacc as bacc
    from concourse.bass_utils import run_bass_kernel_spmd

    x = {k: np.asarray(v) for k, v in inputs.items()}
    arrays = {k: np.ascontiguousarray(x[k]) for k in DIRECT}
    arrays["consts"], arrays["consts2"] = host_consts()
    arrays["columns"] = np.ascontiguousarray(pack_columns(x))
    arrays["rpb_rows"] = rpb_rows(x["rpb_2"])

    def program(notes):
        nc = bacc.Bacc("TRN2", target_bir_lowering=False, num_devices=1)
        args = {k: nc.dram_tensor(f"in_{k}", a.shape, mybir.dt.from_np(a.dtype), kind="ExternalInput").ap()
                for k, a in arrays.items()}
        out = nc.dram_tensor("out_0", (1, T1, D), F32, kind="ExternalOutput").ap()
        return nc, build(nc, args, out, notes)

    _, notes = program(None)
    nc, _ = program(notes)
    r = run_bass_kernel_spmd(nc, [{f"in_{k}": a for k, a in arrays.items()}], core_ids=[0])
    return r.results[0]["out_0"]
```

```python
import math
from contextlib import ExitStack

import numpy as np

import concourse.bass as bass
from concourse import mybir

F32 = mybir.dt.float32
F32R = mybir.dt.float32r
I32 = mybir.dt.int32
U32 = mybir.dt.uint32
ALU = mybir.AluOpType
ACT = mybir.ActivationFunctionType
AX = mybir.AxisListType
ds = bass.ds

P = 128
D = 1024
KT = D // P
T1 = 256
T2 = 512
DEPTH = 2
EPS = 1e-6
A_HEADS, A_QK, A_V = 4, 128, 256
B_HEADS, B_HD = 8, 64
N_EXP, N_GRP, E_GRP = 16, 4, 4
D_EXP = 512
FFN = 2816
FFN_TILES = FFN // P
HALF = FFN_TILES // 2
NMOD2 = 9
HD = 64
LAT_HEADS = 12
SLOTS = 6
SLOT = 2048
LAM_INIT = 0.8 - 0.6 * math.exp(-0.3 * 1)
INVALID = -1e30

COLS = {}
_at = 0
for _name, _n in (("c1", 8), ("c2", 16), ("norm1", 16), ("norm2", 16), ("b_ada", 96), ("a_h_norm", 8),
                  ("b_q_norm", 1), ("b_k_norm", 1), ("b_o_norm", 1), ("b_ada_2", 144),
                  ("norm_g_2", 96), ("qk_g_2", 4), ("conv_w_2", 12), ("b_if", 8), ("router_bias", 16)):
    COLS[_name] = (_at, _n)
    _at += _n
NCOLS = _at

CONST = {}
_at = 0
for _name, _n in (("ident", 128), ("block_ones", 128), ("row_of", 3), ("upper", 128), ("rope1", 128), ("causal", 128),
                  ("iota16", 16), ("iota8", 8), ("invfreq", 1)):
    CONST[_name] = (_at, _n)
    _at += _n
NCONST = _at
KEPT = CONST["upper"][0]
CONST2 = {"rope2": (0, 128), "dup0": (128, 128), "dup1": (256, 128), "cos2": (384, 256), "sin2": (640, 256)}
NCONST2 = 896


START = {"ada_col": 1, "ada_done": 3, "gated": 4, "y_ready": KT}


class Log:

    def __init__(self, notes=None):
        self.notes = notes
        self.count, self.marks, self.loops = dict(START), {}, {}
        self.loop = None

    def enter(self, name, i, turns):
        self.loop, self.before = (name, i), dict(self.count)
        self.loops.setdefault(name, {"turns": turns, "per": {}})

    def leave(self):
        rec = self.loops[self.loop[0]]
        for k, v in self.count.items():
            if per := v - self.before.get(k, 0):
                rec["per"][k] = per
                self.count[k] = self.before.get(k, 0) + per * rec["turns"]
        self.loop = None

    def raised(self, sem, key, by):
        self.count[sem] = self.count.get(sem, 0) + by
        if key is not None:
            self.marks[(sem, key)] = (self.loop and self.loop[0], self.count[sem])

    def value(self, sem, key, loop, back):
        if self.notes is None:
            return 1
        at, v = self.notes.marks[(sem, key)]
        if at is None:
            return v
        rec = self.notes.loops[at]
        per = rec["per"][sem]
        if loop and loop[0] == at:
            return loop[1] * per + (v - back * per)
        return v + (rec["turns"] - 1) * per


def host_consts():
    c = np.zeros((P, NCONST), np.float32)
    p = np.arange(P)
    put = lambda n, a: c.__setitem__((slice(None), slice(CONST[n][0], CONST[n][0] + CONST[n][1])), a)
    put("ident", np.eye(P))
    put("block_ones", (p[:, None] // 64 == p[None, :] // 64))
    put("row_of", (p[:, None] % 32 == np.arange(3)[None, :]))
    put("upper", (p[:, None] <= p[None, :]))
    put("causal", np.where(p[:, None] >= p[None, :], 0.0, INVALID))
    r = np.zeros((P, P))
    freq = np.zeros((P, 1))
    inv = (500000.0 ** (-np.arange(0, 16, 2, dtype=np.float32) / np.float32(16))).astype(np.float32)
    for h in range(2):
        for d in range(8):
            r[64 * h + d + 8, 64 * h + d] = -1
            r[64 * h + d, 64 * h + d + 8] = 1
            freq[64 * h + d] = freq[64 * h + d + 8] = inv[d]
    put("rope1", r)
    put("invfreq", freq)
    put("iota16", np.arange(16)[None, :])
    put("iota8", np.arange(8)[None, :])
    c2 = np.zeros((P, NCONST2), np.float32)
    r = np.zeros((P, P))
    cos, sin = np.zeros((P, T1), np.float32), np.zeros((P, T1), np.float32)
    f = (1.0 / (np.float32(10000.0) ** (np.arange(16, dtype=np.float32) / np.float32(16)))).astype(np.float32)
    pos = np.arange(T1)
    for q in range(P):
        axis, part, i = (q % 64) // 32, (q % 32) // 16, q % 16
        ang = ((pos // 64) if axis == 0 else (pos % 64)).astype(np.float32) * f[i]
        cos[q], sin[q] = np.cos(ang), np.sin(ang)
        if part == 0:
            r[q + 16, q] = -1
        else:
            r[q - 16, q] = 1
    c2[:, 0:128] = r
    c2[:, 128:256] = (p[:, None] == p[None, :] % 64)
    c2[:, 256:384] = (p[:, None] == 64 + p[None, :] % 64)
    c2[:, 384:640], c2[:, 640:896] = cos, sin
    return c, c2


def build(nc, A, out, notes=None):
    log = Log(notes)
    with ExitStack() as ctx:
        sems = {}

        def sem(name):
            if name not in sems:
                sems[name] = ctx.enter_context(nc.semaphore(name))
            return sems[name]

        stage = [""]

        def T(name, key=None, by=1):
            log.raised(name, (stage[0], key) if key is not None else None, by)
            return sem(name), by

        def W(name, key, at=None, back=0):
            return sem(name), log.value(name, (at or stage[0], key), log.loop, back)

        def T_at(name, key):
            log.raised(name, ("load", key), 1)
            return sem(name), 1

        top = [16544]

        def region(nbytes):
            at = top[0]
            top[0] += nbytes
            return at

        def sb(name, shape, dt, at):
            return nc.alloc_sbuf_tensor_at(name, shape, dt, offset=at)[:]

        def take(at):
            pos = [at]

            def f(name, shape, dt=F32):
                t = sb(name, shape, dt, pos[0])
                pos[0] += -(-4 * int(np.prod(shape[1:])) // 32) * 32
                return t
            f.pos = pos
            return f

        raw_at = region(SLOTS * SLOT * 4)
        raw = [sb(f"raw{s}", [P, SLOT], F32, raw_at + s * SLOT * 4) for s in range(SLOTS)]
        split_at = region(4 * SLOT * 4)
        w_hi = [sb(f"w_hi{b}", [P, SLOT], F32R, split_at + 2 * b * SLOT * 4) for b in range(2)]
        w_lo = [sb(f"w_lo{b}", [P, SLOT], F32R, split_at + (2 * b + 1) * SLOT * 4) for b in range(2)]
        X = sb("x_resid", [P, KT, T2], F32, region(KT * T2 * 4))
        h_at = region(2 * KT * T2 * 4)
        h_hi = sb("h_hi", [P, KT, T2], F32R, h_at)
        h_lo = sb("h_lo", [P, KT, T2], F32R, h_at + KT * T2 * 4)
        squares = sb("squares", [P, KT, T2], F32, h_at + KT * T2 * 4)
        a_at = region(2 * HALF * T2 * 4)
        y_at = region(KT * T2 * 4)
        Y = sb("y_out", [P, KT, T2], F32, y_at)
        act_hi = sb("act_hi", [P, HALF, T2], F32R, a_at)
        act_lo = sb("act_lo", [P, HALF, T2], F32R, a_at + HALF * T2 * 4)

        cst = take(region(0))
        consts_a = cst("consts_a", [P, KEPT])
        b_at = cst.pos[0]
        consts_b = cst("consts_b", [P, NCONST - KEPT])
        w_router = cst("w_router_sb", [P, KT, N_EXP])
        cst.pos[0] = max(cst.pos[0], b_at + 4 * NCONST2)
        consts2 = sb("consts2", [P, NCONST2], F32, b_at)
        C = {k: (consts_a[:, a:a + n] if a < KEPT else consts_b[:, a - KEPT:a - KEPT + n]) for k, (a, n) in CONST.items()}
        C2 = {k: consts2[:, a:a + n] for k, (a, n) in CONST2.items()}
        cols_ = cst("cols", [P, NCOLS])
        V = {k: cols_[:, a:a + n] for k, (a, n) in COLS.items()}
        ones = cst("ones", [P, P])
        ident = C["ident"]
        epsc = cst("epsc", [P, 1])
        onec = cst("onec", [P, 1])
        zeroc = cst("zeroc", [P, 1])
        rms4, inv4, warm = cst("rms4", [P, 4]), cst("inv4", [P, 4]), cst("warm", [P, 4])
        mod_first = cst("mod_first", [P, 48])
        mod_all = cst("mod_all", [P, 48 + DEPTH * NMOD2 * KT, 3])
        mod1 = [mod_first, mod_all[:, 0:48, 0]]
        mod2 = mod_all[:, 48:, 1:3].rearrange("p (l m k) s -> p l m k s", l=DEPTH, m=NMOD2)
        pre1 = cst("pre1", [P, DEPTH, 2, KT])
        pre2 = cst("pre2", [P, DEPTH, 3, KT, 2])
        post2 = cst("post2", [P, DEPTH, 3, KT, 2])
        cact = cst("cact", [P, KT, 32])
        small = cst("small", [P, 16])
        tmp_at = cst.pos[0]
        tmp = [cst(f"tmp{i}", [P, T2]) for i in range(2)]
        full = [cst(f"full{i}", [P, T2]) for i in range(2)]
        assert cst.pos[0] <= 229344, cst.pos[0]
        psum = [ctx.enter_context(nc.psum_tensor(f"bank{b}", [P, 512], F32)) for b in range(8)]

        at0 = take(a_at)
        xt = at0("x_tokens", [P, 4, D])
        ada_row0 = sb("ada_row0", [P, 2, 256], F32, h_at)
        m = take(a_at)
        m_q, m_k = m("m_q", [P, A_HEADS, T1]), m("m_k", [P, A_HEADS, T1])
        m_v, m_og = m("m_v", [P, 2, A_HEADS * A_V]), m("m_og", [P, KT, T1])
        w_gate = m("w_gate", [P, KT, 2 * A_HEADS])
        m_g, m_lf, m_u, m_b, m_a = (m(n, [P, 2, 2 * A_HEADS if n == "m_g" else A_HEADS])
                                    for n in ("m_g", "m_lf", "m_u", "m_b", "m_a"))
        m_rows, m_arow = m("m_rows", [A_HEADS, 512]), m("m_arow", [A_HEADS, T1])
        m_d, m_p, m_hh, m_em, m_dn = (m("m_d", [P, 384]), m("m_p", [P, 384]), m("m_hh", [P, 2, T1]),
                                      m("m_em", [P, T1]), m("m_dn", [P, T1]))
        m_full = m("m_full", [P, 2, T1])
        m_rstd = m("m_rstd", [P, T1])
        ada_row1 = m("ada_row1", [P, 2, 256])
        m_d2 = full[0]
        assert m.pos[0] <= y_at + KT * T2 * 4
        d = take(a_at)
        d_q, d_k = d("d_q", [P, B_HEADS, T1]), d("d_k", [P, B_HEADS, T1])
        d_v = d("d_v", [P, 2, D])
        d_cos, d_sin = d("d_cos", [P, T1]), d("d_sin", [P, T1])
        d_ang, d_n = d("d_ang", [P, T1]), d("d_n", [P, T1])
        d_pos = d("d_pos", [P, T1], I32)
        d_lam = d("d_lam", [P, 4, B_HD])
        d_ls = d("d_ls", [P, 8])
        d_raw = [d(f"d_raw{i}", [P, T1]) for i in range(2)]
        d_sq = [d(f"d_sq{i}", [P, T1]) for i in range(2)]
        d_rs = [d(f"d_rs{i}", [P, T1]) for i in range(2)]
        d_p = [d(f"d_p{i}", [P, 2, T1]) for i in range(2)]
        d_st = [d(f"d_st{i}", [P, 8]) for i in range(2)]
        d_at = [d(f"d_at{i}", [P, 2, T1]) for i in range(2)]
        assert d.pos[0] <= y_at + KT * T2 * 4
        e = take(a_at)
        e_hi, e_lo = e("e_hi", [P, 4, T1], F32R), e("e_lo", [P, 4, T1], F32R)
        e_gate = e("e_gate", [P, N_EXP, T1])
        e_s, e_b, e_m, e_w = (e(n, [P, 2, N_EXP]) for n in ("e_s", "e_b", "e_m", "e_w"))
        e_pair, e_g8, e_x8 = e("e_pair", [P, N_GRP, 6]), e("e_g8", [P, 8]), e("e_x8", [P, 8])
        e_i8 = e("e_i8", [P, 8], U32)
        e_f8, e_oh = e("e_f8", [P, 8]), e("e_oh", [P, 8])
        e_row = e("e_row", [N_EXP, T1])
        e_zero = e("e_zero", [P, T2], F32R)
        ada_raw = [e(f"ada_raw{x}", [P, KT, 256]) for x in range(3)]
        ada_row2 = e("ada_row2", [P, 256])
        assert e.pos[0] <= y_at + KT * T2 * 4
        g = take(a_at)
        g_q, g_kb = g("g_q", [P, 6, T2]), g("g_kb", [P, 3, T2])
        g_ka, g_kd = g("g_ka", [P, T2]), g("g_kd", [P, 2, T2])
        g_v = g("g_v", [P, 4, 512])
        g_cx, g_cb, g_cc = (g(n, [P, 2, T2]) for n in ("g_cx", "g_cb", "g_cc"))
        assert g.pos[0] <= y_at
        g = take(y_at)
        g_bias = g("g_bias", [P, 2, 6, T1])
        g_p = [g(f"g_p{i}", [P, T2]) for i in range(2)]
        assert g.pos[0] <= y_at + KT * T2 * 4
        quad = tmp + full
        g_rstd = sb("g_rstd", [P, T2], F32, h_at)
        g_pt = [sb(f"g_pt{i}", [P, 4, T1], F32, tmp_at + i * 4096) for i in range(2)]
        xo = sb("x_out", [P, 2, D], F32, a_at)
        g_st = [small[:, 4 * i:4 * i + 4] for i in range(2)]

        block = ctx.enter_context(nc.Block())

        class Stream:

            def __init__(self):
                self.slot, self.all, self.loop = [0] * SLOTS, 0, None

            def enter(self, i, chunks):
                self.loop = (i, chunks, [len(range(s, chunks, SLOTS)) for s in range(SLOTS)])

            def leave(self, turns):
                _, chunks, per = self.loop
                self.loop = None
                self.all += (turns - 1) * chunks
                self.slot = [n + (turns - 1) * k for n, k in zip(self.slot, per)]

            def next(self, s, split=1):
                self.slot[s] += 1
                self.all += split
                if self.loop is None:
                    return self.slot[s], self.all
                i, chunks, per = self.loop
                return i * per[s] + self.slot[s], i * chunks + self.all

        def w3(ap, k):
            return ap.rearrange("p (k n) -> p k n", k=k)

        def tt(*which, n):
            return [("T", P * x, n) for x in which]

        ITEMS = {"mlstm": [tt(0, 1, n=T1)] * 4 + [[("V", 0, 256, (0, 1))]] * 4 + [tt(0, 1, n=T1)] * 4,
                 "mlstm_out": [tt(0, 1, n=T1)] * 4,
                 "diff": [tt(0, 1, n=T1)] * 8 + [[("V", 0, 256, (0, 1))]] * 4,
                 "diff_out": [tt(0, 1, n=T1)] * 4}
        for l in range(DEPTH):
            n = T1 if l == DEPTH - 1 else T2
            ITEMS[f"in{l}"] = [tt(0, 1, n=n)] * 3 + [tt(0, n=T2) + [("V", 128, 128, (0, 1, 2, 3))], tt(0, 1, n=T2),
                               tt(0, n=T2) + [("V", 128, 128, (0, 1, 2, 3))],
                               [("V", 0, 256, (0, 1)), ("V", 0, 256, (2, 3))]] + [tt(0, 1, n=n)] * 3
            ITEMS[f"attn_out{l}"] = [tt(0, 1, n=n)] * 4

        def in_evac_by(c, n):
            return "evac_v" if (c, n) in ((3, 1), (5, 1)) or c == 6 else "evac_a"

        EVAC = {"mlstm": lambda c, n: "evac_v" if 4 <= c < 8 else "evac_a",
                "diff": lambda c, n: "evac_v" if c >= 8 else "evac_a",
                "mlstm_out": lambda c, n: "evac_v", "diff_out": lambda c, n: "evac_v",
                "in0": in_evac_by, "in1": in_evac_by,
                "attn_out0": lambda c, n: "evac_v", "attn_out1": lambda c, n: "evac_v"}
        UP_BANK = (0, 1, 2, 0)

        def bank_of(name, c, n):
            return (sum(len(x) for x in ITEMS[name][:c]) + n) % 4

        def x_key(at, j):
            return ("evac_v", (j // 2, j % 2), at) if at.endswith("_out") else ("x_ready", j, at)

        def y_key(post, j):
            if post.endswith(".1"):
                return "evac_v", (j // 2, j % 2), f"attn_out{post[4]}"
            name = f"ffn{post[4]}a" if post.startswith("post") and post.endswith(".0") else post[4:]
            return "y_ready", ("g1" if name == LAST else "g", j), name

        ADA_START, ADA_MIX = 8, 16
        EXP_CH, FFN_CH, FFN_UP = 6, HALF + KT, HALF
        DOWN = HALF * P
        LAST = f"ffn{DEPTH - 1}b"

        part1 = lambda l, w: [(0, T1, lambda j: pre1[:, l, w, j:j + 1], lambda j: mod1[l][:, 24 * w + j:24 * w + j + 1])]
        part2 = lambda l, i, both: [(T1 * s, T1 * s + T1, lambda j, s=s: pre2[:, l, i, j, s:s + 1],
                                     lambda j, s=s: mod2[:, l, 3 * i, j, s:s + 1]) for s in range(1 + both)]

        def last_item(name, c):
            return c, len(ITEMS[name][c]) - 1

        def units(l):
            return [(s, hd, qb) for s in range(1 if l == DEPTH - 1 else 2) for hd in range(LAT_HEADS)
                    for qb in range(2)]

        last_head = {"mix0": A_HEADS - 1, "mix1": B_HEADS - 1} | {f"mix2.{l}": len(units(l)) // 2 - 1 for l in range(DEPTH)}

        def keys_of(s):
            return (0, T2) if s == 0 else (T1, T2)

        def halves(l):
            return [(0, 0, T1), (1, T1, T2)][:1 if l == 2 else 2]

        @block.sync
        def _(sp):
            st = Stream()

            def load(c, src, k):
                s = c % SLOTS
                used, _ = st.next(s)
                dst = w3(raw[s], k) if k * (SLOT // k) == SLOT else w3(raw[s][:, 0:DOWN], k)
                sp.wait_ge(sem(f"raw_done{s}"), used)
                sp.dma_start(dst, src).then_inc(sem(f"raw_full{s}"), 16)

            def linear(name, W2d):
                v = W2d.rearrange("(k p) n -> p k n", p=P)
                for c in range(len(ITEMS[name])):
                    load(c, v[:, :, 256 * c:256 * c + 256], KT)

            def ada(first, chunks):
                v = A["w_ada_first"].rearrange("(k p) n -> p k n", p=P)
                for c in range(chunks):
                    load(c, v[:, :, 256 * (first + c):256 * (first + c) + 256], KT)

            def moe(l):
                gu = A["moe_w_gu"][l].rearrange("e (k p) (g c n) -> e p g k c n", p=P, g=2, c=4)
                dn = A["moe_w_down"][l].rearrange("e (k p) n -> e p k n", p=P)
                ada_w = A["w_mods"].rearrange("(k p) n -> p k n", p=P)
                stage[0] = f"moe{l}"
                with sp.Fori(0, N_EXP) as i:
                    st.enter(i, EXP_CH)
                    log.enter(f"moe{l}", i, N_EXP)
                    for c in range(4):
                        s = c
                        used, _ = st.next(s)
                        dst = raw[s].rearrange("p (g k n) -> p g k n", g=2, k=KT)
                        sp.wait_ge(sem(f"raw_done{s}"), used)
                        sp.dma_start(dst, gu[i, :, :, :, c, :]).then_inc(sem(f"raw_full{s}"), 16)
                        if c < 3:
                            if c == 0:
                                sp.wait_ge(*W("h_ready", last_head[f"mix{l}"], at=f"mix{l}"))
                            sp.wait_ge(*W("ada_done", c, back=1))
                            sp.dma_start(ada_raw[c], ada_w[:, :, ds(i * 768 + (N_EXP * 768 * l + c * 256), 256)])\
                                .then_inc(*T(f"ada_full{c}", 0, 16))
                    for c in range(4, 6):
                        load(c, dn[i, :, :, 512 * (c - 4):512 * (c - 3)], 4)
                    log.leave()
                st.leave(N_EXP)

            def ffn(l, which):
                wi = A["ffn_wi_2"][l, which].rearrange("(k p) (g c n) -> p g k c n", p=P, g=2, c=FFN_TILES)
                wo = A["ffn_wo_2"][l, which].rearrange("(t f p) n -> p t f n", t=2, p=P)

                def group(t):
                    for c in range(FFN_UP):
                        s = c % SLOTS
                        used, _ = st.next(s)
                        dst = raw[s].rearrange("p (g k n) -> p g k n", g=2, k=KT)
                        sp.wait_ge(sem(f"raw_done{s}"), used)
                        sp.dma_start(dst, wi[:, :, :, t * HALF + c, :]).then_inc(sem(f"raw_full{s}"), 16)
                    for c in range(KT):
                        load(FFN_UP + c, wo[:, t, :, P * c:P * c + P], HALF)

                if (l, which) == (DEPTH - 1, 1):
                    group(0)
                    group(1)
                else:
                    with sp.Fori(0, 2) as t:
                        st.enter(t, FFN_CH)
                        group(t)
                    st.leave(2)

            stage[0] = "load"
            sp.dma_start(consts_a, A["consts"][:, 0:KEPT]).then_inc(*T("small_in", "ident", 16))
            sp.dma_start(consts_b, A["consts"][:, KEPT:NCONST]).then_inc(*T("small_in", "consts", 16))
            sp.dma_start(cols_, A["columns"]).then_inc(*T("small_in", "cols", 16))
            sp.dma_start(w_router, A["w_router"].rearrange("(k p) n -> p k n", p=P)).then_inc(*T("small_in", "all", 16))
            ada(0, ADA_START)
            linear("mlstm", A["a_w_in"][0])
            ada(ADA_START, ADA_MIX)
            linear("mlstm_out", A["a_w_out"][0])
            moe(0)
            linear("diff", A["b_w_in"][0])
            linear("diff_out", A["b_w_out"][0])
            moe(1)
            for l in range(DEPTH):
                ffn(l, 0)
                linear(f"in{l}", A["w_in_2"][l])
                linear(f"attn_out{l}", A["w_o_2"][l])
                ffn(l, 1)

        @block.gpsimd
        def _(pool):
            stage[0] = "load"
            pool.dma_start(xt[:, 0:2, :], A["x"][0].rearrange("(t p) d -> p t d", p=P)).then_inc(*T("tokens_in", "x", 16))
            pool.dma_start(xt[:, 2:4, :], A["ctx_2"][0].rearrange("(t p) d -> p t d", p=P)).then_inc(*T("tokens_in", "all", 16))
            pool.wait_ge(*W("x_ready", KT - 1, at="turn_in"))
            pool.dma_start(w_gate, A["a_w_in"][0].rearrange("(k p) n -> p k n", p=P)[:, :, 3072:3080])\
                .then_inc(*T("gate_in", 0, 16))
            pool.wait_ge(*W("x_ready", KT - 1, at="moe0"))
            pool.dma_start(d_pos, A["positions"].broadcast_to([P, T1])).then_inc(*T("diff_in", "pos", 16))
            for n, name in enumerate(("b_lam_q1", "b_lam_k1", "b_lam_q2", "b_lam_k2")):
                pool.dma_start(d_lam[:, n, :], A[name].broadcast_to([P, B_HD])).then_inc(*T("diff_in", "all", 16))
            pool.wait_ge(*W("x_ready", KT - 1, at="moe1"))
            pool.dma_start(consts2, A["consts2"]).then_inc(*T("consts2_in", 0, 16))
            for l in range(DEPTH):
                pool.wait_ge(*W("x_ready", KT - 1, at=f"post{l}.0"))
                for r in range(4):
                    pool.dma_start(g_bias[64 * (r % 2):64 * (r % 2) + 64, r // 2, :, :],
                                   A["rpb_rows"][l, r]).then_inc(*T("bias_in", l, 16))
            stage[0] = "store"
            for t in range(2):
                pool.wait_ge(*W("out_tile", t))
                pool.dma_start(out[0, P * t:P * t + P, :], xo[:, t, :]).then_inc(*T("stored", t, 16))
            pool.wait_ge(*W("stored", 1))

        @block.tensor
        def _(pe):
            st = Stream()
            bank_user = {}

            def bank_ready(b):
                if b in bank_user:
                    pe.wait_ge(*W(*bank_user[b][0], **bank_user[b][1]))

            def ada_rows(w, bank):
                for k in range(KT):
                    g = slice(32 * (k % 4), 32 * (k % 4) + 32)
                    mm = pe.matmul(bank[g, 0:256], cact[:, k, :], w[:, k, :], start=(k < 4), stop=(k >= 4))
                return mm

            def ada_turn(dst, row, n):
                for q in range(2):
                    mm = pe.matmul(dst[:, n * q:n * q + n], row[:, P * q:P * q + P], C["row_of"][:, 0:n], start=True, stop=True)
                return mm

            def ada(c, chunks, banks, cols, row):
                if c < chunks:
                    used, _ = st.next(c % SLOTS, 0)
                    pe.wait_ge(sem(f"raw_full{c % SLOTS}"), used * 16)
                    ada_rows(w3(raw[c % SLOTS], KT), banks[c % 2]).then_inc(sem(f"raw_done{c % SLOTS}"), 1)
                if c:
                    pe.wait_ge(*W("ada_row", c - 1))
                    ada_turn(cols[:, 2 * c - 2:2 * c], row[:, (c - 1) % 2, :], 1).then_inc(*T("product", ("turned", c - 1)))

            def turn_in():
                stage[0] = "turn_in"
                pe.wait_ge(*W("tokens_in", "all", at="load"))
                for j in range(KT):
                    for t in range(4):
                        mm = pe.transpose(psum[j][:, P * t:P * t + P], xt[:, t, P * j:P * j + P], ident)
                    mm.then_inc(*T("product", j))

            def sum_squares(name, n):
                stage[0] = name
                nt = n // P
                for j in range(KT):
                    pe.wait_ge(*W("squared", j))
                    if j == 0:
                        pe.matmul(psum[3][:, 0:nt], zeroc[0:1, 0:1].broadcast_to([1, P]), ones[0:1, 0:nt],
                                  start=True, stop=False, skip_group_check=True)
                    for t in range(nt):
                        mm = pe.matmul(psum[3][:, t:t + 1], squares[:, j, P * t:P * t + P], ones[:, 0:1],
                                       start=False, stop=False, skip_group_check=True)
                mm.then_inc(*T("product", "squares"))
                pe.wait_ge(*W("inverse", 0))
                for t in range(nt):
                    mm = pe.matmul(psum[7][:, P * t:P * t + P], inv4[:, t:t + 1].broadcast_to([P, P]), ident,
                                   start=True, stop=True)
                mm.then_inc(*T("product", "rstd"))

            def linear(name, source, per_tile=True):
                stage[0] = name
                for c, items in enumerate(ITEMS[name]):
                    used, _ = st.next(c % SLOTS)
                    pe.wait_ge(sem(f"raw_done{c % SLOTS}"), used + 1)
                    hi, lo = w3(w_hi[c % 2], KT), w3(w_lo[c % 2], KT)

                    def steps(n, it):
                        b = psum[bank_of(name, c, n)]
                        for where, t in ([(slice(0, it[2]), None)] if it[0] == "T" else
                                         [(slice(it[2] * x, it[2] * x + it[2]), t) for x, t in enumerate(it[3])]):
                            for k in range(KT):
                                if t is None:
                                    cut = slice(it[1], it[1] + P)
                                    trio = [(hi[:, k, cut], h_hi[:, k, 0:it[2]]), (hi[:, k, cut], h_lo[:, k, 0:it[2]]),
                                            (lo[:, k, cut], h_hi[:, k, 0:it[2]])]
                                else:
                                    cut, tok = slice(it[1], it[1] + it[2]), slice(P * t, P * t + P)
                                    trio = [(h_hi[:, k, tok], hi[:, k, cut]), (h_hi[:, k, tok], lo[:, k, cut]),
                                            (h_lo[:, k, tok], hi[:, k, cut])]
                                for x, (l_, r_) in enumerate(trio):
                                    mm = pe.matmul(b[:, where], l_, r_, start=(k == 0 and x == 0),
                                                   stop=(k == KT - 1 and x == 2))
                                yield mm

                    if c == 0:
                        for n in range(len(items)):
                            bank_ready(bank_of(name, c, n))
                        rows = [steps(n, it) for n, it in enumerate(items)]
                        for k in range(KT):
                            pe.wait_ge(*W("h_ready", k if per_tile else last_head[source], at=source))
                            last = [next(r) for r in rows]
                        for n, mm in enumerate(last):
                            mm.then_inc(*T("product", (c, n)))
                    else:
                        for n, it in enumerate(items):
                            bank_ready(bank_of(name, c, n))
                            for mm in steps(n, it):
                                pass
                            mm.then_inc(*T("product", (c, n)))
                    for n in range(len(items)):
                        bank_user[bank_of(name, c, n)] = ((EVAC[name](c, n), (c, n)), {"at": name})

            def moe(l):
                name = stage[0] = f"moe{l}"
                for t in range(2):
                    for k in range(KT):
                        if t == 0:
                            pe.wait_ge(*W("h_ready", k, at=f"norm{l}.1"))
                        for x, h in enumerate((h_hi, h_lo)):
                            mm = pe.matmul(psum[0][:, 16 * t:16 * t + 16], h[:, k, P * t:P * t + P].bitcast(F32),
                                           w_router[:, k, :], start=(k == 0 and x == 0), stop=(k == KT - 1 and x == 1))
                mm.then_inc(*T("product", "router"))
                pe.wait_ge(*W("gate_w", "tokens"))
                for t in range(2):
                    mm = pe.transpose(psum[0][0:N_EXP, 128 + P * t:256 + P * t], e_w[:, t, :], ident)
                mm.then_inc(*T("product", "gate_rows"))
                pe.wait_ge(*W("gate_w", "rows"))
                for x in range(N_EXP):
                    if x >= 4:
                        pe.wait_ge(*W("gate_bc", x - 4))
                    mm = pe.matmul(psum[x % 4][:, 0:T1], ident[0:N_EXP, x:x + 1].broadcast_to([N_EXP, P]), e_row,
                                   start=True, stop=True)
                    mm.then_inc(*T("product", ("bc", x)))
                pe.wait_ge(*W("gate_bc", N_EXP - 1))
                for b in range(4, 8):
                    pe.matmul(psum[b][:, :], e_zero[:, 0:P], e_zero, start=True, stop=False, skip_group_check=True)
                with pe.Fori(0, N_EXP) as i:
                    st.enter(i, EXP_CH)
                    log.enter(name, i, N_EXP)
                    for c in range(4):
                        used, _ = st.next(c)
                        hi, lo = w3(w_hi[c % 2], 2 * KT), w3(w_lo[c % 2], 2 * KT)
                        pe.wait_ge(sem(f"raw_done{c}"), used + 1)
                        if c == 3:
                            pe.wait_ge(*W("gated", 0))
                        else:
                            pe.wait_ge(*W("gated", 3 if c == 0 else c, back=1))
                        for q in range(2):
                            o = psum[UP_BANK[c]][:, T1 * q:T1 * q + T1]
                            for k in range(KT):
                                f = q * KT + k
                                pe.matmul(o, hi[:, f, :], h_hi[:, k, 0:T1], start=(k == 0), stop=False)
                                pe.matmul(o, hi[:, f, :], h_lo[:, k, 0:T1], start=False, stop=False)
                                mm = pe.matmul(o, lo[:, f, :], h_hi[:, k, 0:T1], start=False, stop=(k == KT - 1))
                        mm.then_inc(*T("product", ("up", c)))
                        if c:
                            pe.wait_ge(*W("ada_row", c - 1))
                            ada_turn(psum[3][:, T1 + 6 * c - 6:T1 + 6 * c], ada_row2, 3).then_inc(*T("product", ("turned", c - 1)))
                        if c < 3:
                            if c == 0:
                                pe.wait_ge(*W("ada_col", "col", back=1))
                            pe.wait_ge(*W(f"ada_full{c}", 0))
                            ada_rows(ada_raw[c], psum[3]).then_inc(*T("ada_done", c))
                    for c in range(4, 6):
                        used, _ = st.next(c)
                        hi, lo = w3(w_hi[c % 2], 4), w3(w_lo[c % 2], 4)
                        pe.wait_ge(sem(f"raw_done{c}"), used + 1)
                        for k in range(4):
                            if c == 4:
                                pe.wait_ge(*W("act_ready", k))
                            for m_ in range(4):
                                j = 4 * (c - 4) + m_
                                o = psum[4 + j // 2][:, T1 * (j % 2):T1 * (j % 2) + T1]
                                cut = slice(P * m_, P * m_ + P)
                                pe.matmul(o, hi[:, k, cut], e_hi[:, k, :], start=False, stop=False, skip_group_check=True)
                                pe.matmul(o, hi[:, k, cut], e_lo[:, k, :], start=False, stop=False, skip_group_check=True)
                                mm = pe.matmul(o, lo[:, k, cut], e_hi[:, k, :], start=False, stop=False, skip_group_check=True)
                        mm.then_inc(*T("product", ("down", c)))
                    log.leave()
                st.leave(N_EXP)
                bank_user.clear()

            def ffn(l, which):
                name = stage[0] = f"ffn{l}{'ab'[which]}"
                n = T1 if name == LAST else T2

                def group(tag, back):
                    for c in range(FFN_UP):
                        used, _ = st.next(c % SLOTS)
                        hi, lo = w3(w_hi[c % 2], 2 * KT), w3(w_lo[c % 2], 2 * KT)
                        pe.wait_ge(sem(f"raw_done{c % SLOTS}"), used + 1)
                        if c >= 2:
                            pe.wait_ge(*W("gated", (tag, c - 2)))
                        elif back:
                            pe.wait_ge(*W("gated", (back, FFN_UP - 1 - c), back=1 if back == tag else 0))
                        order = [(q, k) for k in range(KT) for q in range(2)] if c == 0 else \
                            [(q, k) for q in range(2) for k in range(KT)]
                        for q, k in order:
                                o = psum[2 * (c % 2) + q][:, 0:n]
                                if q == 0 and c == 0:
                                    pe.wait_ge(*W("h_ready", k, at=f"norm{name}"))
                                f = q * KT + k
                                pe.matmul(o, hi[:, f, :], h_hi[:, k, 0:n], start=(k == 0), stop=False)
                                pe.matmul(o, hi[:, f, :], h_lo[:, k, 0:n], start=False, stop=False)
                                mm = pe.matmul(o, lo[:, f, :], h_hi[:, k, 0:n], start=False, stop=(k == KT - 1))
                        mm.then_inc(*T("product", (tag, c)))
                    for j in range(KT):
                        c = FFN_UP + j
                        used, _ = st.next(c % SLOTS)
                        hi, lo = w3(w_hi[c % 2][:, 0:DOWN], HALF), w3(w_lo[c % 2][:, 0:DOWN], HALF)
                        pe.wait_ge(sem(f"raw_done{c % SLOTS}"), used + 1)
                        if j >= 4:
                            pe.wait_ge(*W("y_ready", (tag, j - 4)))
                        elif back:
                            pe.wait_ge(*W("y_ready", (back, 4 + j), back=1 if back == tag else 0))
                        o = psum[4 + j % 4][:, 0:n]
                        for k in range(HALF):
                            if j == 0:
                                pe.wait_ge(*W("act_ready", (tag, k)))
                            pe.matmul(o, hi[:, k, :], act_hi[:, k, 0:n], start=(k == 0), stop=False)
                            pe.matmul(o, hi[:, k, :], act_lo[:, k, 0:n], start=False, stop=False)
                            mm = pe.matmul(o, lo[:, k, :], act_hi[:, k, 0:n], start=False, stop=(k == HALF - 1))
                        mm.then_inc(*T("product", (tag, c)))

                if name == LAST:
                    group("g0", None)
                    group("g1", "g0")
                else:
                    with pe.Fori(0, 2) as t:
                        st.enter(t, FFN_CH)
                        log.enter(name, t, 2)
                        group("g", "g")
                        log.leave()
                    st.leave(2)
                bank_user.clear()

            def mlstm():
                stage[0] = "mix0"
                for b in range(4):
                    bank_ready(b)
                pe.wait_ge(*W("gate_in", 0, at="load"))
                for t in range(2):
                    for k in range(KT):
                        for x, h in enumerate((h_hi, h_lo)):
                            mm = pe.matmul(psum[4][:, 8 * t:8 * t + 8], h[:, k, P * t:P * t + P].bitcast(F32),
                                           w_gate[:, k, :], start=(k == 0 and x == 0), stop=(k == KT - 1 and x == 1))
                mm.then_inc(*T("product", "gates"))
                chunks = iter(range(ADA_MIX + 1))
                more = lambda: ada(next(chunks), ADA_MIX, psum[6:8], psum[5], ada_row1)
                more()
                pe.wait_ge(*W("gate_v", "log_f"))
                pe.matmul(psum[4][:, 16:20], C["upper"], m_lf[:, 0, :], start=True, stop=True)
                pe.matmul(psum[4][:, 20:24], C["upper"], m_lf[:, 1, :], start=True, stop=False)
                mm = pe.matmul(psum[4][:, 20:24], ones, m_lf[:, 0, :], start=False, stop=True)
                mm.then_inc(*T("product", "cum"))
                pe.wait_ge(*W("gate_v", "a"))
                for n, v in enumerate((m_a, m_b)):
                    for t in range(2):
                        mm = pe.transpose(psum[5][0:A_HEADS, T1 * n + P * t:T1 * n + P * t + P], v[:, t, :], ident)
                mm.then_inc(*T("product", "rows"))
                pe.wait_ge(*W("gate_v", "rows"))
                for _ in range(3):
                    more()
                for h in range(A_HEADS):
                    if h:
                        pe.wait_ge(*W("mix_v", ("masked", h - 1)))
                    pe.matmul(psum[0][:, :], ident[0:A_HEADS, h:h + 1].broadcast_to([A_HEADS, P]), m_rows[0:A_HEADS, :],
                              start=True, stop=True).then_inc(*T("product", ("bc", h)))
                    pe.matmul(psum[1][:, 0:T1], m_k[:, h, 0:P], m_q[:, h, :], start=True, stop=True)
                    pe.matmul(psum[1][:, T1:T1 + P], m_k[:, h, P:T1], m_q[:, h, P:T1], start=True, stop=True)\
                        .then_inc(*T("product", ("scores", h)))
                    more()
                    pe.wait_ge(*W("mix_v", ("masked", h)))
                    if h:
                        pe.wait_ge(*W("mix_v", ("normed", h - 1)))
                    for o, lhs in ((psum[2][:, 0:T1], lambda s: ones),
                                   (psum[3][:, 0:T1], lambda s: m_v[:, s, A_V * h:A_V * h + P]),
                                   (psum[3][:, T1:T2], lambda s: m_v[:, s, A_V * h + P:A_V * h + A_V])):
                        pe.matmul(o, lhs(0), m_p[:, 0:T1], start=True, stop=False)
                        mm = pe.matmul(o[:, P:T1], lhs(1), m_p[:, T1:T1 + P], start=False, stop=True)
                    mm.then_inc(*T("product", ("sums", h)))
                    more()
                    pe.wait_ge(*W("mix_a", ("squared", h)))
                    pe.matmul(psum[2][:, T1:T2], ones, m_d2[:, 0:T1], start=True, stop=False)
                    pe.matmul(psum[2][:, T1:T2], ones, m_d2[:, T1:T2], start=False, stop=True)\
                        .then_inc(*T("product", ("head_sq", h)))
                    more()
                more()
                bank_user.clear()

            def diff():
                stage[0] = "mix1"
                for n in range(16):
                    b = 4 + n % 2
                    pe.wait_ge(*W("mix_a", ("sq", n)))
                    if n >= 2:
                        pe.wait_ge(*W("mix_v", ("roped", n - 2)))
                    pe.matmul(psum[b][:, 0:T1], C["block_ones"], d_sq[n % 2], start=True, stop=True)\
                        .then_inc(*T("product", ("sq", n)))
                    pe.wait_ge(*W("mix_v", ("normed", n)))
                    pe.matmul(psum[b][:, T1:T2], C["rope1"], (d_q if n < 8 else d_k)[:, n % 8, :], start=True, stop=True)\
                        .then_inc(*T("product", ("rot", n)))
                pe.wait_ge(*W("mix_v", ("roped", 15)))
                for b in range(4):
                    bank_ready(b)
                U = 2 * B_HEADS
                for u in range(U + 2):
                    if u < U:
                        h, qb = u // 2, u % 2
                        keys = P * (qb + 1)
                        if u >= 2:
                            pe.wait_ge(*W("mix_a", ("exp", u - 2)))
                        for x in range(2):
                            half = slice(64 * x, 64 * x + 64)
                            mm = pe.matmul(psum[4 * (u % 2) + x][:, 0:keys], d_q[half, h, P * qb:P * qb + P],
                                           d_k[half, h, 0:keys], start=True, stop=True)
                        mm.then_inc(*T("product", ("scores", u)))
                    if 1 <= u <= U:
                        v = u - 1
                        pe.wait_ge(*W("mix_v", ("probs", v)))
                        if v >= 2:
                            pe.wait_ge(*W("mix_a", ("turned", v - 2)))
                        for t in range(v % 2 + 1):
                            mm = pe.transpose(psum[2 + v % 2][:, P * t:P * t + P], d_p[v % 2][:, 0, P * t:P * t + P], ident)
                        mm.then_inc(*T("product", ("turn", v)))
                    if u >= 2 and (u - 2) % 2:
                        h = (u - 2) // 2
                        pe.wait_ge(*W("mix_a", ("turned", u - 2)))
                        if h >= 1:
                            pe.wait_ge(*W("h_ready", h - 1))
                        at = d_at[h % 2]
                        pe.matmul(psum[6][:, 0:T1], d_v[:, 0, P * h:P * h + P], at[:, 0, :], start=True, stop=False)
                        pe.matmul(psum[6][:, P:T1], d_v[:, 1, P * h:P * h + P], at[:, 1, P:T1], start=False, stop=True)\
                            .then_inc(*T("product", ("out", h)))
                        pe.wait_ge(*W("mix_a", ("osq", h)))
                        pe.matmul(psum[7][:, 0:T1], ones, d_sq[0], start=True, stop=True)\
                            .then_inc(*T("product", ("osum", h)))
                bank_user.clear()

            def attention(l):
                stage[0] = f"mix2.{l}"
                nq = T1 if l == DEPTH - 1 else T2
                pe.wait_ge(*W("consts2_in", 0, at="load"))
                for b in range(4):
                    bank_ready(b)
                for n in range(4):
                    w = T2 if n == 3 else nq
                    src = g_ka if n == 3 else g_q[:, n, :]
                    pe.wait_ge(*W("mix_a", ("sq", n)))
                    pe.matmul(psum[4][:, 0:w], C["block_ones"], g_p[n % 2][:, 0:w], start=True, stop=True)\
                        .then_inc(*T("product", ("sq", n)))
                    pe.wait_ge(*W("mix_v", ("normed", n)))
                    pe.matmul(psum[5][:, 0:T1], C2["rope2"], src[:, 0:T1], start=True, stop=True)\
                        .then_inc(*T("product", ("rot", n)))
                    pe.wait_ge(*W("mix_v", ("roped", n)))
                for n, dup in enumerate(("dup0", "dup1")):
                    pe.matmul(psum[4 + n][:, :], C2[dup], g_ka, start=True, stop=True)\
                        .then_inc(*T("product", ("dup", n)))
                pe.wait_ge(*W("mix_a", ("dup", 1)))
                pe.wait_ge(*W("mix_v", "conv"))
                us = units(l)
                for u in range(len(us) + 2):
                    if u < len(us):
                        s, hd, qb = us[u]
                        k0, k1 = keys_of(s)
                        tile, half = hd // 2, slice(64 * (hd % 2), 64 * (hd % 2) + 64)
                        k = g_kd[half, hd // 3, k0:k1] if hd < 6 else g_kb[half, tile - 3, k0:k1]
                        q0 = k0 * 0 + (T1 * s) + P * qb
                        if u >= 2:
                            pe.wait_ge(*W("mix_a", ("exp", u - 2)))
                        pe.matmul(psum[u % 2][:, 0:k1 - k0], g_q[half, tile, q0:q0 + P], k, start=True, stop=True)\
                            .then_inc(*T("product", ("scores", u)))
                    if 1 <= u <= len(us):
                        v = u - 1
                        s = us[v][0]
                        k0, k1 = keys_of(s)
                        pe.wait_ge(*W("mix_v", ("probs", v)))
                        if v >= 2:
                            pe.wait_ge(*W("mix_a", ("turned", v - 2)))
                        for t in range((k1 - k0) // P):
                            mm = pe.transpose(psum[2 + v % 2][:, P * t:P * t + P], g_p[v % 2][:, P * t:P * t + P], ident)
                        mm.then_inc(*T("product", ("turn", v)))
                    if u >= 2 and (u - 2) % 2:
                        v = u - 2
                        s, hd, _ = us[v]
                        k0, k1 = keys_of(s)
                        x = v // 2
                        half = slice(64 * (hd % 2), 64 * (hd % 2) + 64)
                        c0 = 64 * (hd // 3) if hd < 6 else P + 64 * (hd - 6)
                        pe.wait_ge(*W("mix_a", ("turned", v)))
                        if x >= 2:
                            pe.wait_ge(*W("h_ready", x - 2))
                        nt = (k1 - k0) // P
                        for t in range(nt):
                            mm = pe.matmul(psum[6 + x % 2][half, 0:T1], g_v[:, k0 // P + t, c0:c0 + 64],
                                           g_pt[x % 2][:, t, :], start=(t == 0), stop=(t == nt - 1))
                        mm.then_inc(*T("product", ("out", x)))
                bank_user.clear()

            def turn_out():
                stage[0] = "store"
                for t in range(2):
                    for j in range(KT):
                        if t == 0:
                            pe.wait_ge(*W("x_ready", j, at=f"post{LAST}"))
                        mm = pe.transpose(psum[2 * t + j // 4][:, P * (j % 4):P * (j % 4) + P], X[:, j, P * t:P * t + P], ident)
                        if j % 4 == 3:
                            mm.then_inc(*T("product", (t, j // 4)))

            pe.wait_ge(*W("small_in", "all", at="load"))
            pe.wait_ge(*W("setup", "act", at="load"))
            pe.wait_ge(*W("ones_set", 0, at="load"))
            turn_in()
            pe.wait_ge(*W("x_ready", KT - 1, at="turn_in"))
            sum_squares("norm0.0", T1)
            for c in range(ADA_START + 1):
                ada(c, ADA_START, psum[0:2], psum[4], ada_row0)
            linear("mlstm", "norm0.0")
            mlstm()
            linear("mlstm_out", "mix0", per_tile=False)
            sum_squares("norm0.1", T1)
            moe(0)
            sum_squares("norm1.0", T1)
            linear("diff", "norm1.0")
            diff()
            linear("diff_out", "mix1", per_tile=False)
            sum_squares("norm1.1", T1)
            moe(1)
            for l in range(DEPTH):
                last = T1 if l == DEPTH - 1 else T2
                sum_squares(f"normffn{l}a", T2)
                ffn(l, 0)
                sum_squares(f"post{l}.0", T2)
                sum_squares(f"normin{l}", T2)
                linear(f"in{l}", f"normin{l}")
                attention(l)
                linear(f"attn_out{l}", f"mix2.{l}", per_tile=False)
                sum_squares(f"post{l}.1", last)
                sum_squares(f"normffn{l}b", last)
                ffn(l, 1)
                sum_squares(f"postffn{l}b", last)
            turn_out()

        @block.scalar
        def _(act):
            st = Stream()
            split_user = {}

            def step(ins, key=None):
                ins.then_inc(*T("act_step", ("n", log.count.get("act_step", 0))))
                act.wait_ge(sem("act_step"), log.count["act_step"])

            def split_hi(c, size, user, back=0):
                used, n = st.next(c % SLOTS)
                act.wait_ge(sem(f"raw_full{c % SLOTS}"), used * 16)
                if user:
                    act.wait_ge(*W("product", user[0], at=user[1], back=back))
                act.activation(w_hi[c % 2][:, 0:size], raw[c % SLOTS][:, 0:size], ACT.Copy).then_inc(sem("hi_ready"), 1)

            def ada(c, bank, row):
                used, _ = st.next(c % SLOTS, 0)
                act.wait_ge(sem(f"raw_done{c % SLOTS}"), used + 1)
                act.activation(row[:, c % 2, :], bank[:, 0:256], ACT.Copy).then_inc(*T("ada_row", c))

            def root(n):
                act.wait_ge(*W("product", "squares"))
                act.activation(rms4[:, 0:n // P], psum[3][:, 0:n // P], ACT.Sqrt, bias=epsc, scale=1.0 / D).then_inc(*T("rms", 0))

            def norm(name, n, parts, x_at, between=None):
                stage[0] = name
                act.activation(warm[:, 0:1], onec, ACT.Sqrt)
                if x_at.endswith("_out"):
                    act.wait_ge(*W(*x_key(x_at, KT - 1)))
                for j in range(KT):
                    act.wait_ge(*W(*x_key(x_at, j)))
                    act.activation(squares[:, j, 0:n], X[:, j, 0:n], ACT.Square).then_inc(*T("squared", j))
                root(n)
                if between:
                    between()
                for j in range(KT):
                    act.wait_ge(*W("scaled", j))
                    for a, b, _, sh in parts:
                        ins = act.activation(h_hi[:, j, a:b], quad[j % 4][:, a:b], ACT.Identity, bias=sh(j))
                    ins.then_inc(*T("h_upper", j))

            def post(name, n):
                stage[0] = name
                act.activation(warm[:, 0:1], onec, ACT.Sqrt)
                if name.endswith(".1"):
                    act.wait_ge(*W(*y_key(name, KT - 1)))
                for j in range(KT):
                    act.wait_ge(*W(*y_key(name, j)))
                    act.activation(squares[:, j, 0:n], Y[:, j, 0:n], ACT.Square).then_inc(*T("squared", j))
                root(n)

            def linear(name, evac, following):
                stage[0] = name
                chunks = ITEMS[name]
                for c in range(len(chunks)):
                    if c + 1 < len(chunks):
                        split_hi(c + 1, SLOT, split_user.get((c + 1) % 2))
                    elif following:
                        split_hi(0, SLOT, split_user.get(0))
                    split_user[c % 2] = (last_item(name, c), name)
                    for n in range(len(chunks[c])):
                        if EVAC[name](c, n) == "evac_a":
                            act.wait_ge(*W("product", (c, n)))
                            evac(c, n).then_inc(*T("evac_a", (c, n)))

            def moe(l):
                name = stage[0] = f"moe{l}"
                act.wait_ge(*W("product", "router"))
                act.activation(e_s.rearrange("p t e -> p (t e)"), psum[0][:, 0:32], ACT.Sigmoid).then_inc(*T("scores", 0))
                with act.Fori(0, N_EXP) as i:
                    st.enter(i, EXP_CH)
                    log.enter(name, i, N_EXP)
                    def upper(c):
                        act.wait_ge(*W("gated", c))
                        act.activation(e_hi[:, c, :], full[c % 2][:, 0:T1], ACT.Copy).then_inc(*T("act_upper", c))

                    for c in range(EXP_CH):
                        if c == 4:
                            upper(3)
                        if c == 0:
                            split_hi(1, SLOT, (("down", 5), name), back=1)
                        elif c == EXP_CH - 1:
                            split_hi(0, SLOT, (("down", 4), name))
                        else:
                            split_hi(c + 1, SLOT, (("down" if c > 4 else "up", c - 1), name))
                        if 1 <= c <= 3:
                            act.wait_ge(*W("ada_done", c - 1))
                            act.activation(ada_row2, psum[3][:, 0:256], ACT.Copy).then_inc(*T("ada_row", c - 1))
                        if c < 4:
                            act.wait_ge(*W("product", ("up", c)))
                            act.activation(tmp[c % 2][:, 0:T1], psum[UP_BANK[c]][:, 0:T1], ACT.Silu).then_inc(*T("silu", c))
                        if 1 <= c <= 3:
                            upper(c - 1)
                    log.leave()
                st.leave(N_EXP)
                split_user[0], split_user[1] = (("down", 4), name), (("down", 5), name)

            def ffn(l, which, following):
                name = stage[0] = f"ffn{l}{'ab'[which]}"
                n = T1 if name == LAST else T2

                def group(tag, more):
                    def upper(c):
                        act.wait_ge(*W("gated", (tag, c)))
                        act.activation(act_hi[:, c, 0:n], full[c % 2][:, 0:n], ACT.Copy).then_inc(*T("act_upper", (tag, c)))

                    for c in range(FFN_CH):
                        if c == FFN_UP:
                            upper(c - 1)
                        if c + 1 < FFN_CH:
                            user = ((tag, c - 1), name) if c else split_user.get(1)
                            split_hi(c + 1, SLOT if c + 1 < FFN_UP else DOWN, user)
                        if c < FFN_UP:
                            act.wait_ge(*W("product", (tag, c)))
                            act.activation(tmp[c % 2][:, 0:n], psum[2 * (c % 2)][:, 0:n], ACT.Silu).then_inc(*T("silu", (tag, c)))
                        if 1 <= c < FFN_UP:
                            upper(c - 1)
                    if more:
                        split_hi(0, SLOT, ((tag, FFN_CH - 1), name))
                    split_user[0], split_user[1] = ((tag, FFN_CH - 1), name), ((tag, FFN_CH - 2), name)

                if name == LAST:
                    group("g0", True)
                    group("g1", following)
                else:
                    act.wait_ge(*W("product", split_user[1][0], at=split_user[1][1]))
                    split_user.pop(1)
                    with act.Fori(0, 2) as t:
                        st.enter(t, FFN_CH)
                        log.enter(name, t, 2)
                        group("g", True)
                        log.leave()
                    st.leave(2)

            def mlstm_evac(c, n):
                b = psum[bank_of("mlstm", c, n)][:, 0:T1]
                if c < 4:
                    j = 2 * (c % 2) + n
                    return act.activation((m_q if c < 2 else m_k)[:, j, :], b, ACT.Copy, scale=1.0 if c < 2 else A_QK ** -0.5)
                return act.activation(m_og[:, 2 * (c - 8) + n, :], b, ACT.Sigmoid)

            def mlstm():
                stage[0] = "mix0"
                act.wait_ge(*W("gate_v", "gates"))
                step(act.activation(m_u, m_g[:, :, A_HEADS:], ACT.Abs))
                step(act.activation(m_u, m_u, ACT.Exp, scale=-1.0))
                act.activation(m_u, m_u, ACT.Ln, bias=onec).then_inc(*T("mix_a", "log1p"))
                chunks = iter(range(ADA_MIX))

                def more():
                    c = next(chunks)
                    ada(c, psum[6 + c % 2], ada_row1)

                for _ in range(4):
                    more()
                for h in range(A_HEADS):
                    act.wait_ge(*W("mix_v", ("gap", h)))
                    act.activation(m_d, m_d, ACT.Exp, scale=-1.0).then_inc(*T("mix_a", ("decay", h)))
                    act.activation(m_em, psum[0][:, T1:T2], ACT.Exp, scale=-1.0).then_inc(*T("mix_a", ("floor", h)))
                    more()
                    act.wait_ge(*W("product", ("sums", h)))
                    act.activation(m_dn, psum[2][:, 0:T1], ACT.Abs).then_inc(*T("mix_a", ("den", h)))
                    more()
                    act.wait_ge(*W("mix_v", ("normed", h)))
                    act.activation(m_d2, m_hh.rearrange("p a t -> p (a t)"), ACT.Square).then_inc(*T("mix_a", ("squared", h)))
                    act.wait_ge(*W("product", ("head_sq", h)))
                    act.activation(m_rstd[:, 0:T1], psum[2][:, T1:T2], ACT.Sqrt, bias=epsc, scale=1.0 / A_V).then_inc(*T("mix_a", ("rms", h)))
                    more()
                    if h == A_HEADS - 1:
                        split_hi(0, SLOT, split_user.get(0))
                    act.wait_ge(*W("mix_v", ("out", h)))
                    act.activation(h_hi[:, 2 * h:2 * h + 2, 0:T1], m_full, ACT.Copy).then_inc(*T("mix_a", ("upper", h)))

            def diff_evac(c, n):
                j = 2 * (c % 4) + n
                return act.activation((d_q if c < 4 else d_k)[:, j, :], psum[bank_of("diff", c, n)][:, 0:T1], ACT.Copy)

            def diff():
                stage[0] = "mix1"
                act.wait_ge(*W("mix_v", "angles"))
                act.activation(d_sin, d_ang, ACT.Sin)
                act.activation(d_n, d_n, ACT.Sin).then_inc(*T("mix_a", "sines"))
                act.wait_ge(*W("mix_v", "dots"))
                act.activation(d_ls[:, 2:4], d_ls[:, 0:2], ACT.Exp).then_inc(*T("mix_a", "lam"))
                for n in range(16):
                    if n == 0:
                        act.wait_ge(*W("evac_a", (7, 1), at="diff"))
                    if n >= 2:
                        act.wait_ge(*W("product", ("sq", n - 2)))
                    act.activation(d_sq[n % 2], (d_q if n < 8 else d_k)[:, n % 8, :], ACT.Square).then_inc(*T("mix_a", ("sq", n)))
                    act.wait_ge(*W("product", ("sq", n)))
                    if n >= 2:
                        act.wait_ge(*W("mix_v", ("normed", n - 2)))
                    act.activation(d_rs[n % 2], psum[4 + n % 2][:, 0:T1], ACT.Sqrt, bias=epsc, scale=1.0 / B_HD)\
                        .then_inc(*T("mix_a", ("rms", n)))
                U = 2 * B_HEADS
                for u in range(U + 2):
                    if u < U:
                        keys = P * (u % 2 + 1)
                        act.wait_ge(*W("mix_v", ("max", u)))
                        if u >= 2:
                            act.wait_ge(*W("product", ("turn", u - 2)))
                        for x in range(2):
                            ins = act.activation(d_p[u % 2][:, x, 0:keys], psum[4 * (u % 2) + x][:, 0:keys], ACT.Exp,
                                                 bias=d_st[u % 2][:, x:x + 1], accum_out=d_st[u % 2][:, 2 + x:3 + x])
                        ins.then_inc(*T("mix_a", ("exp", u)))
                    if 1 <= u <= U:
                        v = u - 1
                        act.wait_ge(*W("product", ("turn", v)))
                        if v >= 4:
                            act.wait_ge(*W("product", ("out", v // 2 - 2)))
                        t = v % 2 + 1
                        act.activation(d_at[(v // 2) % 2][:, 0:t, P * (v % 2):P * (v % 2) + P],
                                       psum[2 + v % 2][:, 0:P * t].rearrange("p (t n) -> p t n", t=t), ACT.Copy)\
                            .then_inc(*T("mix_a", ("turned", v)))
                    if u >= 2 and (u - 2) % 2:
                        h = (u - 2) // 2
                        act.wait_ge(*W("product", ("out", h)))
                        act.activation(d_sq[0], psum[6][:, 0:T1], ACT.Square).then_inc(*T("mix_a", ("osq", h)))
                        act.wait_ge(*W("product", ("osum", h)))
                        act.activation(d_rs[0], psum[7][:, 0:T1], ACT.Sqrt, bias=epsc, scale=1.0 / (2 * B_HD)).then_inc(*T("mix_a", ("orms", h)))
                        act.wait_ge(*W("mix_v", ("out", h)))
                        act.activation(h_hi[:, h, 0:T1], d_raw[0], ACT.Copy).then_inc(*T("mix_a", ("upper", h)))

            def in_evac(name, l):
                nq = T1 if l == DEPTH - 1 else T2

                def f(c, n):
                    bank = psum[bank_of(name, c, n)]
                    if c < 3:
                        j = 2 * c + n
                        return act.activation(g_q[:, j, 0:nq], bank[:, 0:nq], ACT.Copy, scale=1.0 if j < 3 else HD ** -0.5)
                    if c == 3:
                        return act.activation(g_ka, bank[:, :], ACT.Copy)
                    if c in (4, 5):
                        return act.activation(g_kb[:, 2 * (c - 4) + n, :], bank[:, :], ACT.Copy)
                    dst = (g_cx, g_cb, g_cc)[c - 7]
                    return act.activation(dst[:, n, 0:nq], bank[:, 0:nq], ACT.Copy)
                return f

            def attention(l):
                stage[0] = f"mix2.{l}"
                nq = T1 if l == DEPTH - 1 else T2
                for n in range(4):
                    w = T2 if n == 3 else nq
                    src = g_ka if n == 3 else g_q[:, n, :]
                    if n == 0:
                        act.wait_ge(*W("evac_a", (9, 1), at=f"in{l}"))
                    if n >= 2:
                        act.wait_ge(*W("product", ("sq", n - 2)))
                    act.activation(g_p[n % 2][:, 0:w], src[:, 0:w], ACT.Square).then_inc(*T("mix_a", ("sq", n)))
                    act.wait_ge(*W("product", ("sq", n)))
                    if n:
                        act.wait_ge(*W("mix_v", ("normed", n - 1)))
                    act.activation(g_rstd[:, 0:w], psum[4][:, 0:w], ACT.Sqrt, bias=epsc, scale=1.0 / HD).then_inc(*T("mix_a", ("rms", n)))
                for n in range(2):
                    act.wait_ge(*W("product", ("dup", n)))
                    act.activation(g_kd[:, n, :], psum[4 + n][:, :], ACT.Copy).then_inc(*T("mix_a", ("dup", n)))
                for n in range(2):
                    act.wait_ge(*W("mix_v", ("conv", n)))
                    act.activation(h_hi[:, 6 + n, 0:nq], full[0][:, 0:nq], ACT.Copy).then_inc(*T("mix_a", ("conv", n)))
                us = units(l)
                for u in range(len(us) + 2):
                    if u < len(us):
                        s = us[u][0]
                        k0, k1 = keys_of(s)
                        act.wait_ge(*W("mix_v", ("max", u)))
                        if u >= 2:
                            act.wait_ge(*W("product", ("turn", u - 2)))
                        act.activation(g_p[u % 2][:, 0:k1 - k0], psum[u % 2][:, 0:k1 - k0], ACT.Exp,
                                       bias=g_st[u % 2][:, 0:1], accum_out=g_st[u % 2][:, 1:2]).then_inc(*T("mix_a", ("exp", u)))
                    if 1 <= u <= len(us):
                        v = u - 1
                        s, hd, qb = us[v]
                        k0, k1 = keys_of(s)
                        nt = (k1 - k0) // P
                        act.wait_ge(*W("product", ("turn", v)))
                        if v >= 4:
                            act.wait_ge(*W("product", ("out", v // 2 - 2)))
                        if v == 0:
                            act.wait_ge(*W("mix_v", "conv"))
                        act.activation(g_pt[(v // 2) % 2][:, 0:nt, P * qb:P * qb + P],
                                       psum[2 + v % 2][:, 0:P * nt].rearrange("p (t n) -> p t n", t=nt), ACT.Copy)\
                            .then_inc(*T("mix_a", ("turned", v)))
                    if u >= 2 and (u - 2) % 2:
                        v = u - 2
                        s, hd, _ = us[v]
                        x = v // 2
                        half = slice(64 * (hd % 2), 64 * (hd % 2) + 64)
                        act.wait_ge(*W("product", ("out", x)))
                        act.activation(h_hi[half, hd // 2, T1 * s:T1 * s + T1], psum[6 + x % 2][half, 0:T1], ACT.Copy)\
                            .then_inc(*T("mix_a", ("upper", x)))

            act.wait_ge(*W("small_in", "all", at="load"))
            act.wait_ge(*W("ones_set", 0, at="load"))
            act.activation(cact[:, :, 0], V["c1"], ACT.Silu)
            act.activation(cact[:, :, 1:3], V["c2"].rearrange("p (k s) -> p k s", k=KT), ACT.Silu).then_inc(*T_at("setup", "act"))
            def start():
                for c in range(ADA_START):
                    ada(c, psum[c % 2], ada_row0)
                split_hi(0, SLOT, None)
                act.wait_ge(*W("mods", "0.0", at="load"))

            norm("norm0.0", T1, part1(0, 0), "turn_in", start)
            linear("mlstm", mlstm_evac, False)
            mlstm()
            linear("mlstm_out", None, True)
            act.wait_ge(*W("mods", "0.1", at="load"))
            norm("norm0.1", T1, part1(0, 1), "mlstm_out")
            moe(0)
            act.wait_ge(*W("mods", "1", at="load"))
            norm("norm1.0", T1, part1(1, 0), "moe0")
            linear("diff", diff_evac, True)
            diff()
            linear("diff_out", None, True)
            norm("norm1.1", T1, part1(1, 1), "diff_out")
            moe(1)
            act.wait_ge(*W("mods", "2", at="load"))
            for l in range(DEPTH):
                both = l < DEPTH - 1
                n = T2 if both else T1
                norm(f"normffn{l}a", T2, part2(l, 0, 1), "moe1" if l == 0 else f"postffn{l - 1}b")
                ffn(l, 0, True)
                post(f"post{l}.0", T2)
                norm(f"normin{l}", T2, part2(l, 1, 1), f"post{l}.0")
                linear(f"in{l}", in_evac(f"in{l}", l), True)
                attention(l)
                linear(f"attn_out{l}", None, True)
                post(f"post{l}.1", n)
                norm(f"normffn{l}b", n, part2(l, 2, both), f"post{l}.1")
                ffn(l, 1, both)
                post(f"postffn{l}b", n)

        @block.vector
        def _(dve):
            st = Stream()

            def step(ins):
                ins.then_inc(*T("vec_step"))
                dve.wait_ge(sem("vec_step"), log.count["vec_step"])

            def split_lo(c, size):
                _, n = st.next(c % SLOTS)
                dve.wait_ge(sem("hi_ready"), n)
                dve.tensor_tensor(w_lo[c % 2][:, 0:size], raw[c % SLOTS][:, 0:size], w_hi[c % 2][:, 0:size].bitcast(F32),
                                  ALU.subtract).then_inc(sem(f"raw_done{c % SLOTS}"), 1)

            def mods_first(lo, hi, cols, w):
                step(dve.tensor_tensor(mod_first[:, lo:hi], cols[:, 0:hi - lo], V["b_ada"][:, lo:hi], ALU.add))
                pre_scales(0, w).then_inc(*T_at("mods", f"0.{w}"))
                dve.wait_ge(*W("mods", f"0.{w}", at="load"))

            def pre_scales(l, w):
                return dve.scalar_tensor_tensor(pre1[:, l, w, :], mod1[l][:, 24 * w + 8:24 * w + 16], 1.0,
                                                V["norm1" if w == 0 else "norm2"][:, 8 * l:8 * l + 8], ALU.add, ALU.mult)

            def mods_second():
                step(dve.tensor_tensor(mod1[1], mod1[1], V["b_ada"][:, 48:96], ALU.add))
                pre_scales(1, 0)
                pre_scales(1, 1).then_inc(*T_at("mods", "1"))
                dve.wait_ge(*W("mods", "1", at="load"))

            def mods_latent():
                m2 = mod_all[:, 48:, :]
                for s in range(2):
                    ins = dve.tensor_tensor(m2[:, :, 1 + s], m2[:, :, 1 + s], V["b_ada_2"], ALU.add)
                step(ins)
                ng = V["norm_g_2"].rearrange("p (l g k) -> p l g k", l=DEPTH, g=6)
                for l in range(DEPTH):
                    for i in range(3):
                        for s in range(2):
                            dve.scalar_tensor_tensor(pre2[:, l, i, :, s], mod2[:, l, 3 * i + 1, :, s], 1.0, ng[:, l, 2 * i, :],
                                                     ALU.add, ALU.mult)
                            ins = dve.scalar_tensor_tensor(post2[:, l, i, :, s], mod2[:, l, 3 * i + 2, :, s],
                                                           1.0 if i == 1 else 0.5, ng[:, l, 2 * i + 1, :], ALU.mult, ALU.mult)
                ins.then_inc(*T_at("mods", "2"))
                dve.wait_ge(*W("mods", "2", at="load"))

            def turn_in():
                stage[0] = "turn_in"
                for j in range(KT):
                    dve.wait_ge(*W("product", j))
                    dve.tensor_copy(X[:, j, :], psum[j][:, :]).then_inc(*T("x_ready", j))

            def inverse(n):
                dve.wait_ge(*W("rms", 0))
                dve.reciprocal(inv4[:, 0:n // P], rms4[:, 0:n // P]).then_inc(*T("inverse", 0))
                dve.wait_ge(*W("product", "rstd"))

            def norm(name, n, parts, between=None):
                stage[0] = name
                inverse(n)
                if between:
                    between()
                for j in range(KT + 1):
                    if j < KT:
                        if j >= 4:
                            dve.wait_ge(*W("h_ready", j - 4))
                        for a, b, sc, _ in parts:
                            ins = dve.scalar_tensor_tensor(quad[j % 4][:, a:b], X[:, j, a:b], sc(j), psum[7][:, a:b], ALU.mult, ALU.mult)
                        ins.then_inc(*T("scaled", j))
                    if j:
                        k = j - 1
                        dve.wait_ge(*W("h_upper", k))
                        for a, b, _, sh in parts:
                            ins = dve.scalar_tensor_tensor(h_lo[:, k, a:b], quad[k % 4][:, a:b], sh(k), h_hi[:, k, a:b].bitcast(F32),
                                                           ALU.add, ALU.subtract)
                        ins.then_inc(*T("h_ready", k))

            def post(name, n, l, i):
                stage[0] = name
                inverse(n)
                for j in range(KT + 1):
                    if j < KT:
                        if j >= 2:
                            dve.wait_ge(*W("x_ready", j - 2))
                        dve.tensor_tensor(tmp[j % 2][:, 0:n], Y[:, j, 0:n], psum[7][:, 0:n], ALU.mult).then_inc(*T("scaled", j))
                    if j:
                        k = j - 1
                        dve.wait_ge(*W("scaled", k))
                        for s in range(n // T1):
                            cut = slice(T1 * s, T1 * s + T1)
                            ins = dve.scalar_tensor_tensor(X[:, k, cut], tmp[k % 2][:, cut], post2[:, l, i, k, s:s + 1],
                                                           X[:, k, cut], ALU.mult, ALU.add)
                        ins.then_inc(*T("x_ready", k))
                dve.wait_ge(*W("x_ready", KT - 1))

            def linear(name, evac, following):
                stage[0] = name
                chunks = ITEMS[name]
                for c in range(len(chunks)):
                    if c + 1 < len(chunks):
                        split_lo(c + 1, SLOT)
                    elif following:
                        split_lo(0, SLOT)
                    for n in range(len(chunks[c])):
                        if EVAC[name](c, n) == "evac_v":
                            dve.wait_ge(*W("product", (c, n)))
                            evac(c, n).then_inc(*T("evac_v", (c, n)))

            def residual(name, l, w):
                def f(c, n):
                    j = 2 * c + n
                    return dve.scalar_tensor_tensor(X[:, j, 0:T1], psum[bank_of(name, c, n)][:, 0:T1],
                                                    mod1[l][:, 24 * w + 16 + j:24 * w + 17 + j], X[:, j, 0:T1], ALU.mult, ALU.add)
                return f

            def moe(l):
                name = stage[0] = f"moe{l}"
                dve.memset(e_zero.bitcast(U32), 0)
                dve.wait_ge(*W("scores", 0))
                for t in range(2):
                    step(dve.tensor_tensor(e_b[:, t, :], e_s[:, t, :], V["router_bias"], ALU.add))
                for t in range(2):
                    b = e_b[:, t, :].rearrange("p (g e) -> p g e", g=N_GRP)
                    pairs = [(x, y) for x in range(E_GRP) for y in range(x + 1, E_GRP)]
                    for n, (x, y) in enumerate(pairs):
                        ins = dve.tensor_tensor(e_pair[:, :, n:n + 1], b[:, :, x:x + 1], b[:, :, y:y + 1], ALU.add)
                    step(ins)
                    step(dve.memset(e_g8, INVALID))
                    step(dve.tensor_reduce(e_g8[:, 0:N_GRP], e_pair, AX.X, ALU.max))
                    step(dve.max(e_x8, e_g8))
                    step(dve.max_index(e_i8, e_x8, e_g8))
                    step(dve.tensor_copy(e_f8, e_i8))
                    step(dve.tensor_scalar(e_oh, C["iota8"], e_f8[:, 0:1], None, ALU.is_equal))
                    for q in range(N_GRP):
                        ins = dve.tensor_scalar(e_m[:, t, 4 * q:4 * q + 4], e_b[:, t, 4 * q:4 * q + 4], e_oh[:, q:q + 1], None, ALU.mult)
                    step(ins)
                    step(dve.tensor_scalar(e_oh, e_oh, -1.0, -INVALID, ALU.add, ALU.mult))
                    for q in range(N_GRP):
                        ins = dve.tensor_scalar(e_m[:, t, 4 * q:4 * q + 4], e_m[:, t, 4 * q:4 * q + 4], e_oh[:, q:q + 1], None, ALU.add)
                    step(ins)
                    step(dve.max(e_x8, e_m[:, t, :]))
                    step(dve.max_index(e_i8, e_x8, e_m[:, t, :]))
                    step(dve.tensor_copy(e_f8, e_i8))
                    step(dve.tensor_scalar(e_w[:, t, :], C["iota16"], e_f8[:, 0:1], None, ALU.is_equal))
                    step(dve.scalar_tensor_tensor(e_w[:, t, :], C["iota16"], e_f8[:, 1:2], e_w[:, t, :], ALU.is_equal, ALU.add))
                    step(dve.tensor_tensor(e_w[:, t, :], e_w[:, t, :], e_s[:, t, :], ALU.mult))
                    step(dve.tensor_reduce(e_f8[:, 0:1], e_w[:, t, :], AX.X, ALU.add))
                    step(dve.reciprocal(e_f8[:, 1:2], e_f8[:, 0:1]))
                    ins = dve.tensor_scalar(e_w[:, t, :], e_w[:, t, :], e_f8[:, 1:2], None, ALU.mult)
                    if t == 0:
                        step(ins)
                ins.then_inc(*T("gate_w", "tokens"))
                dve.wait_ge(*W("product", "gate_rows"))
                dve.tensor_copy(e_row, psum[0][0:N_EXP, 128:128 + T1]).then_inc(*T("gate_w", "rows"))
                for x in range(N_EXP):
                    dve.wait_ge(*W("product", ("bc", x)))
                    dve.tensor_copy(e_gate[:, x, :], psum[x % 4][:, 0:T1]).then_inc(*T("gate_bc", x))
                dve.wait_ge(*W("gate_bc", N_EXP - 1))
                with dve.Fori(0, N_EXP) as i:
                    st.enter(i, EXP_CH)
                    log.enter(name, i, N_EXP)

                    def lower(c):
                        dve.wait_ge(*W("act_upper", c))
                        dve.tensor_tensor(e_lo[:, c, :], full[c % 2][:, 0:T1], e_hi[:, c, :].bitcast(F32), ALU.subtract)\
                            .then_inc(*T("act_ready", c))

                    for c in range(EXP_CH):
                        if c == 4:
                            lower(3)
                            dve.wait_ge(*W("product", ("turned", 2)))
                            dve.tensor_copy(mod_all.rearrange("p m s -> p (m s)")[:, ds(i * 18 + 18 * N_EXP * l, 18)],
                                            psum[3][:, T1:T1 + 18]).then_inc(*T("ada_col", "col"))
                        split_lo((c + 1) % EXP_CH, SLOT)
                        if c < 4:
                            dve.wait_ge(*W("silu", c))
                            dve.tensor_tensor(tmp[c % 2][:, T1:T2], tmp[c % 2][:, 0:T1], e_gate[:, ds(i, 1), :].rearrange("p e t -> p (e t)"), ALU.mult)\
                                .then_inc(*T("weighted", c))
                            dve.wait_ge(*W("weighted", c))
                            dve.tensor_tensor(full[c % 2][:, 0:T1], psum[UP_BANK[c]][:, T1:T2], tmp[c % 2][:, T1:T2], ALU.mult)\
                                .then_inc(*T("gated", c))
                        if 1 <= c <= 3:
                            lower(c - 1)
                    log.leave()
                st.leave(N_EXP)
                dve.wait_ge(*W("ada_col", "col"))
                if l == 0:
                    mods_second()
                else:
                    mods_latent()
                dve.wait_ge(*W("product", ("down", 5)))
                for j in range(KT):
                    dve.scalar_tensor_tensor(X[:, j, 0:T1], psum[4 + j // 2][:, T1 * (j % 2):T1 * (j % 2) + T1],
                                             mod1[l][:, 40 + j:41 + j], X[:, j, 0:T1], ALU.mult, ALU.add).then_inc(*T("x_ready", j))

            def ffn(l, which, following):
                name = stage[0] = f"ffn{l}{'ab'[which]}"
                n = T1 if name == LAST else T2
                step(dve.memset(Y, 0.0))

                def group(tag, more):
                    def lower(c):
                        dve.wait_ge(*W("act_upper", (tag, c)))
                        dve.tensor_tensor(act_lo[:, c, 0:n], full[c % 2][:, 0:n], act_hi[:, c, 0:n].bitcast(F32), ALU.subtract)\
                            .then_inc(*T("act_ready", (tag, c)))

                    for c in range(FFN_CH):
                        if c == FFN_UP:
                            lower(c - 1)
                            dve.wait_ge(*W("act_ready", (tag, c - 1)))
                        if c + 1 < FFN_CH:
                            split_lo(c + 1, SLOT if c + 1 < FFN_UP else DOWN)
                        if c < FFN_UP:
                            dve.wait_ge(*W("silu", (tag, c)))
                            if c >= 2:
                                dve.wait_ge(*W("act_ready", (tag, c - 2)))
                            dve.tensor_tensor(full[c % 2][:, 0:n], psum[2 * (c % 2) + 1][:, 0:n], tmp[c % 2][:, 0:n], ALU.mult)\
                                .then_inc(*T("gated", (tag, c)))
                        if 1 <= c < FFN_UP:
                            lower(c - 1)
                        if c >= FFN_UP:
                            j = c - FFN_UP
                            dve.wait_ge(*W("product", (tag, c)))
                            dve.tensor_tensor(Y[:, j, 0:n], Y[:, j, 0:n], psum[4 + j % 4][:, 0:n], ALU.add)\
                                .then_inc(*T("y_ready", (tag, j)))
                    if more:
                        split_lo(0, SLOT)

                if name == LAST:
                    group("g0", True)
                    group("g1", following)
                else:
                    with dve.Fori(0, 2) as t:
                        st.enter(t, FFN_CH)
                        log.enter(name, t, 2)
                        group("g", True)
                        log.leave()
                    st.leave(2)

            def mlstm_evac(c, n):
                return dve.tensor_copy(m_v[:, :, 256 * (c - 4):256 * (c - 4) + 256],
                                       psum[bank_of("mlstm", c, n)][:, :].rearrange("p (t n) -> p t n", t=2))

            def mlstm():
                stage[0] = "mix0"
                dve.wait_ge(*W("product", "gates"))
                for t in range(2):
                    ins = dve.tensor_tensor(m_g[:, t, :], psum[4][:, 8 * t:8 * t + 8], V["b_if"], ALU.add)
                ins.then_inc(*T("gate_v", "gates"))
                dve.wait_ge(*W("mix_a", "log1p"))
                dve.scalar_tensor_tensor(m_lf, m_g[:, :, A_HEADS:], 0.0, m_u, ALU.min, ALU.subtract).then_inc(*T("gate_v", "log_f"))
                dve.wait_ge(*W("product", "cum"))
                step(dve.tensor_copy(m_b.rearrange("p t h -> p (t h)"), psum[4][:, 16:24]))
                dve.tensor_tensor(m_a, m_g[:, :, 0:A_HEADS], m_b, ALU.subtract).then_inc(*T("gate_v", "a"))
                dve.wait_ge(*W("product", "rows"))
                step(dve.tensor_copy(m_arow[0:A_HEADS, :], psum[5][0:A_HEADS, 0:T1]))
                step(dve.tensor_tensor_scan(m_rows[0:A_HEADS, 0:T1], m_arow[0:A_HEADS, :], m_arow[0:A_HEADS, :], 0.0, ALU.max, ALU.max))
                dve.tensor_tensor(m_rows[0:A_HEADS, T1:T2], m_rows[0:A_HEADS, 0:T1], psum[5][0:A_HEADS, T1:T2], ALU.add)\
                    .then_inc(*T("gate_v", "rows"))
                for h in range(A_HEADS):
                    dve.wait_ge(*W("product", ("bc", h)))
                    dve.tensor_scalar(m_d[:, 0:T1], psum[0][:, 0:T1], m_a[:, 0, h:h + 1], 0.0, ALU.subtract, ALU.max)
                    dve.tensor_scalar(m_d[:, T1:T1 + P], psum[0][:, P:T1], m_a[:, 1, h:h + 1], 0.0, ALU.subtract, ALU.max)\
                        .then_inc(*T("mix_v", ("gap", h)))
                    dve.wait_ge(*W("mix_a", ("floor", h)))
                    dve.wait_ge(*W("product", ("scores", h)))
                    step(dve.tensor_tensor(m_p, psum[1][:, 0:384], m_d, ALU.mult))
                    dve.tensor_tensor(m_p[:, 0:P], m_p[:, 0:P], C["upper"], ALU.mult)
                    dve.tensor_tensor(m_p[:, T1:T1 + P], m_p[:, T1:T1 + P], C["upper"], ALU.mult).then_inc(*T("mix_v", ("masked", h)))
                    dve.wait_ge(*W("mix_a", ("den", h)))
                    step(dve.tensor_tensor(m_dn, m_dn, m_em, ALU.max))
                    step(dve.reciprocal(m_dn, m_dn))
                    for q in range(2):
                        ins = dve.tensor_tensor(m_hh[:, q, :], psum[3][:, T1 * q:T1 * q + T1], m_dn, ALU.mult)
                    ins.then_inc(*T("mix_v", ("normed", h)))
                    dve.wait_ge(*W("mix_v", ("normed", h)))
                    dve.wait_ge(*W("mix_a", ("rms", h)))
                    step(dve.reciprocal(m_rstd[:, 0:T1], m_rstd[:, 0:T1]))
                    for q in range(2):
                        j = 2 * h + q
                        ins = dve.scalar_tensor_tensor(m_full[:, q, :], m_hh[:, q, :], V["a_h_norm"][:, j:j + 1], m_rstd[:, 0:T1], ALU.mult, ALU.mult)
                    step(ins)
                    dve.tensor_tensor(m_full, m_full, m_og[:, 2 * h:2 * h + 2, :], ALU.mult).then_inc(*T("mix_v", ("out", h)))
                    dve.wait_ge(*W("mix_a", ("upper", h)))
                    ins = dve.tensor_tensor(h_lo[:, 2 * h:2 * h + 2, 0:T1], m_full, h_hi[:, 2 * h:2 * h + 2, 0:T1].bitcast(F32), ALU.subtract)
                    ins.then_inc(*T("h_ready", h))
                split_lo(0, SLOT)
                dve.wait_ge(*W("product", ("turned", ADA_MIX - 1)))
                mods_first(2 * ADA_START, 48, psum[5], 1)

            def diff_evac(c, n):
                return dve.tensor_copy(d_v[:, :, 256 * (c - 8):256 * (c - 8) + 256],
                                       psum[bank_of("diff", c, n)][:, :].rearrange("p (t n) -> p t n", t=2))

            def diff():
                stage[0] = "mix1"
                TWO_PI = 2 * math.pi
                c1 = 6.28125
                c2 = float(np.float32(np.round((TWO_PI - c1) * 2 ** 22) / 2 ** 22))
                c3 = float(np.float32(TWO_PI - c1 - c2))
                ROUND = 1.5 * 2 ** 23
                dve.wait_ge(*W("diff_in", "all", at="load"))
                step(dve.tensor_copy(d_ang, d_pos))
                step(dve.tensor_scalar(d_ang, d_ang, C["invfreq"], None, ALU.mult))
                step(dve.tensor_scalar(d_n, d_ang, 1.0 / TWO_PI, ROUND, ALU.mult, ALU.add))
                step(dve.tensor_scalar(d_n, d_n, ROUND, None, ALU.subtract))
                for cc in (c1, c2, c3):
                    step(dve.scalar_tensor_tensor(d_ang, d_n, -cc, d_ang, ALU.mult, ALU.add))
                step(dve.tensor_scalar(d_ang, d_ang, math.pi - 1e-6, -(math.pi - 1e-6), ALU.min, ALU.max))
                dve.tensor_scalar(d_n, d_ang, 0.5, None, ALU.mult).then_inc(*T("mix_v", "angles"))
                dve.wait_ge(*W("mix_a", "sines"))
                step(dve.tensor_tensor(d_cos, d_n, d_n, ALU.mult))
                step(dve.tensor_scalar(d_cos, d_cos, -2.0, 1.0, ALU.mult, ALU.add))
                for n in range(2):
                    step(dve.tensor_tensor(d_lam[:, 2 * n, :], d_lam[:, 2 * n, :], d_lam[:, 2 * n + 1, :], ALU.mult))
                    ins = dve.tensor_reduce(d_ls[:, n:n + 1], d_lam[:, 2 * n, :], AX.X, ALU.add)
                ins.then_inc(*T("mix_v", "dots"))
                dve.wait_ge(*W("mix_a", "lam"))
                step(dve.tensor_tensor(d_ls[:, 4:5], d_ls[:, 3:4], d_ls[:, 2:3], ALU.subtract))
                step(dve.tensor_scalar(d_ls[:, 5:6], d_ls[:, 4:5], LAM_INIT, None, ALU.subtract))
                for n in range(16):
                    x = (d_q if n < 8 else d_k)[:, n % 8, :]
                    gain = V["b_q_norm" if n < 8 else "b_k_norm"]
                    dve.wait_ge(*W("mix_a", ("rms", n)))
                    step(dve.reciprocal(d_rs[n % 2], d_rs[n % 2]))
                    if n < 8:
                        step(dve.tensor_scalar(d_rs[n % 2], d_rs[n % 2], B_HD ** -0.5, None, ALU.mult))
                    dve.scalar_tensor_tensor(x, x, gain, d_rs[n % 2], ALU.mult, ALU.mult).then_inc(*T("mix_v", ("normed", n)))
                    dve.wait_ge(*W("product", ("rot", n)))
                    step(dve.tensor_tensor(d_raw[n % 2], psum[4 + n % 2][:, T1:T2], d_sin, ALU.mult))
                    step(dve.tensor_tensor(x, x, d_cos, ALU.mult))
                    dve.tensor_tensor(x, x, d_raw[n % 2], ALU.add).then_inc(*T("mix_v", ("roped", n)))
                U = 2 * B_HEADS
                for u in range(U + 2):
                    if u < U:
                        keys = P * (u % 2 + 1)
                        dve.wait_ge(*W("product", ("scores", u)))
                        for x in range(2):
                            s = psum[4 * (u % 2) + x]
                            ins = dve.tensor_tensor(s[:, keys - P:keys], s[:, keys - P:keys], C["causal"], ALU.add)
                        step(ins)
                        for x in range(2):
                            ins = dve.tensor_reduce(d_st[u % 2][:, x:x + 1], psum[4 * (u % 2) + x][:, 0:keys], AX.X, ALU.max, negate=True)
                        ins.then_inc(*T("mix_v", ("max", u)))
                    if 1 <= u <= U:
                        v = u - 1
                        stt, p = d_st[v % 2], d_p[v % 2]
                        keys = P * (v % 2 + 1)
                        dve.wait_ge(*W("mix_a", ("exp", v)))
                        step(dve.reciprocal(stt[:, 4:6], stt[:, 2:4]))
                        step(dve.tensor_scalar(stt[:, 5:6], stt[:, 5:6], d_ls[:, 5:6], None, ALU.mult))
                        step(dve.tensor_scalar(p[:, 1, 0:keys], p[:, 1, 0:keys], stt[:, 5:6], None, ALU.mult))
                        dve.scalar_tensor_tensor(p[:, 0, 0:keys], p[:, 0, 0:keys], stt[:, 4:5], p[:, 1, 0:keys], ALU.mult, ALU.add)\
                            .then_inc(*T("mix_v", ("probs", v)))
                    if u >= 2 and (u - 2) % 2:
                        h = (u - 2) // 2
                        dve.wait_ge(*W("mix_a", ("orms", h)))
                        step(dve.reciprocal(d_rs[0], d_rs[0]))
                        step(dve.scalar_tensor_tensor(d_raw[0], psum[6][:, 0:T1], V["b_o_norm"], d_rs[0], ALU.mult, ALU.mult))
                        dve.tensor_scalar(d_raw[0], d_raw[0], 1.0 - LAM_INIT, None, ALU.mult).then_inc(*T("mix_v", ("out", h)))
                        dve.wait_ge(*W("mix_a", ("upper", h)))
                        dve.tensor_tensor(h_lo[:, h, 0:T1], d_raw[0], h_hi[:, h, 0:T1].bitcast(F32), ALU.subtract).then_inc(*T("h_ready", h))

            def in_evac(name, l):
                def f(c, n):
                    bank = psum[bank_of(name, c, n)]
                    if c in (3, 5):
                        at = 0 if c == 3 else P
                        return dve.tensor_copy(g_v[:, :, at:at + P], bank[:, :].rearrange("p (t n) -> p t n", t=4))
                    return dve.tensor_copy(g_v[:, 2 * n:2 * n + 2, 256:512], bank[:, :].rearrange("p (t n) -> p t n", t=2))
                return f

            def y_evac(name, n_tok):
                def f(c, n):
                    return dve.tensor_copy(Y[:, 2 * c + n, 0:n_tok], psum[bank_of(name, c, n)][:, 0:n_tok])
                return f

            def attention(l):
                stage[0] = f"mix2.{l}"
                nq = T1 if l == DEPTH - 1 else T2
                qk = V["qk_g_2"]
                dve.wait_ge(*W("consts2_in", 0, at="load"))
                for n in range(4):
                    w = T2 if n == 3 else nq
                    src = g_ka if n == 3 else g_q[:, n, :]
                    dve.wait_ge(*W("mix_a", ("rms", n)))
                    step(dve.reciprocal(g_rstd[:, 0:w], g_rstd[:, 0:w]))
                    if n < 3:
                        step(dve.tensor_scalar(g_rstd[:, 0:w], g_rstd[:, 0:w], HD ** -0.5, None, ALU.mult))
                    dve.scalar_tensor_tensor(src[:, 0:w], src[:, 0:w], qk[:, 2 * l + n // 3:2 * l + n // 3 + 1], g_rstd[:, 0:w],
                                             ALU.mult, ALU.mult).then_inc(*T("mix_v", ("normed", n)))
                    dve.wait_ge(*W("product", ("rot", n)))
                    step(dve.tensor_tensor(full[0][:, 0:T1], psum[5][:, 0:T1], C2["sin2"], ALU.mult))
                    step(dve.tensor_tensor(src[:, 0:T1], src[:, 0:T1], C2["cos2"], ALU.mult))
                    dve.tensor_tensor(src[:, 0:T1], src[:, 0:T1], full[0][:, 0:T1], ALU.add).then_inc(*T("mix_v", ("roped", n)))
                dve.wait_ge(*W("evac_a", (9, 1), at=f"in{l}"))
                w = V["conv_w_2"].rearrange("p (l t n) -> p l t n", l=DEPTH, t=3)
                for n in range(2):
                    step(dve.tensor_tensor(g_cx[:, n, 0:nq], g_cx[:, n, 0:nq], g_cc[:, n, 0:nq], ALU.mult))
                    step(dve.tensor_scalar(tmp[0][:, 0:nq], g_cx[:, n, 0:nq], w[:, l, 1, n:n + 1], None, ALU.mult))
                    for s in range(nq // T1):
                        a, b = T1 * s, T1 * s + T1
                        step(dve.scalar_tensor_tensor(tmp[0][:, a + 1:b], g_cx[:, n, a:b - 1], w[:, l, 0, n:n + 1], tmp[0][:, a + 1:b], ALU.mult, ALU.add))
                        step(dve.scalar_tensor_tensor(tmp[0][:, a:b - 1], g_cx[:, n, a + 1:b], w[:, l, 2, n:n + 1], tmp[0][:, a:b - 1], ALU.mult, ALU.add))
                    dve.tensor_tensor(full[0][:, 0:nq], tmp[0][:, 0:nq], g_cb[:, n, 0:nq], ALU.mult).then_inc(*T("mix_v", ("conv", n)))
                    dve.wait_ge(*W("mix_a", ("conv", n)))
                    ins = dve.tensor_tensor(h_lo[:, 6 + n, 0:nq], full[0][:, 0:nq], h_hi[:, 6 + n, 0:nq].bitcast(F32), ALU.subtract)
                    if n == 0:
                        step(ins)
                ins.then_inc(*T("mix_v", "conv"))
                dve.wait_ge(*W("mix_v", "conv"))
                dve.wait_ge(*W("bias_in", l, at="load"))
                us = units(l)
                for u in range(len(us) + 2):
                    if u < len(us):
                        s, hd, qb = us[u]
                        k0, k1 = keys_of(s)
                        sc = psum[u % 2][:, 0:k1 - k0]
                        dve.wait_ge(*W("product", ("scores", u)))
                        if s == 0 and hd >= 6:
                            step(dve.tensor_tensor(sc[:, 0:T1], sc[:, 0:T1], g_bias[:, qb, hd - 6, :], ALU.add))
                        dve.tensor_reduce(g_st[u % 2][:, 0:1], sc, AX.X, ALU.max, negate=True).then_inc(*T("mix_v", ("max", u)))
                    if 1 <= u <= len(us):
                        v = u - 1
                        k0, k1 = keys_of(us[v][0])
                        dve.wait_ge(*W("mix_a", ("exp", v)))
                        step(dve.reciprocal(g_st[v % 2][:, 2:3], g_st[v % 2][:, 1:2]))
                        dve.tensor_scalar(g_p[v % 2][:, 0:k1 - k0], g_p[v % 2][:, 0:k1 - k0], g_st[v % 2][:, 2:3], None, ALU.mult)\
                            .then_inc(*T("mix_v", ("probs", v)))
                    if u >= 2 and (u - 2) % 2:
                        v = u - 2
                        s, hd, _ = us[v]
                        x = v // 2
                        half = slice(64 * (hd % 2), 64 * (hd % 2) + 64)
                        cut = slice(T1 * s, T1 * s + T1)
                        dve.wait_ge(*W("mix_a", ("upper", x)))
                        dve.tensor_tensor(h_lo[half, hd // 2, cut], psum[6 + x % 2][half, 0:T1], h_hi[half, hd // 2, cut].bitcast(F32),
                                          ALU.subtract).then_inc(*T("h_ready", x))

            def turn_out():
                stage[0] = "store"
                for t in range(2):
                    for q in range(2):
                        dve.wait_ge(*W("product", (t, q)))
                        ins = dve.tensor_copy(xo[:, t, 512 * q:512 * q + 512], psum[2 * t + q][:, :])
                    ins.then_inc(*T("out_tile", t))

            for s in range(SLOTS):
                dve.sem_inc(sem(f"raw_done{s}"), 1)
            for name, start in START.items():
                dve.sem_inc(sem(name), start)
            dve.memset(epsc, EPS)
            dve.memset(onec, 1.0)
            dve.memset(zeroc, 0.0)
            dve.memset(cact, 0.0)
            dve.memset(ones, 1.0).then_inc(*T_at("ones_set", 0))
            turn_in()

            def start():
                dve.wait_ge(*W("product", ("turned", ADA_START - 1)))
                mods_first(0, 2 * ADA_START, psum[4], 0)
                split_lo(0, SLOT)

            dve.wait_ge(*W("small_in", "all", at="load"))
            norm("norm0.0", T1, part1(0, 0), start)
            linear("mlstm", mlstm_evac, False)
            mlstm()
            linear("mlstm_out", residual("mlstm_out", 0, 0), True)
            norm("norm0.1", T1, part1(0, 1))
            moe(0)
            norm("norm1.0", T1, part1(1, 0))
            linear("diff", diff_evac, True)
            diff()
            linear("diff_out", residual("diff_out", 1, 0), True)
            norm("norm1.1", T1, part1(1, 1))
            moe(1)
            for l in range(DEPTH):
                both = l < DEPTH - 1
                n = T2 if both else T1
                norm(f"normffn{l}a", T2, part2(l, 0, 1))
                ffn(l, 0, True)
                post(f"post{l}.0", T2, l, 0)
                norm(f"normin{l}", T2, part2(l, 1, 1))
                linear(f"in{l}", in_evac(f"in{l}", l), True)
                attention(l)
                linear(f"attn_out{l}", y_evac(f"attn_out{l}", n), True)
                post(f"post{l}.1", n, l, 1)
                norm(f"normffn{l}b", n, part2(l, 2, both))
                ffn(l, 1, both)
                post(f"postffn{l}b", n, l, 2)
            turn_out()
    return log


def pack_columns(x):
    col = lambda v: np.asarray(v, np.float32).reshape(-1, P).T
    twice = lambda v: np.concatenate([np.asarray(v).reshape(-1, HD)] * 2, axis=1).T
    rows = lambda v: np.repeat(np.asarray(v).reshape(1, -1), P, axis=0)
    both = np.stack([np.asarray(x["c_2"]).reshape(KT, P), np.asarray(x["c_ctx_2"]).reshape(KT, P)], axis=1)
    parts = {"c1": col(x["c"]), "c2": both.reshape(2 * KT, P).T, "norm1": col(x["norm1"]), "norm2": col(x["norm2"]),
             "b_ada": col(x["b_ada"]), "a_h_norm": col(x["a_h_norm"]), "b_q_norm": twice(x["b_q_norm"]),
             "b_k_norm": twice(x["b_k_norm"]), "b_o_norm": col(x["b_o_norm"]), "b_ada_2": col(x["b_ada_2"]),
             "norm_g_2": col(x["norm_g_2"]), "qk_g_2": twice(x["qk_g_2"]), "conv_w_2": col(x["conv_w_2"]),
             "b_if": rows(x["a_b_if"]), "router_bias": rows(x["router_bias"])}
    return np.concatenate([parts[k] for k in COLS], axis=1)


def rpb_rows(rpb):
    out = np.full((DEPTH, 4, 64, 6, 4, 64), INVALID, np.float32)
    for r in range(4):
        for c in range(64):
            first = min(max(c - 8, 0), 48)
            for kr in range(4):
                out[:, r, c, :, kr, first:first + 16] = rpb[:, :, kr - r + 7, first - c + 15:first - c + 31]
    return out.reshape(DEPTH, 4, 64, 6, T1)


DIRECT = ["x", "ctx_2", "positions", "a_w_in", "a_w_out", "b_w_in", "b_w_out", "w_router",
          "b_lam_q1", "b_lam_k1", "b_lam_q2", "b_lam_k2", "moe_w_gu", "moe_w_down", "w_in_2", "w_o_2",
          "ffn_wi_2", "ffn_wo_2"]


def mod_weights(x):
    return {"w_ada_first": np.ascontiguousarray(x["w_ada"][0]),
            "w_mods": np.concatenate([x["w_ada"][1], x["w_ada_2"][0], x["w_ada_2"][1]], axis=1)}


def kernel(**inputs):
    import concourse.bacc as bacc
    from concourse.bass_utils import run_bass_kernel_spmd

    x = {k: np.asarray(v) for k, v in inputs.items()}
    arrays = {k: np.ascontiguousarray(x[k]) for k in DIRECT}
    arrays["consts"], arrays["consts2"] = host_consts()
    arrays["columns"] = np.ascontiguousarray(pack_columns(x))
    arrays["rpb_rows"] = rpb_rows(x["rpb_2"])
    arrays.update(mod_weights(x))

    def program(notes):
        nc = bacc.Bacc("TRN2", target_bir_lowering=False, num_devices=1)
        args = {k: nc.dram_tensor(f"in_{k}", a.shape, mybir.dt.from_np(a.dtype), kind="ExternalInput").ap()
                for k, a in arrays.items()}
        out = nc.dram_tensor("out_0", (1, T1, D), F32, kind="ExternalOutput").ap()
        return nc, build(nc, args, out, notes)

    _, notes = program(None)
    nc, _ = program(notes)
    r = run_bass_kernel_spmd(nc, [{f"in_{k}": a for k, a in arrays.items()}], core_ids=[0])
    return r.results[0]["out_0"]
```

```python
import math
from contextlib import ExitStack

import numpy as np

import concourse.bass as bass
from concourse import mybir

F32 = mybir.dt.float32
F32R = mybir.dt.float32r
I32 = mybir.dt.int32
U32 = mybir.dt.uint32
ALU = mybir.AluOpType
ACT = mybir.ActivationFunctionType
AX = mybir.AxisListType
ds = bass.ds

P = 128
D = 1024
KT = D // P
T1 = 256
T2 = 512
DEPTH = 2
EPS = 1e-6
A_HEADS, A_QK, A_V = 4, 128, 256
B_HEADS, B_HD = 8, 64
N_EXP, N_GRP, E_GRP = 16, 4, 4
D_EXP = 512
FFN = 2816
FFN_TILES = FFN // P
HALF = FFN_TILES // 2
NMOD2 = 9
HD = 64
LAT_HEADS = 12
SLOTS = 6
SLOT = 2048
LAM_INIT = 0.8 - 0.6 * math.exp(-0.3 * 1)
INVALID = -1e30

COLS = {}
_at = 0
for _name, _n in (("c1", 8), ("c2", 16), ("norm1", 16), ("norm2", 16), ("b_ada", 96), ("a_h_norm", 8),
                  ("b_q_norm", 1), ("b_k_norm", 1), ("b_o_norm", 1), ("b_ada_2", 144),
                  ("norm_g_2", 96), ("qk_g_2", 4), ("conv_w_2", 12), ("b_if", 8), ("router_bias", 16)):
    COLS[_name] = (_at, _n)
    _at += _n
NCOLS = _at

CONST = {}
_at = 0
for _name, _n in (("ident", 128), ("block_ones", 128), ("row_of", 3), ("upper", 128), ("rope1", 128), ("causal", 128),
                  ("iota16", 16), ("iota8", 8), ("invfreq", 1)):
    CONST[_name] = (_at, _n)
    _at += _n
NCONST = _at
KEPT = CONST["upper"][0]
CONST2 = {"rope2": (0, 128), "dup0": (128, 128), "dup1": (256, 128), "cos2": (384, 256), "sin2": (640, 256)}
NCONST2 = 896


START = {"ada_col": 1, "ada_done": 3, "gated": 4}


class Log:

    def __init__(self, notes=None):
        self.notes = notes
        self.count, self.marks, self.loops = dict(START), {}, {}
        self.loop = None

    def enter(self, name, i, turns):
        self.loop, self.before = (name, i), dict(self.count)
        self.loops.setdefault(name, {"turns": turns, "per": {}})

    def leave(self):
        rec = self.loops[self.loop[0]]
        for k, v in self.count.items():
            if per := v - self.before.get(k, 0):
                rec["per"][k] = per
                self.count[k] = self.before.get(k, 0) + per * rec["turns"]
        self.loop = None

    def raised(self, sem, key, by):
        self.count[sem] = self.count.get(sem, 0) + by
        if key is not None:
            self.marks[(sem, key)] = (self.loop and self.loop[0], self.count[sem])

    def value(self, sem, key, loop, back):
        if self.notes is None:
            return 1
        at, v = self.notes.marks[(sem, key)]
        if at is None:
            return v
        rec = self.notes.loops[at]
        per = rec["per"][sem]
        if loop and loop[0] == at:
            return loop[1] * per + (v - back * per)
        return v + (rec["turns"] - 1) * per


def host_consts():
    c = np.zeros((P, NCONST), np.float32)
    p = np.arange(P)
    put = lambda n, a: c.__setitem__((slice(None), slice(CONST[n][0], CONST[n][0] + CONST[n][1])), a)
    put("ident", np.eye(P))
    put("block_ones", (p[:, None] // 64 == p[None, :] // 64))
    put("row_of", (p[:, None] % 32 == np.arange(3)[None, :]))
    put("upper", (p[:, None] <= p[None, :]))
    put("causal", np.where(p[:, None] >= p[None, :], 0.0, INVALID))
    r = np.zeros((P, P))
    freq = np.zeros((P, 1))
    inv = (500000.0 ** (-np.arange(0, 16, 2, dtype=np.float32) / np.float32(16))).astype(np.float32)
    for h in range(2):
        for d in range(8):
            r[64 * h + d + 8, 64 * h + d] = -1
            r[64 * h + d, 64 * h + d + 8] = 1
            freq[64 * h + d] = freq[64 * h + d + 8] = inv[d]
    put("rope1", r)
    put("invfreq", freq)
    put("iota16", np.arange(16)[None, :])
    put("iota8", np.arange(8)[None, :])
    c2 = np.zeros((P, NCONST2), np.float32)
    r = np.zeros((P, P))
    cos, sin = np.zeros((P, T1), np.float32), np.zeros((P, T1), np.float32)
    f = (1.0 / (np.float32(10000.0) ** (np.arange(16, dtype=np.float32) / np.float32(16)))).astype(np.float32)
    pos = np.arange(T1)
    for q in range(P):
        axis, part, i = (q % 64) // 32, (q % 32) // 16, q % 16
        ang = ((pos // 64) if axis == 0 else (pos % 64)).astype(np.float32) * f[i]
        cos[q], sin[q] = np.cos(ang), np.sin(ang)
        if part == 0:
            r[q + 16, q] = -1
        else:
            r[q - 16, q] = 1
    c2[:, 0:128] = r
    c2[:, 128:256] = (p[:, None] == p[None, :] % 64)
    c2[:, 256:384] = (p[:, None] == 64 + p[None, :] % 64)
    c2[:, 384:640], c2[:, 640:896] = cos, sin
    return c, c2


def build(nc, A, out, notes=None):
    log = Log(notes)
    with ExitStack() as ctx:
        sems = {}

        def sem(name):
            if name not in sems:
                sems[name] = ctx.enter_context(nc.semaphore(name))
            return sems[name]

        stage = [""]

        def T(name, key=None, by=1, stage_of=None):
            log.raised(name, (stage_of or stage[0], key) if key is not None else None, by)
            return sem(name), by

        def W(name, key, at=None, back=0):
            return sem(name), log.value(name, (at or stage[0], key), log.loop, back)

        def T_at(name, key):
            log.raised(name, ("load", key), 1)
            return sem(name), 1

        top = [16544]

        def region(nbytes):
            at = top[0]
            top[0] += nbytes
            return at

        def sb(name, shape, dt, at):
            return nc.alloc_sbuf_tensor_at(name, shape, dt, offset=at)[:]

        def take(at):
            pos = [at]

            def f(name, shape, dt=F32):
                t = sb(name, shape, dt, pos[0])
                pos[0] += -(-4 * int(np.prod(shape[1:])) // 32) * 32
                return t
            f.pos = pos
            return f

        raw_at = region(SLOTS * SLOT * 4)
        raw = [sb(f"raw{s}", [P, SLOT], F32, raw_at + s * SLOT * 4) for s in range(SLOTS)]
        split_at = region(4 * SLOT * 4)
        w_hi = [sb(f"w_hi{b}", [P, SLOT], F32R, split_at + 2 * b * SLOT * 4) for b in range(2)]
        w_lo = [sb(f"w_lo{b}", [P, SLOT], F32R, split_at + (2 * b + 1) * SLOT * 4) for b in range(2)]
        X = sb("x_resid", [P, KT, T2], F32, region(KT * T2 * 4))
        h_at = region(2 * KT * T2 * 4)
        h_hi = sb("h_hi", [P, KT, T2], F32R, h_at)
        h_lo = sb("h_lo", [P, KT, T2], F32R, h_at + KT * T2 * 4)
        squares = sb("squares", [P, KT, T2], F32, h_at + KT * T2 * 4)
        a_at = region(2 * HALF * T2 * 4)
        squares_a = sb("squares_a", [P, KT, T2], F32, a_at)
        y_at = region(KT * T2 * 4)
        Y = sb("y_out", [P, KT, T2], F32, y_at)
        act_hi = sb("act_hi", [P, HALF, T2], F32R, a_at)
        act_lo = sb("act_lo", [P, HALF, T2], F32R, a_at + HALF * T2 * 4)

        cst = take(region(0))
        consts_a = cst("consts_a", [P, KEPT])
        b_at = cst.pos[0]
        consts_b = cst("consts_b", [P, NCONST - KEPT])
        w_router = cst("w_router_sb", [P, KT, N_EXP])
        cst.pos[0] = max(cst.pos[0], b_at + 4 * NCONST2)
        consts2 = sb("consts2", [P, NCONST2], F32, b_at)
        C = {k: (consts_a[:, a:a + n] if a < KEPT else consts_b[:, a - KEPT:a - KEPT + n]) for k, (a, n) in CONST.items()}
        C2 = {k: consts2[:, a:a + n] for k, (a, n) in CONST2.items()}
        cols_ = cst("cols", [P, NCOLS])
        V = {k: cols_[:, a:a + n] for k, (a, n) in COLS.items()}
        ones = cst("ones", [P, P])
        ident = C["ident"]
        epsc = cst("epsc", [P, 1])
        onec = cst("onec", [P, 1])
        zeroc = cst("zeroc", [P, 1])
        epsq, epso = cst("epsq", [P, 1]), cst("epso", [P, 1])
        rms8, inv8 = cst("rms8", [P, 16]), cst("inv8", [P, 16])
        rms4, inv4, warm = cst("rms4", [P, 4]), cst("inv4", [P, 4]), cst("warm", [P, 4])
        mod_first = cst("mod_first", [P, 48])
        mod_all = cst("mod_all", [P, 48 + DEPTH * NMOD2 * KT, 3])
        mod1 = [mod_first, mod_all[:, 0:48, 0]]
        mod2 = mod_all[:, 48:, 1:3].rearrange("p (l m k) s -> p l m k s", l=DEPTH, m=NMOD2)
        pre1 = cst("pre1", [P, DEPTH, 2, KT])
        pre2 = cst("pre2", [P, DEPTH, 3, KT, 2])
        post2 = cst("post2", [P, DEPTH, 3, KT, 2])
        cact = cst("cact", [P, KT, 32])
        small = cst("small", [P, 16])
        tmp_at = cst.pos[0]
        tmp = [cst(f"tmp{i}", [P, T2]) for i in range(2)]
        full = [cst(f"full{i}", [P, T2]) for i in range(2)]
        assert cst.pos[0] <= 229344, cst.pos[0]
        psum = [ctx.enter_context(nc.psum_tensor(f"bank{b}", [P, 512], F32)) for b in range(8)]

        at0 = take(a_at)
        xt = at0("x_tokens", [P, 4, D])
        ada_row0 = sb("ada_row0", [P, 2, 256], F32, h_at)
        m = take(a_at)
        m_q, m_k = m("m_q", [P, A_HEADS, T1]), m("m_k", [P, A_HEADS, T1])
        m_v, m_og = m("m_v", [P, 2, A_HEADS * A_V]), m("m_og", [P, KT, T1])
        w_gate = m("w_gate", [P, KT, 2 * A_HEADS])
        m_g, m_lf, m_u, m_b, m_a = (m(n, [P, 2, 2 * A_HEADS if n == "m_g" else A_HEADS])
                                    for n in ("m_g", "m_lf", "m_u", "m_b", "m_a"))
        m_rows, m_arow = m("m_rows", [A_HEADS, 512]), m("m_arow", [A_HEADS, T1])
        m_d, m_p, m_hh, m_em, m_dn = (m("m_d", [P, 384]), m("m_p", [P, 384]), m("m_hh", [P, KT, T1]),
                                      m("m_em", [P, 2, T1]), m("m_dn", [P, T1]))
        ada_row1 = m("ada_row1", [P, 2, 256])
        assert m.pos[0] <= y_at + KT * T2 * 4
        d = take(a_at)
        d_q, d_k = d("d_q", [P, B_HEADS, T1]), d("d_k", [P, B_HEADS, T1])
        d_v = d("d_v", [P, 2, D])
        d_p = [d(f"d_p{i}", [P, 2, T1]) for i in range(3)]
        d_st = [d(f"d_st{i}", [P, 8]) for i in range(2)]
        d_at = [d(f"d_at{i}", [P, 2, T1]) for i in range(2)]
        d_osq = [d(f"d_osq{n}", [P, T2]) for n in range(4)]
        tables_at = y_at + 4 * KT * T2 - 6400
        dt = take(tables_at)
        d_cos, d_sin = dt("d_cos", [P, T1]), dt("d_sin", [P, T1])
        d_ang, d_n = dt("d_ang", [P, T1]), dt("d_n", [P, T1])
        d_pos = dt("d_pos", [P, T1], I32)
        d_lam = dt("d_lam", [P, 4, B_HD])
        d_ls = dt("d_ls", [P, 8])
        assert dt.pos[0] <= y_at + 4 * KT * T2 and max(m.pos[0], d.pos[0]) <= tables_at
        e = take(a_at)
        e_hi, e_lo = e("e_hi", [P, 4, T1], F32R), e("e_lo", [P, 4, T1], F32R)
        e_gate = e("e_gate", [P, N_EXP, T1])
        e_s, e_b, e_m, e_w = (e(n, [P, 2, N_EXP]) for n in ("e_s", "e_b", "e_m", "e_w"))
        e_pair, e_g8, e_x8 = e("e_pair", [P, N_GRP, 6]), e("e_g8", [P, 8]), e("e_x8", [P, 8])
        e_i8 = e("e_i8", [P, 8], U32)
        e_f8, e_oh = e("e_f8", [P, 8]), e("e_oh", [P, 8])
        e_row = e("e_row", [N_EXP, T1])
        e_zero = e("e_zero", [P, T2], F32R)
        ada_raw = [e(f"ada_raw{x}", [P, KT, 256]) for x in range(3)]
        ada_row2 = e("ada_row2", [P, 256])
        assert e.pos[0] <= tables_at
        g = take(a_at)
        g_q, g_kb = g("g_q", [P, 6, T2]), g("g_kb", [P, 3, T2])
        g_ka, g_kd = g("g_ka", [P, T2]), g("g_kd", [P, 2, T2])
        g_v = g("g_v", [P, 4, 512])
        g_cx, g_cb, g_cc = (g(n, [P, 2, T2]) for n in ("g_cx", "g_cb", "g_cc"))
        assert g.pos[0] <= y_at
        g = take(y_at)
        g_bias = g("g_bias", [P, 2, 6, T1])
        g_tap = g("g_tap", [P, T2])
        assert g.pos[0] <= y_at + KT * T2 * 4
        quad = tmp + full
        g_p = [sb(f"g_p{i}", [P, 2, T2], F32, split_at + (2 * SLOT + 2 * T2 * i) * 4) for i in range(3)]
        g_pt = [sb(f"g_pt{i}", [P, 2, 4, P], F32, tmp_at + i * 4096) for i in range(2)]
        xo = sb("x_out", [P, 2, D], F32, a_at)
        g_st = [small[:, 8 * i:8 * i + 8] for i in range(2)]

        block = ctx.enter_context(nc.Block())

        class Stream:

            def __init__(self):
                self.slot, self.all, self.loop = [0] * SLOTS, 0, None

            def enter(self, i, chunks):
                self.loop = (i, chunks, [len(range(s, chunks, SLOTS)) for s in range(SLOTS)])

            def leave(self, turns):
                _, chunks, per = self.loop
                self.loop = None
                self.all += (turns - 1) * chunks
                self.slot = [n + (turns - 1) * k for n, k in zip(self.slot, per)]

            def next(self, s, split=1):
                self.slot[s] += 1
                self.all += split
                if self.loop is None:
                    return self.slot[s], self.all
                i, chunks, per = self.loop
                return i * per[s] + self.slot[s], i * chunks + self.all

        def w3(ap, k):
            return ap.rearrange("p (k n) -> p k n", k=k)

        def tt(*which, n):
            return [("T", P * x, n) for x in which]

        ITEMS = {"mlstm": [tt(0, 1, n=T1)] * 4 + [[("V", 0, 256, (0, 1))]] * 4 + [tt(0, 1, n=T1)] * 4,
                 "mlstm_out": [tt(0, 1, n=T1)] * 4,
                 "diff": [tt(0, 1, n=T1)] * 8 + [[("V", 0, 256, (0, 1))]] * 4,
                 "diff_out": [tt(0, 1, n=T1)] * 4}
        for l in range(DEPTH):
            n = T1 if l == DEPTH - 1 else T2
            ITEMS[f"in{l}"] = [tt(0, 1, n=n)] * 3 + [tt(0, n=T2) + [("V", 128, 128, (0, 1, 2, 3))], tt(0, 1, n=T2),
                               tt(0, n=T2) + [("V", 128, 128, (0, 1, 2, 3))],
                               [("V", 0, 256, (0, 1)), ("V", 0, 256, (2, 3))]] + [tt(0, 1, n=n)] * 3
            ITEMS[f"attn_out{l}"] = [tt(0, 1, n=n)] * 4

        def in_evac_by(c, n):
            return "evac_v" if (c, n) in ((3, 1), (5, 1)) or c == 6 else "evac_a"

        EVAC = {"mlstm": lambda c, n: "evac_v" if 4 <= c < 8 else "evac_a",
                "diff": lambda c, n: "evac_v" if c >= 8 else "evac_a",
                "mlstm_out": lambda c, n: "evac_v", "diff_out": lambda c, n: "evac_v",
                "in0": in_evac_by, "in1": in_evac_by,
                "attn_out0": lambda c, n: "evac_v", "attn_out1": lambda c, n: "evac_v"}
        UP_BANK = (0, 1, 2, 0)

        def bank_of(name, c, n):
            return (sum(len(x) for x in ITEMS[name][:c]) + n) % 4

        def x_key(at, j):
            return ("evac_v", (j // 2, j % 2), at) if at.endswith("_out") else ("x_ready", j, at)

        def y_key(post, j):
            if post.endswith(".1"):
                return "evac_v", (j // 2, j % 2), f"attn_out{post[4]}"
            name = f"ffn{post[4]}a" if post.endswith(".0") else post[4:]
            return "y_ready", ("g1", j), name

        MADE_BY = {"mlstm_out": "norm0.1", "diff_out": "norm1.1", "attn_out0": "post0.1", "attn_out1": "post1.1"}
        MADE_BY |= {f"ffn{l}a": f"post{l}.0" for l in range(DEPTH)} | {f"ffn{l}b": f"postffn{l}b" for l in range(DEPTH)}
        LINEAR_MADE = [v for k, v in MADE_BY.items() if k.endswith("_out") or k.startswith("attn")]
        squares_of = lambda name: squares_a if name in LINEAR_MADE else squares
        sums_bank = lambda name: psum[4] if name in LINEAR_MADE else psum[3]
        SQUARED = {v: 6 if v in LINEAR_MADE else KT - 1 for v in MADE_BY.values()}
        SUMMED = {v: 4 if v in LINEAR_MADE else KT - 2 for v in MADE_BY.values()}

        ADA_START, ADA_MIX = 8, 16
        EXP_CH, FFN_CH, FFN_UP = 6, HALF + KT, HALF
        DOWN = HALF * P
        LAST = f"ffn{DEPTH - 1}b"

        def ffn_chunk(at):
            return f"g{at // FFN_CH}", at % FFN_CH

        part1 = lambda l, w: [(0, T1, lambda j: pre1[:, l, w, j:j + 1], lambda j: mod1[l][:, 24 * w + j:24 * w + j + 1])]
        part2 = lambda l, i, both: [(T1 * s, T1 * s + T1, lambda j, s=s: pre2[:, l, i, j, s:s + 1],
                                     lambda j, s=s: mod2[:, l, 3 * i, j, s:s + 1]) for s in range(1 + both)]

        def last_item(name, c):
            return c, len(ITEMS[name][c]) - 1

        def units(l):
            return [(s, pair, qb) for s in range(1 if l == DEPTH - 1 else 2) for pair in range(LAT_HEADS // 2)
                    for qb in range(2)]

        def head_norms(name):
            if name == "diff":
                flat = lambda x: x.rearrange("p a t -> p (a t)")
                return [(flat((d_q if n < 4 else d_k)[:, 2 * (n % 4):2 * (n % 4) + 2, :]), (n, 1),
                         V["b_q_norm" if n < 4 else "b_k_norm"], n < 4, T2) for n in range(8)]
            l = int(name[2])
            nq = T1 if l == DEPTH - 1 else T2
            qk = V["qk_g_2"]
            return [(g_q[:, n, 0:nq], (n // 2, n % 2), qk[:, 2 * l:2 * l + 1], True, T1) for n in range(3)] + \
                [(g_ka, (3, 0), qk[:, 2 * l + 1:2 * l + 2], False, T1)]

        last_head = {"mix0": A_HEADS - 1, "mix1": B_HEADS - 1} | {f"mix2.{l}": len(units(l)) - 1 for l in range(DEPTH)}

        def keys_of(s):
            return (0, T2) if s == 0 else (T1, T2)

        @block.sync
        def _(sp):
            st = Stream()

            def load(c, src, k):
                s = c % SLOTS
                used, _ = st.next(s)
                dst = w3(raw[s], k) if k * (SLOT // k) == SLOT else w3(raw[s][:, 0:DOWN], k)
                sp.wait_ge(sem(f"raw_done{s}"), used)
                sp.dma_start(dst, src).then_inc(sem(f"raw_full{s}"), 16)

            def linear(name, W2d):
                v = W2d.rearrange("(k p) n -> p k n", p=P)
                for c in range(len(ITEMS[name])):
                    load(c, v[:, :, 256 * c:256 * c + 256], KT)

            def ada(first, chunks):
                v = A["w_ada_first"].rearrange("(k p) n -> p k n", p=P)
                for c in range(chunks):
                    load(c, v[:, :, 256 * (first + c):256 * (first + c) + 256], KT)

            def moe(l):
                gu = A["moe_w_gu"][l].rearrange("e (k p) (g c n) -> e p g k c n", p=P, g=2, c=4)
                dn = A["moe_w_down"][l].rearrange("e (k p) n -> e p k n", p=P)
                ada_w = A["w_mods"].rearrange("(k p) n -> p k n", p=P)
                stage[0] = f"moe{l}"
                with sp.Fori(0, N_EXP) as i:
                    st.enter(i, EXP_CH)
                    log.enter(f"moe{l}", i, N_EXP)
                    for c in range(4):
                        s = c
                        used, _ = st.next(s)
                        dst = raw[s].rearrange("p (g k n) -> p g k n", g=2, k=KT)
                        sp.wait_ge(sem(f"raw_done{s}"), used)
                        sp.dma_start(dst, gu[i, :, :, :, c, :]).then_inc(sem(f"raw_full{s}"), 16)
                        if c < 3:
                            if c == 0:
                                sp.wait_ge(*W("h_ready", last_head[f"mix{l}"], at=f"mix{l}"))
                            sp.wait_ge(*W("ada_done", c, back=1))
                            sp.dma_start(ada_raw[c], ada_w[:, :, ds(i * 768 + (N_EXP * 768 * l + c * 256), 256)])\
                                .then_inc(*T(f"ada_full{c}", 0, 16))
                    for c in range(4, 6):
                        load(c, dn[i, :, :, 512 * (c - 4):512 * (c - 3)], 4)
                    log.leave()
                st.leave(N_EXP)

            def ffn(l, which):
                wi = A["ffn_wi_2"][l, which].rearrange("(k p) (g c n) -> p g k c n", p=P, g=2, c=FFN_TILES)
                wo = A["ffn_wo_2"][l, which].rearrange("(t f p) n -> p t f n", t=2, p=P)

                for at in range(2 * FFN_CH):
                    t, c = divmod(at, FFN_CH)
                    if c < FFN_UP:
                        s = at % SLOTS
                        used, _ = st.next(s)
                        dst = raw[s].rearrange("p (g k n) -> p g k n", g=2, k=KT)
                        sp.wait_ge(sem(f"raw_done{s}"), used)
                        sp.dma_start(dst, wi[:, :, :, t * HALF + c, :]).then_inc(sem(f"raw_full{s}"), 16)
                    else:
                        load(at, wo[:, t, :, P * (c - FFN_UP):P * (c - FFN_UP) + P], HALF)

            stage[0] = "load"
            sp.dma_start(consts_a, A["consts"][:, 0:KEPT]).then_inc(*T("small_in", "ident", 16))
            sp.dma_start(consts_b, A["consts"][:, KEPT:NCONST]).then_inc(*T("small_in", "consts", 16))
            sp.dma_start(cols_, A["columns"]).then_inc(*T("small_in", "cols", 16))
            sp.dma_start(w_router, A["w_router"].rearrange("(k p) n -> p k n", p=P)).then_inc(*T("small_in", "all", 16))
            ada(0, ADA_START)
            linear("mlstm", A["a_w_in"][0])
            ada(ADA_START, ADA_MIX)
            linear("mlstm_out", A["a_w_out"][0])
            moe(0)
            linear("diff", A["b_w_in"][0])
            linear("diff_out", A["b_w_out"][0])
            moe(1)
            for l in range(DEPTH):
                ffn(l, 0)
                linear(f"in{l}", A["w_in_2"][l])
                linear(f"attn_out{l}", A["w_o_2"][l])
                ffn(l, 1)

        @block.gpsimd
        def _(pool):
            def step(ins):
                ins.then_inc(*T("pool_step"))
                pool.wait_ge(sem("pool_step"), log.count["pool_step"])

            stage[0] = "load"
            pool.dma_start(xt[:, 0:2, :], A["x"][0].rearrange("(t p) d -> p t d", p=P)).then_inc(*T("tokens_in", "x", 16))
            pool.dma_start(xt[:, 2:4, :], A["ctx_2"][0].rearrange("(t p) d -> p t d", p=P)).then_inc(*T("tokens_in", "all", 16))
            pool.dma_start(d_pos, A["positions"].broadcast_to([P, T1])).then_inc(*T("diff_in", "pos", 16))
            for n, name in enumerate(("b_lam_q1", "b_lam_k1", "b_lam_q2", "b_lam_k2")):
                pool.dma_start(d_lam[:, n, :], A[name].broadcast_to([P, B_HD])).then_inc(*T("diff_in", "all", 16))
            pool.wait_ge(*W("x_ready", KT - 1, at="turn_in"))
            pool.dma_start(w_gate, A["a_w_in"][0].rearrange("(k p) n -> p k n", p=P)[:, :, 3072:3080])\
                .then_inc(*T("gate_in", 0, 16))
            pool.wait_ge(*W("x_ready", KT - 1, at="moe1"))
            pool.dma_start(consts2, A["consts2"]).then_inc(*T("consts2_in", 0, 16))
            for l in range(DEPTH):
                pool.wait_ge(*W("x_ready", KT - 1, at=f"post{l}.0"))
                for r in range(4):
                    pool.dma_start(g_bias[64 * (r % 2):64 * (r % 2) + 64, r // 2, :, :],
                                   A["rpb_rows"][l, r]).then_inc(*T("bias_in", l, 16))
                stage[0] = f"mix2.{l}"
                nq = T1 if l == DEPTH - 1 else T2
                w = V["conv_w_2"].rearrange("p (l t n) -> p l t n", l=DEPTH, t=3)
                pool.wait_ge(*W("evac_a", (9, 1), at=f"in{l}"))
                for n in range(2):
                    z, out_ = g_cx[:, n, 0:nq], g_cc[:, n, 0:nq]
                    step(pool.tensor_tensor(z, z, g_cc[:, n, 0:nq], ALU.mult))
                    step(pool.tensor_scalar(out_, z, w[:, l, 1, n:n + 1], None, ALU.mult))
                    for tap in (0, 2):
                        step(pool.tensor_scalar(g_tap[:, 0:nq], z, w[:, l, tap, n:n + 1], None, ALU.mult))
                        for s in range(nq // T1):
                            to, of = T1 * s + (tap == 0), T1 * s + (tap == 2)
                            ins = pool.tensor_tensor(g_cc[:, n, to:to + T1 - 1], g_cc[:, n, to:to + T1 - 1],
                                                     g_tap[:, of:of + T1 - 1], ALU.add)
                        step(ins)
                    pool.tensor_tensor(g_cb[:, n, 0:nq], out_, g_cb[:, n, 0:nq], ALU.mult).then_inc(*T("conv", n))
                    pool.wait_ge(*W("conv_upper", n))
                    pool.tensor_tensor(h_lo[:, 6 + n, 0:nq], g_cb[:, n, 0:nq], h_hi[:, 6 + n, 0:nq].bitcast(F32),
                                       ALU.subtract).then_inc(*T("conv_ready", n))
                stage[0] = "load"
            stage[0] = "store"
            for t in range(2):
                pool.wait_ge(*W("out_tile", t))
                pool.dma_start(out[0, P * t:P * t + P, :], xo[:, t, :]).then_inc(*T("stored", t, 16))
            pool.wait_ge(*W("stored", 1))

        @block.tensor
        def _(pe):
            st = Stream()
            bank_user = {}

            def bank_ready(b):
                if b in bank_user:
                    pe.wait_ge(*W(*bank_user[b][0], **bank_user[b][1]))

            def ada_rows(w, bank):
                for k in range(KT):
                    g = slice(32 * (k % 4), 32 * (k % 4) + 32)
                    mm = pe.matmul(bank[g, 0:256], cact[:, k, :], w[:, k, :], start=(k < 4), stop=(k >= 4))
                return mm

            def ada_turn(dst, row, n):
                for q in range(2):
                    mm = pe.matmul(dst[:, n * q:n * q + n], row[:, P * q:P * q + P], C["row_of"][:, 0:n], start=True, stop=True)
                return mm

            def ada(c, chunks, banks, cols, row):
                if c < chunks:
                    used, _ = st.next(c % SLOTS, 0)
                    pe.wait_ge(sem(f"raw_full{c % SLOTS}"), used * 16)
                    ada_rows(w3(raw[c % SLOTS], KT), banks[c % 2]).then_inc(sem(f"raw_done{c % SLOTS}"), 1)
                if c:
                    pe.wait_ge(*W("ada_row", c - 1))
                    ada_turn(cols[:, 2 * c - 2:2 * c], row[:, (c - 1) % 2, :], 1).then_inc(*T("product", ("turned", c - 1)))

            def turn_in():
                stage[0] = "turn_in"
                pe.wait_ge(*W("tokens_in", "all", at="load"))
                for j in range(KT):
                    for t in range(4):
                        mm = pe.transpose(psum[j][:, P * t:P * t + P], xt[:, t, P * j:P * j + P], ident)
                    mm.then_inc(*T("product", j))

            def sum_tile(name, j, n):
                pe.wait_ge(*W("squared", j, at=name))
                bank = sums_bank(name)
                if j == 0:
                    pe.matmul(bank[:, 0:n // P], zeroc[0:1, 0:1].broadcast_to([1, P]), ones[0:1, 0:n // P],
                              start=True, stop=False, skip_group_check=True)
                for t in range(n // P):
                    mm = pe.matmul(bank[:, t:t + 1], squares_of(name)[:, j, P * t:P * t + P], ones[:, 0:1],
                                   start=False, stop=False, skip_group_check=True)
                return mm

            def sum_squares(name, n):
                stage[0] = name
                nt = n // P
                for j in range(SUMMED.get(name, 0), KT):
                    mm = sum_tile(name, j, n)
                mm.then_inc(*T("product", "squares"))
                pe.wait_ge(*W("inverse", 0))
                for t in range(nt):
                    mm = pe.matmul(psum[7][:, P * t:P * t + P], inv4[:, t:t + 1].broadcast_to([P, P]), ident,
                                   start=True, stop=True)
                mm.then_inc(*T("product", "rstd"))

            def linear(name, source, per_tile=True, after=None):
                stage[0] = name
                for c, items in enumerate(ITEMS[name]):
                    used, _ = st.next(c % SLOTS)
                    pe.wait_ge(sem(f"raw_done{c % SLOTS}"), used + 1)
                    hi, lo = w3(w_hi[c % 2], KT), w3(w_lo[c % 2], KT)

                    def steps(n, it):
                        b = psum[bank_of(name, c, n)]
                        for where, t in ([(slice(0, it[2]), None)] if it[0] == "T" else
                                         [(slice(it[2] * x, it[2] * x + it[2]), t) for x, t in enumerate(it[3])]):
                            for k in range(KT):
                                if t is None:
                                    cut = slice(it[1], it[1] + P)
                                    trio = [(hi[:, k, cut], h_hi[:, k, 0:it[2]]), (hi[:, k, cut], h_lo[:, k, 0:it[2]]),
                                            (lo[:, k, cut], h_hi[:, k, 0:it[2]])]
                                else:
                                    cut, tok = slice(it[1], it[1] + it[2]), slice(P * t, P * t + P)
                                    trio = [(h_hi[:, k, tok], hi[:, k, cut]), (h_hi[:, k, tok], lo[:, k, cut]),
                                            (h_lo[:, k, tok], hi[:, k, cut])]
                                for x, (l_, r_) in enumerate(trio):
                                    mm = pe.matmul(b[:, where], l_, r_, start=(k == 0 and x == 0),
                                                   stop=(k == KT - 1 and x == 2))
                                yield mm

                    if c == 0:
                        for n in range(len(items)):
                            bank_ready(bank_of(name, c, n))
                        rows = [steps(n, it) for n, it in enumerate(items)]
                        for k in range(KT):
                            pe.wait_ge(*W("h_ready", k if per_tile else last_head[source], at=source))
                            last = [next(r) for r in rows]
                        for n, mm in enumerate(last):
                            mm.then_inc(*T("product", (c, n)))
                    else:
                        for n, it in enumerate(items):
                            bank_ready(bank_of(name, c, n))
                            for mm in steps(n, it):
                                pass
                            mm.then_inc(*T("product", (c, n)))
                    for n in range(len(items)):
                        bank_user[bank_of(name, c, n)] = ((EVAC[name](c, n), (c, n)), {"at": name})
                    if after:
                        after(c)
                    if name in MADE_BY and c >= 2:
                        for j in (2 * c - 4, 2 * c - 3):
                            sum_tile(MADE_BY[name], j, items[0][2])

            def head_pipe(name):
                work = head_norms(name)
                if name != "diff":
                    pe.wait_ge(*W("consts2_in", 0, at="load"))
                rope = C["rope1"] if name == "diff" else C2["rope2"]

                def after(c):
                    if 0 <= (n := c - 3) < len(work):
                        x, _, _, _, turned = work[n]
                        pe.wait_ge(*W("mix_v", ("normed", n)))
                        if n:
                            pe.wait_ge(*W("mix_v", ("roped", n - 1)))
                        pe.matmul(psum[6][:, 0:turned], rope, x[:, 0:turned], start=True, stop=True)\
                            .then_inc(*T("product", ("rot", n)))
                    if 0 <= (n := c - 2) < len(work):
                        pe.wait_ge(*W("mix_v", ("inverse", n)))
                        for b in range(work[n][0].shape[1] // P):
                            for x in range(2):
                                mm = pe.matmul(psum[5][HD * x:HD * x + HD, P * b:P * b + P],
                                               inv8[:, 2 * b + x:2 * b + x + 1].broadcast_to([P, HD]), ident, start=True, stop=True)
                        mm.then_inc(*T("product", ("bcast", n)))
                    if 0 <= (n := c - 1) < len(work):
                        pe.wait_ge(*W("mix_a", ("sq", n)))
                        for b in range(work[n][0].shape[1] // P):
                            mm = pe.matmul(psum[4][:, 2 * b:2 * b + 2], tmp[0][:, P * b:P * b + P], C["block_ones"][:, 0:P:HD],
                                           start=True, stop=True)
                        mm.then_inc(*T("product", ("sums", n)))
                    if name != "diff" and c == 7:
                        pe.wait_ge(*W("mix_v", ("roped", 3)))
                        for n, dup in enumerate(("dup0", "dup1")):
                            pe.matmul(psum[4 + n][:, :], C2[dup], g_ka, start=True, stop=True)\
                                .then_inc(*T("product", ("dup", n)))
                return after

            def moe(l):
                name = stage[0] = f"moe{l}"
                for t in range(2):
                    for k in range(KT):
                        if t == 0:
                            pe.wait_ge(*W("h_ready", k, at=f"norm{l}.1"))
                        for x, h in enumerate((h_hi, h_lo)):
                            mm = pe.matmul(psum[0][:, 16 * t:16 * t + 16], h[:, k, P * t:P * t + P].bitcast(F32),
                                           w_router[:, k, :], start=(k == 0 and x == 0), stop=(k == KT - 1 and x == 1))
                mm.then_inc(*T("product", "router"))
                pe.wait_ge(*W("gate_w", "tokens"))
                for t in range(2):
                    mm = pe.transpose(psum[0][0:N_EXP, 128 + P * t:256 + P * t], e_w[:, t, :], ident)
                mm.then_inc(*T("product", "gate_rows"))
                pe.wait_ge(*W("gate_w", "rows"))
                for x in range(N_EXP):
                    if x >= 4:
                        pe.wait_ge(*W("gate_bc", x - 4))
                    mm = pe.matmul(psum[x % 4][:, 0:T1], ident[0:N_EXP, x:x + 1].broadcast_to([N_EXP, P]), e_row,
                                   start=True, stop=True)
                    mm.then_inc(*T("product", ("bc", x)))
                pe.wait_ge(*W("gate_bc", N_EXP - 1))
                for b in range(4, 8):
                    pe.matmul(psum[b][:, :], e_zero[:, 0:P], e_zero, start=True, stop=False, skip_group_check=True)
                with pe.Fori(0, N_EXP) as i:
                    st.enter(i, EXP_CH)
                    log.enter(name, i, N_EXP)
                    for c in range(4):
                        used, _ = st.next(c)
                        hi, lo = w3(w_hi[c % 2], 2 * KT), w3(w_lo[c % 2], 2 * KT)
                        pe.wait_ge(sem(f"raw_done{c}"), used + 1)
                        if c == 3:
                            pe.wait_ge(*W("gated", 0))
                        else:
                            pe.wait_ge(*W("gated", 3 if c == 0 else c, back=1))
                        for q in range(2):
                            o = psum[UP_BANK[c]][:, T1 * q:T1 * q + T1]
                            for k in range(KT):
                                f = q * KT + k
                                pe.matmul(o, hi[:, f, :], h_hi[:, k, 0:T1], start=(k == 0), stop=False)
                                pe.matmul(o, hi[:, f, :], h_lo[:, k, 0:T1], start=False, stop=False)
                                mm = pe.matmul(o, lo[:, f, :], h_hi[:, k, 0:T1], start=False, stop=(k == KT - 1))
                        mm.then_inc(*T("product", ("up", c)))
                        if c:
                            pe.wait_ge(*W("ada_row", c - 1))
                            ada_turn(psum[3][:, T1 + 6 * c - 6:T1 + 6 * c], ada_row2, 3).then_inc(*T("product", ("turned", c - 1)))
                        if c < 3:
                            if c == 0:
                                pe.wait_ge(*W("ada_col", "col", back=1))
                            pe.wait_ge(*W(f"ada_full{c}", 0))
                            ada_rows(ada_raw[c], psum[3]).then_inc(*T("ada_done", c))
                    for c in range(4, 6):
                        used, _ = st.next(c)
                        hi, lo = w3(w_hi[c % 2], 4), w3(w_lo[c % 2], 4)
                        pe.wait_ge(sem(f"raw_done{c}"), used + 1)
                        for k in range(4):
                            if c == 4:
                                pe.wait_ge(*W("act_ready", k))
                            for m_ in range(4):
                                j = 4 * (c - 4) + m_
                                o = psum[4 + j // 2][:, T1 * (j % 2):T1 * (j % 2) + T1]
                                cut = slice(P * m_, P * m_ + P)
                                pe.matmul(o, hi[:, k, cut], e_hi[:, k, :], start=False, stop=False, skip_group_check=True)
                                pe.matmul(o, hi[:, k, cut], e_lo[:, k, :], start=False, stop=False, skip_group_check=True)
                                mm = pe.matmul(o, lo[:, k, cut], e_hi[:, k, :], start=False, stop=False, skip_group_check=True)
                        mm.then_inc(*T("product", ("down", c)))
                    log.leave()
                st.leave(N_EXP)
                bank_user.clear()

            def ffn(l, which):
                name = stage[0] = f"ffn{l}{'ab'[which]}"
                n = T1 if name == LAST else T2

                def group(tag, back, first):
                    for c in range(FFN_UP):
                        s, b = (first + c) % SLOTS, (first + c) % 2
                        used, _ = st.next(s)
                        hi, lo = w3(w_hi[b], 2 * KT), w3(w_lo[b], 2 * KT)
                        pe.wait_ge(sem(f"raw_done{s}"), used + 1)
                        if c >= 2:
                            pe.wait_ge(*W("gated", (tag, c - 2)))
                        elif back:
                            pe.wait_ge(*W("gated", (back, FFN_UP - 1 - c)))
                        order = [(q, k) for k in range(KT) for q in range(2)] if c == 0 else \
                            [(q, k) for q in range(2) for k in range(KT)]
                        for q, k in order:
                            o = psum[2 * (c % 2) + q][:, 0:n]
                            if tag == "g0" and q == 0 and c == 0:
                                pe.wait_ge(*W("h_ready", k, at=f"norm{name}"))
                            f = q * KT + k
                            pe.matmul(o, hi[:, f, :], h_hi[:, k, 0:n], start=(k == 0), stop=False)
                            pe.matmul(o, hi[:, f, :], h_lo[:, k, 0:n], start=False, stop=False)
                            mm = pe.matmul(o, lo[:, f, :], h_hi[:, k, 0:n], start=False, stop=(k == KT - 1))
                        mm.then_inc(*T("product", (tag, c)))
                    for j in range(KT):
                        c = FFN_UP + j
                        s, b = (first + c) % SLOTS, (first + c) % 2
                        used, _ = st.next(s)
                        hi, lo = w3(w_hi[b][:, 0:DOWN], HALF), w3(w_lo[b][:, 0:DOWN], HALF)
                        pe.wait_ge(sem(f"raw_done{s}"), used + 1)
                        if j >= 4:
                            pe.wait_ge(*W("y_ready", (tag, j - 4)))
                        elif back:
                            pe.wait_ge(*W("y_ready", (back, 4 + j)))
                        o = psum[4 + j % 4][:, 0:n]
                        for k in range(HALF):
                            if j == 0:
                                pe.wait_ge(*W("act_ready", (tag, k)))
                            pe.matmul(o, hi[:, k, :], act_hi[:, k, 0:n], start=(k == 0), stop=False)
                            pe.matmul(o, hi[:, k, :], act_lo[:, k, 0:n], start=False, stop=False)
                            mm = pe.matmul(o, lo[:, k, :], act_hi[:, k, 0:n], start=False, stop=(k == HALF - 1))
                        mm.then_inc(*T("product", (tag, c)))
                        if tag == "g1" and j >= 2:
                            sum_tile(MADE_BY[name], j - 2, n)

                group("g0", None, 0)
                group("g1", "g0", FFN_CH)
                bank_user.clear()

            def mlstm():
                stage[0] = "mix0"
                for b in range(4):
                    bank_ready(b)
                pe.wait_ge(*W("gate_in", 0, at="load"))
                for t in range(2):
                    for k in range(KT):
                        for x, h in enumerate((h_hi, h_lo)):
                            mm = pe.matmul(psum[4][:, 8 * t:8 * t + 8], h[:, k, P * t:P * t + P].bitcast(F32),
                                           w_gate[:, k, :], start=(k == 0 and x == 0), stop=(k == KT - 1 and x == 1))
                mm.then_inc(*T("product", "gates"))
                chunks = iter(range(ADA_MIX + 1))
                more = lambda: ada(next(chunks), ADA_MIX, psum[6:8], psum[5], ada_row1)
                more()
                pe.wait_ge(*W("gate_v", "log_f"))
                pe.matmul(psum[4][:, 16:20], C["upper"], m_lf[:, 0, :], start=True, stop=True)
                pe.matmul(psum[4][:, 20:24], C["upper"], m_lf[:, 1, :], start=True, stop=False)
                mm = pe.matmul(psum[4][:, 20:24], ones, m_lf[:, 0, :], start=False, stop=True)
                mm.then_inc(*T("product", "cum"))
                pe.wait_ge(*W("gate_v", "a"))
                for n, v in enumerate((m_a, m_b)):
                    for t in range(2):
                        mm = pe.transpose(psum[5][0:A_HEADS, T1 * n + P * t:T1 * n + P * t + P], v[:, t, :], ident)
                mm.then_inc(*T("product", "rows"))
                pe.wait_ge(*W("gate_v", "rows"))
                for _ in range(3):
                    more()
                def scores(h):
                    pe.matmul(psum[0][:, :], ident[0:A_HEADS, h:h + 1].broadcast_to([A_HEADS, P]), m_rows[0:A_HEADS, :],
                              start=True, stop=True).then_inc(*T("product", ("bc", h)))
                    pe.matmul(psum[1][:, 0:T1], m_k[:, h, 0:P], m_q[:, h, :], start=True, stop=True)
                    pe.matmul(psum[1][:, T1:T1 + P], m_k[:, h, P:T1], m_q[:, h, P:T1], start=True, stop=True)\
                        .then_inc(*T("product", ("scores", h)))

                def head_squares(h):
                    pe.wait_ge(*W("mix_a", ("squared", h)))
                    for b in range(2):
                        for q in range(2):
                            mm = pe.matmul(psum[4][:, 2 * h + b:2 * h + b + 1], quad[h][:, T1 * q + P * b:T1 * q + P * b + P],
                                           ones[:, 0:1], start=(q == 0), stop=(q == 1))
                    return mm

                scores(0)
                for h in range(A_HEADS):
                    pe.wait_ge(*W("mix_v", ("masked", h)))
                    if h + 1 < A_HEADS:
                        scores(h + 1)
                    more()
                    if h:
                        pe.wait_ge(*W("mix_v", ("normed", h - 1)))
                    for o, lhs in ((psum[2][:, 0:T1], lambda s: ones),
                                   (psum[3][:, 0:T1], lambda s: m_v[:, s, A_V * h:A_V * h + P]),
                                   (psum[3][:, T1:T2], lambda s: m_v[:, s, A_V * h + P:A_V * h + A_V])):
                        pe.matmul(o, lhs(0), m_p[:, 0:T1], start=True, stop=False)
                        mm = pe.matmul(o[:, P:T1], lhs(1), m_p[:, T1:T1 + P], start=False, stop=True)
                    mm.then_inc(*T("product", ("sums", h)))
                    more()
                    if h:
                        head_squares(h - 1)
                    more()
                head_squares(A_HEADS - 1).then_inc(*T("product", "head_sq"))
                more()
                pe.wait_ge(*W("mix_v", "inverse"))
                for h in range(A_HEADS):
                    for b in range(2):
                        at = T1 * (h % 2) + P * b
                        mm = pe.matmul(psum[h // 2][:, at:at + P], inv8[:, 2 * h + b:2 * h + b + 1].broadcast_to([P, P]), ident,
                                       start=True, stop=True)
                mm.then_inc(*T("product", "head_inv"))
                bank_user.clear()

            def diff():
                stage[0] = "mix1"
                pe.wait_ge(*W("mix_v", ("roped", 7), at="diff"))
                for b in range(4):
                    bank_ready(b)
                U = 2 * B_HEADS
                for u in range(U + 3):
                    if u < U:
                        h, qb = u // 2, u % 2
                        keys = P * (qb + 1)
                        if u >= 2:
                            pe.wait_ge(*W("mix_a", ("exp", u - 2)))
                        for x in range(2):
                            half = slice(64 * x, 64 * x + 64)
                            mm = pe.matmul(psum[4 * (u % 2) + x][:, 0:keys], d_q[half, h, P * qb:P * qb + P],
                                           d_k[half, h, 0:keys], start=True, stop=True)
                        mm.then_inc(*T("product", ("scores", u)))
                    if 2 <= u < U + 2:
                        v = u - 2
                        pe.wait_ge(*W("mix_v", ("probs", v)))
                        if v >= 2:
                            pe.wait_ge(*W("mix_a", ("turned", v - 2)))
                        for t in range(v % 2 + 1):
                            mm = pe.transpose(psum[2 + v % 2][:, P * t:P * t + P], d_p[v % 3][:, 0, P * t:P * t + P], ident)
                        mm.then_inc(*T("product", ("turn", v)))
                    if u >= 3 and (u - 3) % 2:
                        h = (u - 3) // 2
                        pe.wait_ge(*W("mix_a", ("turned", u - 3)))
                        if h >= 2:
                            pe.wait_ge(*W("mix_a", ("out", h - 2)))
                        at, o = d_at[h % 2], psum[6 + h % 2]
                        pe.matmul(o[:, 0:T1], d_v[:, 0, P * h:P * h + P], at[:, 0, :], start=True, stop=False)
                        pe.matmul(o[:, P:T1], d_v[:, 1, P * h:P * h + P], at[:, 1, P:T1], start=False, stop=True)\
                            .then_inc(*T("product", ("out", h)))
                for n in range(4):
                    pe.wait_ge(*W("mix_a", ("osq", n)))
                    for b in range(4):
                        mm = pe.matmul(psum[4][:, 4 * n + b:4 * n + b + 1], d_osq[n][:, P * b:P * b + P], ones[:, 0:1],
                                       start=True, stop=True)
                mm.then_inc(*T("product", "osums"))
                pe.wait_ge(*W("mix_v", "oinverse"))
                for n in range(4):
                    for b in range(4):
                        mm = pe.matmul(psum[n][:, P * b:P * b + P], inv8[:, 4 * n + b:4 * n + b + 1].broadcast_to([P, P]), ident,
                                       start=True, stop=True)
                    mm.then_inc(*T("product", ("obcast", n)))
                bank_user.clear()

            def attention(l):
                stage[0] = f"mix2.{l}"
                pe.wait_ge(*W("mix_v", ("roped", 3), at=f"in{l}"))
                pe.wait_ge(*W("mix_a", ("dup", 1), at=f"in{l}"))
                for b in range(4):
                    bank_ready(b)
                us = units(l)
                for u in range(len(us) + 3):
                    if u < len(us):
                        s, pair, qb = us[u]
                        k0, k1 = keys_of(s)
                        if u >= 2:
                            pe.wait_ge(*W("mix_a", ("exp", u - 2)))
                        for x in range(2):
                            half = slice(64 * x, 64 * x + 64)
                            k = g_kd[half, (2 * pair + x) // 3, k0:k1] if pair < 3 else g_kb[half, pair - 3, k0:k1]
                            mm = pe.matmul(psum[4 * (u % 2) + x][:, 0:k1 - k0], g_q[half, pair, T1 * s + P * qb:T1 * s + P * qb + P], k,
                                           start=True, stop=True)
                        mm.then_inc(*T("product", ("scores", u)))
                    if 2 <= u < len(us) + 2:
                        v = u - 2
                        k0, k1 = keys_of(us[v][0])
                        pe.wait_ge(*W("mix_v", ("probs", v)))
                        if v:
                            pe.wait_ge(*W("mix_a", ("turned", v - 1)))
                        for x in range(2):
                            for t in range((k1 - k0) // P):
                                mm = pe.transpose(psum[2 + x][:, P * t:P * t + P], g_p[v % 3][:, x, P * t:P * t + P], ident)
                        mm.then_inc(*T("product", ("turn", v)))
                    if u >= 3:
                        v = u - 3
                        s, pair, _ = us[v]
                        k0, k1 = keys_of(s)
                        pe.wait_ge(*W("mix_a", ("turned", v)))
                        if v >= 2:
                            pe.wait_ge(*W("h_ready", v - 2))
                        nt = (k1 - k0) // P
                        for t in range(nt):
                            for x in range(2):
                                c0 = 64 * ((2 * pair + x) // 3) if pair < 3 else P + 64 * (2 * pair + x - 6)
                                mm = pe.matmul(psum[6 + v % 2][64 * x:64 * x + 64, 0:P], g_v[:, k0 // P + t, c0:c0 + 64],
                                               g_pt[v % 2][:, x, t, :], start=(t == 0), stop=(t == nt - 1))
                        mm.then_inc(*T("product", ("out", v)))
                pe.wait_ge(*W("conv_ready", 1))
                bank_user.clear()

            def turn_out():
                stage[0] = "store"
                for t in range(2):
                    for j in range(KT):
                        if t == 0:
                            pe.wait_ge(*W("x_ready", j, at=f"post{LAST}"))
                        mm = pe.transpose(psum[2 * t + j // 4][:, P * (j % 4):P * (j % 4) + P], X[:, j, P * t:P * t + P], ident)
                        if j % 4 == 3:
                            mm.then_inc(*T("product", (t, j // 4)))

            pe.wait_ge(*W("small_in", "all", at="load"))
            pe.wait_ge(*W("setup", "act", at="load"))
            pe.wait_ge(*W("ones_set", 0, at="load"))
            turn_in()
            pe.wait_ge(*W("x_ready", KT - 1, at="turn_in"))
            sum_squares("norm0.0", T1)
            for c in range(ADA_START + 1):
                ada(c, ADA_START, psum[0:2], psum[4], ada_row0)
            linear("mlstm", "norm0.0")
            mlstm()
            linear("mlstm_out", "mix0", per_tile=False)
            sum_squares("norm0.1", T1)
            moe(0)
            sum_squares("norm1.0", T1)
            linear("diff", "norm1.0", after=head_pipe("diff"))
            diff()
            linear("diff_out", "mix1", per_tile=False)
            sum_squares("norm1.1", T1)
            moe(1)
            for l in range(DEPTH):
                last = T1 if l == DEPTH - 1 else T2
                sum_squares(f"normffn{l}a", T2)
                ffn(l, 0)
                sum_squares(f"post{l}.0", T2)
                sum_squares(f"normin{l}", T2)
                linear(f"in{l}", f"normin{l}", after=head_pipe(f"in{l}"))
                attention(l)
                linear(f"attn_out{l}", f"mix2.{l}", per_tile=False)
                sum_squares(f"post{l}.1", last)
                sum_squares(f"normffn{l}b", last)
                ffn(l, 1)
                sum_squares(f"postffn{l}b", last)
            turn_out()

        @block.scalar
        def _(act):
            st = Stream()
            split_user = {}

            def step(ins, key=None):
                ins.then_inc(*T("act_step", ("n", log.count.get("act_step", 0))))
                act.wait_ge(sem("act_step"), log.count["act_step"])

            def split_hi(c, size, user, back=0):
                used, n = st.next(c % SLOTS)
                act.wait_ge(sem(f"raw_full{c % SLOTS}"), used * 16)
                if user:
                    act.wait_ge(*W("product", user[0], at=user[1], back=back))
                act.activation(w_hi[c % 2][:, 0:size], raw[c % SLOTS][:, 0:size], ACT.Copy).then_inc(sem("hi_ready"), 1)

            def ada(c, bank, row):
                used, _ = st.next(c % SLOTS, 0)
                act.wait_ge(sem(f"raw_done{c % SLOTS}"), used + 1)
                act.activation(row[:, c % 2, :], bank[:, 0:256], ACT.Copy).then_inc(*T("ada_row", c))

            def root(n):
                act.wait_ge(*W("product", "squares"))
                act.activation(rms4[:, 0:n // P], sums_bank(stage[0])[:, 0:n // P], ACT.Sqrt, bias=epsc, scale=1.0 / D).then_inc(*T("rms", 0))

            def square(name, src, key, j, n):
                act.wait_ge(*W(*key))
                act.activation(squares_of(name)[:, j, 0:n], src[:, j, 0:n], ACT.Square)\
                    .then_inc(*T("squared", j, stage_of=name))

            def norm(name, n, parts, x_at, between=None):
                stage[0] = name
                act.activation(warm[:, 0:1], onec, ACT.Sqrt)
                for j in range(SQUARED.get(name, 0), KT):
                    square(name, X, x_key(x_at, j), j, n)
                root(n)
                if between:
                    between()
                for j in range(KT):
                    act.wait_ge(*W("scaled", j))
                    for a, b, _, sh in parts:
                        ins = act.activation(h_hi[:, j, a:b], quad[j % 4][:, a:b], ACT.Identity, bias=sh(j))
                    ins.then_inc(*T("h_upper", j))

            def post(name, n):
                stage[0] = name
                for j in range(SQUARED[name], KT):
                    square(name, Y, y_key(name, j), j, n)
                root(n)

            def head_pipe(name):
                work = head_norms(name)

                def after(c):
                    if 0 <= (n := c - 1) < len(work):
                        x, _, _, query, _ = work[n]
                        w = x.shape[1] // HD
                        act.wait_ge(*W("product", ("sums", n)))
                        act.activation(rms8[:, 0:w], psum[4][:, 0:w], ACT.Sqrt, bias=epsq if query else epsc,
                                       scale=1.0 if query else 1.0 / HD).then_inc(*T("mix_a", ("rms", n)))
                    if c < len(work):
                        x, source, _, _, _ = work[c]
                        act.wait_ge(*W("evac_a", source))
                        act.activation(tmp[0][:, 0:x.shape[1]], x, ACT.Square).then_inc(*T("mix_a", ("sq", c)))
                    if name != "diff" and c == 7:
                        for n in range(2):
                            act.wait_ge(*W("product", ("dup", n)))
                            act.activation(g_kd[:, n, :], psum[4 + n][:, :], ACT.Copy).then_inc(*T("mix_a", ("dup", n)))
                return after

            def linear(name, evac, following, after=None):
                stage[0] = name
                chunks = ITEMS[name]
                for c in range(len(chunks)):
                    if c + 1 < len(chunks):
                        split_hi(c + 1, SLOT, split_user.get((c + 1) % 2))
                    elif following:
                        split_hi(0, SLOT, split_user.get(0))
                    split_user[c % 2] = (last_item(name, c), name)
                    for n in range(len(chunks[c])):
                        if EVAC[name](c, n) == "evac_a":
                            act.wait_ge(*W("product", (c, n)))
                            evac(c, n).then_inc(*T("evac_a", (c, n)))
                    if after:
                        after(c)
                    if name in MADE_BY and c:
                        for j in (2 * c - 2, 2 * c - 1):
                            square(MADE_BY[name], Y if name.startswith("attn") else X, ("evac_v", (c - 1, j % 2)), j, chunks[0][0][2])

            def moe(l):
                name = stage[0] = f"moe{l}"
                act.wait_ge(*W("product", "router"))
                act.activation(e_s.rearrange("p t e -> p (t e)"), psum[0][:, 0:32], ACT.Sigmoid).then_inc(*T("scores", 0))
                with act.Fori(0, N_EXP) as i:
                    st.enter(i, EXP_CH)
                    log.enter(name, i, N_EXP)
                    def upper(c):
                        act.wait_ge(*W("gated", c))
                        act.activation(e_hi[:, c, :], full[c % 2][:, 0:T1], ACT.Copy).then_inc(*T("act_upper", c))

                    for c in range(EXP_CH):
                        if c == 4:
                            upper(3)
                        if c == 0:
                            split_hi(1, SLOT, (("down", 5), name), back=1)
                        elif c == EXP_CH - 1:
                            split_hi(0, SLOT, (("down", 4), name))
                        else:
                            split_hi(c + 1, SLOT, (("down" if c > 4 else "up", c - 1), name))
                        if 1 <= c <= 3:
                            act.wait_ge(*W("ada_done", c - 1))
                            act.activation(ada_row2, psum[3][:, 0:256], ACT.Copy).then_inc(*T("ada_row", c - 1))
                        if c < 4:
                            act.wait_ge(*W("product", ("up", c)))
                            act.activation(tmp[c % 2][:, 0:T1], psum[UP_BANK[c]][:, 0:T1], ACT.Silu).then_inc(*T("silu", c))
                        if 1 <= c <= 3:
                            upper(c - 1)
                    log.leave()
                st.leave(N_EXP)
                split_user[0], split_user[1] = (("down", 4), name), (("down", 5), name)

            def ffn(l, which, following):
                name = stage[0] = f"ffn{l}{'ab'[which]}"
                n = T1 if name == LAST else T2

                def upper(tag, c):
                    act.wait_ge(*W("gated", (tag, c)))
                    act.activation(act_hi[:, c, 0:n], full[c % 2][:, 0:n], ACT.Copy).then_inc(*T("act_upper", (tag, c)))

                for at in range(2 * FFN_CH):
                    tag, c = ffn_chunk(at)
                    if c == FFN_UP:
                        upper(tag, c - 1)
                    if at + 1 < 2 * FFN_CH:
                        split_hi(at + 1, SLOT if (at + 1) % FFN_CH < FFN_UP else DOWN,
                                 (ffn_chunk(at - 1), name) if at else split_user.get(1))
                    elif following:
                        split_hi(0, SLOT, (ffn_chunk(at - 1), name))
                    if c < FFN_UP:
                        act.wait_ge(*W("product", (tag, c)))
                        act.activation(tmp[c % 2][:, 0:n], psum[2 * (c % 2)][:, 0:n], ACT.Silu).then_inc(*T("silu", (tag, c)))
                        if c:
                            upper(tag, c - 1)
                    if tag == "g1" and c > FFN_UP:
                        if c == FFN_UP + 1:
                            act.activation(warm[:, 0:1], onec, ACT.Sqrt)
                        square(MADE_BY[name], Y, y_key(MADE_BY[name], c - FFN_UP - 1), c - FFN_UP - 1, n)
                split_user[0], split_user[1] = (ffn_chunk(2 * FFN_CH - 2), name), (ffn_chunk(2 * FFN_CH - 1), name)

            def mlstm_evac(c, n):
                b = psum[bank_of("mlstm", c, n)][:, 0:T1]
                if c < 4:
                    j = 2 * (c % 2) + n
                    return act.activation((m_q if c < 2 else m_k)[:, j, :], b, ACT.Copy, scale=1.0 if c < 2 else A_QK ** -0.5)
                return act.activation(m_og[:, 2 * (c - 8) + n, :], b, ACT.Sigmoid)

            def mlstm():
                stage[0] = "mix0"
                act.wait_ge(*W("gate_v", "gates"))
                step(act.activation(m_u, m_g[:, :, A_HEADS:], ACT.Abs))
                step(act.activation(m_u, m_u, ACT.Exp, scale=-1.0))
                act.activation(m_u, m_u, ACT.Ln, bias=onec).then_inc(*T("mix_a", "log1p"))
                chunks = iter(range(ADA_MIX))

                def more():
                    c = next(chunks)
                    ada(c, psum[6 + c % 2], ada_row1)

                for _ in range(4):
                    more()
                def decays(h):
                    act.wait_ge(*W("mix_v", ("gap", h)))
                    act.activation(m_d, m_d, ACT.Exp, scale=-1.0).then_inc(*T("mix_a", ("decay", h)))
                    act.activation(m_em[:, h % 2, :], psum[0][:, T1:T2], ACT.Exp, scale=-1.0).then_inc(*T("mix_a", ("floor", h)))

                decays(0)
                for h in range(A_HEADS):
                    if h + 1 < A_HEADS:
                        decays(h + 1)
                    more()
                    act.wait_ge(*W("product", ("sums", h)))
                    act.activation(m_dn, psum[2][:, 0:T1], ACT.Abs).then_inc(*T("mix_a", ("den", h)))
                    more()
                    act.wait_ge(*W("mix_v", ("normed", h)))
                    act.activation(quad[h], m_hh[:, 2 * h:2 * h + 2, :].rearrange("p a t -> p (a t)"), ACT.Square)\
                        .then_inc(*T("mix_a", ("squared", h)))
                    more()
                act.wait_ge(*W("product", "head_sq"))
                act.activation(rms8[:, 0:8], psum[4][:, 0:8], ACT.Sqrt, bias=epsc, scale=1.0 / A_V).then_inc(*T("mix_a", "rms"))
                split_hi(0, SLOT, split_user.get(0))
                for h in range(A_HEADS):
                    act.wait_ge(*W("mix_v", ("out", h)))
                    act.activation(h_hi[:, 2 * h:2 * h + 2, 0:T1], m_hh[:, 2 * h:2 * h + 2, :], ACT.Copy).then_inc(*T("mix_a", ("upper", h)))

            def diff_evac(c, n):
                j = 2 * (c % 4) + n
                return act.activation((d_q if c < 4 else d_k)[:, j, :], psum[bank_of("diff", c, n)][:, 0:T1], ACT.Copy)

            def sines():
                act.wait_ge(*W("diff_tables", "angles", at="load"))
                act.activation(d_sin, d_ang, ACT.Sin)
                act.activation(d_n, d_n, ACT.Sin).then_inc(*T_at("diff_sines", 0))
                act.wait_ge(*W("diff_tables", "dots", at="load"))
                act.activation(d_ls[:, 2:4], d_ls[:, 0:2], ACT.Exp).then_inc(*T_at("diff_lam", 0))

            def diff():
                stage[0] = "mix1"
                U = 2 * B_HEADS
                for u in range(U + 3):
                    if u < U:
                        keys = P * (u % 2 + 1)
                        act.wait_ge(*W("mix_v", ("max", u)))
                        if u >= 3:
                            act.wait_ge(*W("product", ("turn", u - 3)))
                        for x in range(2):
                            ins = act.activation(d_p[u % 3][:, x, 0:keys], psum[4 * (u % 2) + x][:, 0:keys], ACT.Exp,
                                                 bias=d_st[u % 2][:, x:x + 1], accum_out=d_st[u % 2][:, 2 + x:3 + x])
                        ins.then_inc(*T("mix_a", ("exp", u)))
                    if 2 <= u < U + 2:
                        v = u - 2
                        act.wait_ge(*W("product", ("turn", v)))
                        if v >= 4:
                            act.wait_ge(*W("product", ("out", v // 2 - 2)))
                        t = v % 2 + 1
                        act.activation(d_at[(v // 2) % 2][:, 0:t, P * (v % 2):P * (v % 2) + P],
                                       psum[2 + v % 2][:, 0:P * t].rearrange("p (t n) -> p t n", t=t), ACT.Copy)\
                            .then_inc(*T("mix_a", ("turned", v)))
                    if u >= 3 and (u - 3) % 2:
                        h = (u - 3) // 2
                        act.wait_ge(*W("product", ("out", h)))
                        act.activation(d_q[:, h, :], psum[6 + h % 2][:, 0:T1], ACT.Copy).then_inc(*T("mix_a", ("out", h)))
                        if h % 2:
                            act.wait_ge(*W("mix_a", ("out", h)))
                            act.activation(d_osq[h // 2], d_q[:, h - 1:h + 1, :].rearrange("p a t -> p (a t)"), ACT.Square)\
                                .then_inc(*T("mix_a", ("osq", h // 2)))
                act.wait_ge(*W("product", "osums"))
                c = (1.0 - LAM_INIT) ** 2
                act.activation(rms8, psum[4][:, 0:16], ACT.Sqrt, bias=epso, scale=1.0 / (2 * B_HD * c)).then_inc(*T("mix_a", "orms"))
                for n in range(4):
                    act.wait_ge(*W("mix_v", ("onormed", n)))
                    act.activation(h_hi[:, 2 * n:2 * n + 2, 0:T1], d_q[:, 2 * n:2 * n + 2, :], ACT.Copy).then_inc(*T("mix_a", ("upper", n)))

            def in_evac(name, l):
                nq = T1 if l == DEPTH - 1 else T2

                def f(c, n):
                    bank = psum[bank_of(name, c, n)]
                    if c < 3:
                        j = 2 * c + n
                        return act.activation(g_q[:, j, 0:nq], bank[:, 0:nq], ACT.Copy, scale=1.0 if j < 3 else HD ** -0.5)
                    if c == 3:
                        return act.activation(g_ka, bank[:, :], ACT.Copy)
                    if c in (4, 5):
                        return act.activation(g_kb[:, 2 * (c - 4) + n, :], bank[:, :], ACT.Copy)
                    dst = (g_cx, g_cb, g_cc)[c - 7]
                    return act.activation(dst[:, n, 0:nq], bank[:, 0:nq], ACT.Copy)
                return f

            def attention(l):
                stage[0] = f"mix2.{l}"
                nq = T1 if l == DEPTH - 1 else T2
                us = units(l)
                split_user[1] = (("turn", len(us) - 1), f"mix2.{l}")
                for u in range(len(us) + 3):
                    if u < len(us):
                        k0, k1 = keys_of(us[u][0])
                        act.wait_ge(*W("mix_v", ("max", u)))
                        if u >= 3:
                            act.wait_ge(*W("product", ("turn", u - 3)))
                        for x in range(2):
                            ins = act.activation(g_p[u % 3][:, x, 0:k1 - k0], psum[4 * (u % 2) + x][:, 0:k1 - k0], ACT.Exp,
                                                 bias=g_st[u % 2][:, x:x + 1], accum_out=g_st[u % 2][:, 2 + x:3 + x])
                        ins.then_inc(*T("mix_a", ("exp", u)))
                    if u in (1, 2):
                        act.wait_ge(*W("conv", u - 1))
                        act.activation(h_hi[:, 5 + u, 0:nq], g_cb[:, u - 1, 0:nq], ACT.Copy).then_inc(*T("conv_upper", u - 1))
                    if 2 <= u < len(us) + 2:
                        v = u - 2
                        nt = (keys_of(us[v][0])[1] - keys_of(us[v][0])[0]) // P
                        act.wait_ge(*W("product", ("turn", v)))
                        if v >= 2:
                            act.wait_ge(*W("product", ("out", v - 2)))
                        for x in range(2):
                            ins = act.activation(g_pt[v % 2][:, x, 0:nt, :].rearrange("p t n -> p (t n)"), psum[2 + x][:, 0:P * nt], ACT.Copy)
                        ins.then_inc(*T("mix_a", ("turned", v)))
                    if u >= 3:
                        v = u - 3
                        s, pair, qb = us[v]
                        act.wait_ge(*W("product", ("out", v)))
                        act.activation(h_hi[:, pair, T1 * s + P * qb:T1 * s + P * qb + P], psum[6 + v % 2][:, 0:P], ACT.Copy)\
                            .then_inc(*T("mix_a", ("upper", v)))

            act.wait_ge(*W("small_in", "all", at="load"))
            act.wait_ge(*W("ones_set", 0, at="load"))
            act.activation(cact[:, :, 0], V["c1"], ACT.Silu)
            act.activation(cact[:, :, 1:3], V["c2"].rearrange("p (k s) -> p k s", k=KT), ACT.Silu).then_inc(*T_at("setup", "act"))
            def start():
                for c in range(ADA_START):
                    if c == 4:
                        sines()
                    ada(c, psum[c % 2], ada_row0)
                split_hi(0, SLOT, None)
                act.wait_ge(*W("mods", "0.0", at="load"))

            norm("norm0.0", T1, part1(0, 0), "turn_in", start)
            linear("mlstm", mlstm_evac, False)
            mlstm()
            linear("mlstm_out", None, True)
            act.wait_ge(*W("mods", "0.1", at="load"))
            norm("norm0.1", T1, part1(0, 1), "mlstm_out")
            moe(0)
            act.wait_ge(*W("mods", "1", at="load"))
            norm("norm1.0", T1, part1(1, 0), "moe0")
            linear("diff", diff_evac, True, head_pipe("diff"))
            diff()
            linear("diff_out", None, True)
            norm("norm1.1", T1, part1(1, 1), "diff_out")
            moe(1)
            act.wait_ge(*W("mods", "2", at="load"))
            for l in range(DEPTH):
                both = l < DEPTH - 1
                n = T2 if both else T1
                norm(f"normffn{l}a", T2, part2(l, 0, 1), "moe1" if l == 0 else f"postffn{l - 1}b")
                ffn(l, 0, True)
                post(f"post{l}.0", T2)
                norm(f"normin{l}", T2, part2(l, 1, 1), f"post{l}.0")
                linear(f"in{l}", in_evac(f"in{l}", l), True, head_pipe(f"in{l}"))
                attention(l)
                linear(f"attn_out{l}", None, True)
                post(f"post{l}.1", n)
                norm(f"normffn{l}b", n, part2(l, 2, both), f"post{l}.1")
                ffn(l, 1, both)
                post(f"postffn{l}b", n)

        @block.vector
        def _(dve):
            st = Stream()

            def step(ins):
                ins.then_inc(*T("vec_step"))
                dve.wait_ge(sem("vec_step"), log.count["vec_step"])

            def split_lo(c, size):
                _, n = st.next(c % SLOTS)
                dve.wait_ge(sem("hi_ready"), n)
                dve.tensor_tensor(w_lo[c % 2][:, 0:size], raw[c % SLOTS][:, 0:size], w_hi[c % 2][:, 0:size].bitcast(F32),
                                  ALU.subtract).then_inc(sem(f"raw_done{c % SLOTS}"), 1)

            def mods_first(lo, hi, cols, w):
                step(dve.tensor_tensor(mod_first[:, lo:hi], cols[:, 0:hi - lo], V["b_ada"][:, lo:hi], ALU.add))
                pre_scales(0, w).then_inc(*T_at("mods", f"0.{w}"))
                dve.wait_ge(*W("mods", f"0.{w}", at="load"))

            def pre_scales(l, w):
                return dve.scalar_tensor_tensor(pre1[:, l, w, :], mod1[l][:, 24 * w + 8:24 * w + 16], 1.0,
                                                V["norm1" if w == 0 else "norm2"][:, 8 * l:8 * l + 8], ALU.add, ALU.mult)

            def mods_second():
                step(dve.tensor_tensor(mod1[1], mod1[1], V["b_ada"][:, 48:96], ALU.add))
                pre_scales(1, 0)
                pre_scales(1, 1).then_inc(*T_at("mods", "1"))
                dve.wait_ge(*W("mods", "1", at="load"))

            def mods_latent():
                m2 = mod_all[:, 48:, :]
                for s in range(2):
                    ins = dve.tensor_tensor(m2[:, :, 1 + s], m2[:, :, 1 + s], V["b_ada_2"], ALU.add)
                step(ins)
                ng = V["norm_g_2"].rearrange("p (l g k) -> p l g k", l=DEPTH, g=6)
                for l in range(DEPTH):
                    for i in range(3):
                        for s in range(2):
                            dve.scalar_tensor_tensor(pre2[:, l, i, :, s], mod2[:, l, 3 * i + 1, :, s], 1.0, ng[:, l, 2 * i, :],
                                                     ALU.add, ALU.mult)
                            ins = dve.scalar_tensor_tensor(post2[:, l, i, :, s], mod2[:, l, 3 * i + 2, :, s],
                                                           1.0 if i == 1 else 0.5, ng[:, l, 2 * i + 1, :], ALU.mult, ALU.mult)
                ins.then_inc(*T_at("mods", "2"))
                dve.wait_ge(*W("mods", "2", at="load"))

            def turn_in():
                stage[0] = "turn_in"
                for j in range(KT):
                    dve.wait_ge(*W("product", j))
                    dve.tensor_copy(X[:, j, :], psum[j][:, :]).then_inc(*T("x_ready", j))

            def inverse(n):
                dve.wait_ge(*W("rms", 0))
                dve.reciprocal(inv4[:, 0:n // P], rms4[:, 0:n // P]).then_inc(*T("inverse", 0))
                dve.wait_ge(*W("product", "rstd"))

            def norm(name, n, parts, between=None):
                stage[0] = name
                inverse(n)
                if between:
                    between()
                for j in range(KT + 1):
                    if j < KT:
                        if j >= 4:
                            dve.wait_ge(*W("h_ready", j - 4))
                        for a, b, sc, _ in parts:
                            ins = dve.scalar_tensor_tensor(quad[j % 4][:, a:b], X[:, j, a:b], sc(j), psum[7][:, a:b], ALU.mult, ALU.mult)
                        ins.then_inc(*T("scaled", j))
                    if j:
                        k = j - 1
                        dve.wait_ge(*W("h_upper", k))
                        for a, b, _, sh in parts:
                            ins = dve.scalar_tensor_tensor(h_lo[:, k, a:b], quad[k % 4][:, a:b], sh(k), h_hi[:, k, a:b].bitcast(F32),
                                                           ALU.add, ALU.subtract)
                        ins.then_inc(*T("h_ready", k))

            def post(name, n, l, i):
                stage[0] = name
                inverse(n)
                for j in range(KT + 1):
                    if j < KT:
                        if j >= 2:
                            dve.wait_ge(*W("x_ready", j - 2))
                        dve.tensor_tensor(tmp[j % 2][:, 0:n], Y[:, j, 0:n], psum[7][:, 0:n], ALU.mult).then_inc(*T("scaled", j))
                    if j:
                        k = j - 1
                        dve.wait_ge(*W("scaled", k))
                        for s in range(n // T1):
                            cut = slice(T1 * s, T1 * s + T1)
                            ins = dve.scalar_tensor_tensor(X[:, k, cut], tmp[k % 2][:, cut], post2[:, l, i, k, s:s + 1],
                                                           X[:, k, cut], ALU.mult, ALU.add)
                        ins.then_inc(*T("x_ready", k))
                dve.wait_ge(*W("x_ready", KT - 1))

            def head_pipe(name):
                work = head_norms(name)
                if name != "diff":
                    dve.wait_ge(*W("consts2_in", 0, at="load"))

                def after(c):
                    if 0 <= (n := c - 1) < len(work):
                        w = work[n][0].shape[1] // HD
                        dve.wait_ge(*W("mix_a", ("rms", n)))
                        dve.reciprocal(inv8[:, 0:w], rms8[:, 0:w]).then_inc(*T("mix_v", ("inverse", n)))
                    if 0 <= (n := c - 2) < len(work):
                        x, _, gain, _, _ = work[n]
                        dve.wait_ge(*W("product", ("bcast", n)))
                        dve.scalar_tensor_tensor(x, x, gain, psum[5][:, 0:x.shape[1]], ALU.mult, ALU.mult).then_inc(*T("mix_v", ("normed", n)))
                    if 0 <= (n := c - 3) < len(work):
                        x, _, _, _, turned = work[n]
                        cos, sin = (d_cos, d_sin) if name == "diff" else (C2["cos2"], C2["sin2"])
                        dve.wait_ge(*W("product", ("rot", n)))
                        for a in range(0, turned, T1):
                            dve.tensor_tensor(full[0][:, a:a + T1], psum[6][:, a:a + T1], sin, ALU.mult)
                            step(dve.tensor_tensor(x[:, a:a + T1], x[:, a:a + T1], cos, ALU.mult))
                            ins = dve.tensor_tensor(x[:, a:a + T1], x[:, a:a + T1], full[0][:, a:a + T1], ALU.add)
                        ins.then_inc(*T("mix_v", ("roped", n)))
                return after

            def linear(name, evac, following, after=None):
                stage[0] = name
                chunks = ITEMS[name]
                for c in range(len(chunks)):
                    if c + 1 < len(chunks):
                        split_lo(c + 1, SLOT)
                    elif following:
                        split_lo(0, SLOT)
                    for n in range(len(chunks[c])):
                        if EVAC[name](c, n) == "evac_v":
                            dve.wait_ge(*W("product", (c, n)))
                            evac(c, n).then_inc(*T("evac_v", (c, n)))
                    if after:
                        after(c)

            def residual(name, l, w):
                def f(c, n):
                    j = 2 * c + n
                    return dve.scalar_tensor_tensor(X[:, j, 0:T1], psum[bank_of(name, c, n)][:, 0:T1],
                                                    mod1[l][:, 24 * w + 16 + j:24 * w + 17 + j], X[:, j, 0:T1], ALU.mult, ALU.add)
                return f

            def moe(l):
                name = stage[0] = f"moe{l}"
                dve.memset(e_zero.bitcast(U32), 0)
                dve.wait_ge(*W("scores", 0))
                for t in range(2):
                    step(dve.tensor_tensor(e_b[:, t, :], e_s[:, t, :], V["router_bias"], ALU.add))
                for t in range(2):
                    b = e_b[:, t, :].rearrange("p (g e) -> p g e", g=N_GRP)
                    pairs = [(x, y) for x in range(E_GRP) for y in range(x + 1, E_GRP)]
                    for n, (x, y) in enumerate(pairs):
                        ins = dve.tensor_tensor(e_pair[:, :, n:n + 1], b[:, :, x:x + 1], b[:, :, y:y + 1], ALU.add)
                    step(ins)
                    step(dve.memset(e_g8, INVALID))
                    step(dve.tensor_reduce(e_g8[:, 0:N_GRP], e_pair, AX.X, ALU.max))
                    step(dve.max(e_x8, e_g8))
                    step(dve.max_index(e_i8, e_x8, e_g8))
                    step(dve.tensor_copy(e_f8, e_i8))
                    step(dve.tensor_scalar(e_oh, C["iota8"], e_f8[:, 0:1], None, ALU.is_equal))
                    for q in range(N_GRP):
                        ins = dve.tensor_scalar(e_m[:, t, 4 * q:4 * q + 4], e_b[:, t, 4 * q:4 * q + 4], e_oh[:, q:q + 1], None, ALU.mult)
                    step(ins)
                    step(dve.tensor_scalar(e_oh, e_oh, -1.0, -INVALID, ALU.add, ALU.mult))
                    for q in range(N_GRP):
                        ins = dve.tensor_scalar(e_m[:, t, 4 * q:4 * q + 4], e_m[:, t, 4 * q:4 * q + 4], e_oh[:, q:q + 1], None, ALU.add)
                    step(ins)
                    step(dve.max(e_x8, e_m[:, t, :]))
                    step(dve.max_index(e_i8, e_x8, e_m[:, t, :]))
                    step(dve.tensor_copy(e_f8, e_i8))
                    step(dve.tensor_scalar(e_w[:, t, :], C["iota16"], e_f8[:, 0:1], None, ALU.is_equal))
                    step(dve.scalar_tensor_tensor(e_w[:, t, :], C["iota16"], e_f8[:, 1:2], e_w[:, t, :], ALU.is_equal, ALU.add))
                    step(dve.tensor_tensor(e_w[:, t, :], e_w[:, t, :], e_s[:, t, :], ALU.mult))
                    step(dve.tensor_reduce(e_f8[:, 0:1], e_w[:, t, :], AX.X, ALU.add))
                    step(dve.reciprocal(e_f8[:, 1:2], e_f8[:, 0:1]))
                    ins = dve.tensor_scalar(e_w[:, t, :], e_w[:, t, :], e_f8[:, 1:2], None, ALU.mult)
                    if t == 0:
                        step(ins)
                ins.then_inc(*T("gate_w", "tokens"))
                dve.wait_ge(*W("product", "gate_rows"))
                dve.tensor_copy(e_row, psum[0][0:N_EXP, 128:128 + T1]).then_inc(*T("gate_w", "rows"))
                for x in range(N_EXP):
                    dve.wait_ge(*W("product", ("bc", x)))
                    dve.tensor_copy(e_gate[:, x, :], psum[x % 4][:, 0:T1]).then_inc(*T("gate_bc", x))
                dve.wait_ge(*W("gate_bc", N_EXP - 1))
                with dve.Fori(0, N_EXP) as i:
                    st.enter(i, EXP_CH)
                    log.enter(name, i, N_EXP)

                    def lower(c):
                        dve.wait_ge(*W("act_upper", c))
                        dve.tensor_tensor(e_lo[:, c, :], full[c % 2][:, 0:T1], e_hi[:, c, :].bitcast(F32), ALU.subtract)\
                            .then_inc(*T("act_ready", c))

                    for c in range(EXP_CH):
                        if c == 4:
                            lower(3)
                            dve.wait_ge(*W("product", ("turned", 2)))
                            dve.tensor_copy(mod_all.rearrange("p m s -> p (m s)")[:, ds(i * 18 + 18 * N_EXP * l, 18)],
                                            psum[3][:, T1:T1 + 18]).then_inc(*T("ada_col", "col"))
                        split_lo((c + 1) % EXP_CH, SLOT)
                        if c < 4:
                            dve.wait_ge(*W("silu", c))
                            dve.tensor_tensor(tmp[c % 2][:, T1:T2], tmp[c % 2][:, 0:T1], e_gate[:, ds(i, 1), :].rearrange("p e t -> p (e t)"), ALU.mult)\
                                .then_inc(*T("weighted", c))
                            dve.wait_ge(*W("weighted", c))
                            dve.tensor_tensor(full[c % 2][:, 0:T1], psum[UP_BANK[c]][:, T1:T2], tmp[c % 2][:, T1:T2], ALU.mult)\
                                .then_inc(*T("gated", c))
                        if 1 <= c <= 3:
                            lower(c - 1)
                    log.leave()
                st.leave(N_EXP)
                dve.wait_ge(*W("ada_col", "col"))
                if l == 0:
                    mods_second()
                else:
                    mods_latent()
                dve.wait_ge(*W("product", ("down", 5)))
                for j in range(KT):
                    dve.scalar_tensor_tensor(X[:, j, 0:T1], psum[4 + j // 2][:, T1 * (j % 2):T1 * (j % 2) + T1],
                                             mod1[l][:, 40 + j:41 + j], X[:, j, 0:T1], ALU.mult, ALU.add).then_inc(*T("x_ready", j))

            def ffn(l, which, following):
                name = stage[0] = f"ffn{l}{'ab'[which]}"
                n = T1 if name == LAST else T2

                def lower(tag, c):
                    dve.wait_ge(*W("act_upper", (tag, c)))
                    dve.tensor_tensor(act_lo[:, c, 0:n], full[c % 2][:, 0:n], act_hi[:, c, 0:n].bitcast(F32), ALU.subtract)\
                        .then_inc(*T("act_ready", (tag, c)))

                for at in range(2 * FFN_CH):
                    tag, c = ffn_chunk(at)
                    if c == FFN_UP:
                        lower(tag, c - 1)
                        dve.wait_ge(*W("act_ready", (tag, c - 1)))
                    if at + 1 < 2 * FFN_CH:
                        split_lo(at + 1, SLOT if (at + 1) % FFN_CH < FFN_UP else DOWN)
                    elif following:
                        split_lo(0, SLOT)
                    if c < FFN_UP:
                        dve.wait_ge(*W("silu", (tag, c)))
                        if c >= 2:
                            dve.wait_ge(*W("act_ready", (tag, c - 2)))
                        dve.tensor_tensor(full[c % 2][:, 0:n], psum[2 * (c % 2) + 1][:, 0:n], tmp[c % 2][:, 0:n], ALU.mult)\
                            .then_inc(*T("gated", (tag, c)))
                        if c:
                            lower(tag, c - 1)
                    else:
                        j = c - FFN_UP
                        dve.wait_ge(*W("product", (tag, c)))
                        if tag == "g0":
                            ins = dve.tensor_copy(Y[:, j, 0:n], psum[4 + j % 4][:, 0:n])
                        else:
                            ins = dve.tensor_tensor(Y[:, j, 0:n], Y[:, j, 0:n], psum[4 + j % 4][:, 0:n], ALU.add)
                        ins.then_inc(*T("y_ready", (tag, j)))

            def mlstm_evac(c, n):
                return dve.tensor_copy(m_v[:, :, 256 * (c - 4):256 * (c - 4) + 256],
                                       psum[bank_of("mlstm", c, n)][:, :].rearrange("p (t n) -> p t n", t=2))

            def mlstm():
                stage[0] = "mix0"
                dve.wait_ge(*W("product", "gates"))
                for t in range(2):
                    ins = dve.tensor_tensor(m_g[:, t, :], psum[4][:, 8 * t:8 * t + 8], V["b_if"], ALU.add)
                ins.then_inc(*T("gate_v", "gates"))
                dve.wait_ge(*W("mix_a", "log1p"))
                dve.scalar_tensor_tensor(m_lf, m_g[:, :, A_HEADS:], 0.0, m_u, ALU.min, ALU.subtract).then_inc(*T("gate_v", "log_f"))
                dve.wait_ge(*W("product", "cum"))
                step(dve.tensor_copy(m_b.rearrange("p t h -> p (t h)"), psum[4][:, 16:24]))
                dve.tensor_tensor(m_a, m_g[:, :, 0:A_HEADS], m_b, ALU.subtract).then_inc(*T("gate_v", "a"))
                dve.wait_ge(*W("product", "rows"))
                step(dve.tensor_copy(m_arow[0:A_HEADS, :], psum[5][0:A_HEADS, 0:T1]))
                step(dve.tensor_tensor_scan(m_rows[0:A_HEADS, 0:T1], m_arow[0:A_HEADS, :], m_arow[0:A_HEADS, :], 0.0, ALU.max, ALU.max))
                dve.tensor_tensor(m_rows[0:A_HEADS, T1:T2], m_rows[0:A_HEADS, 0:T1], psum[5][0:A_HEADS, T1:T2], ALU.add)\
                    .then_inc(*T("gate_v", "rows"))
                def gap(h):
                    dve.wait_ge(*W("product", ("bc", h)))
                    dve.tensor_scalar(m_d[:, 0:T1], psum[0][:, 0:T1], m_a[:, 0, h:h + 1], 0.0, ALU.subtract, ALU.max)
                    dve.tensor_scalar(m_d[:, T1:T1 + P], psum[0][:, P:T1], m_a[:, 1, h:h + 1], 0.0, ALU.subtract, ALU.max)\
                        .then_inc(*T("mix_v", ("gap", h)))

                gap(0)
                for h in range(A_HEADS):
                    dve.wait_ge(*W("mix_a", ("floor", h)))
                    dve.wait_ge(*W("product", ("scores", h)))
                    step(dve.tensor_tensor(m_p, psum[1][:, 0:384], m_d, ALU.mult))
                    dve.tensor_tensor(m_p[:, 0:P], m_p[:, 0:P], C["upper"], ALU.mult)
                    dve.tensor_tensor(m_p[:, T1:T1 + P], m_p[:, T1:T1 + P], C["upper"], ALU.mult).then_inc(*T("mix_v", ("masked", h)))
                    if h + 1 < A_HEADS:
                        gap(h + 1)
                    dve.wait_ge(*W("mix_a", ("den", h)))
                    step(dve.tensor_tensor(m_dn, m_dn, m_em[:, h % 2, :], ALU.max))
                    step(dve.reciprocal(m_dn, m_dn))
                    for q in range(2):
                        ins = dve.tensor_tensor(m_hh[:, 2 * h + q, :], psum[3][:, T1 * q:T1 * q + T1], m_dn, ALU.mult)
                    ins.then_inc(*T("mix_v", ("normed", h)))
                dve.wait_ge(*W("mix_a", "rms"))
                dve.reciprocal(inv8[:, 0:8], rms8[:, 0:8]).then_inc(*T("mix_v", "inverse"))
                split_lo(0, SLOT)
                dve.wait_ge(*W("product", "head_inv"))
                for h in range(A_HEADS + 1):
                    if h < A_HEADS:
                        for q in range(2):
                            j = 2 * h + q
                            ins = dve.scalar_tensor_tensor(m_hh[:, j, :], m_hh[:, j, :], V["a_h_norm"][:, j:j + 1],
                                                           psum[h // 2][:, T1 * (h % 2):T1 * (h % 2) + T1], ALU.mult, ALU.mult)
                        step(ins)
                        both = m_hh[:, 2 * h:2 * h + 2, :]
                        dve.tensor_tensor(both, both, m_og[:, 2 * h:2 * h + 2, :], ALU.mult).then_inc(*T("mix_v", ("out", h)))
                    if h:
                        k = h - 1
                        dve.wait_ge(*W("mix_a", ("upper", k)))
                        dve.tensor_tensor(h_lo[:, 2 * k:2 * k + 2, 0:T1], m_hh[:, 2 * k:2 * k + 2, :],
                                          h_hi[:, 2 * k:2 * k + 2, 0:T1].bitcast(F32), ALU.subtract).then_inc(*T("h_ready", k))
                dve.wait_ge(*W("product", ("turned", ADA_MIX - 1)))
                mods_first(2 * ADA_START, 48, psum[5], 1)

            def diff_evac(c, n):
                return dve.tensor_copy(d_v[:, :, 256 * (c - 8):256 * (c - 8) + 256],
                                       psum[bank_of("diff", c, n)][:, :].rearrange("p (t n) -> p t n", t=2))

            def angles():
                TWO_PI = 2 * math.pi
                c1 = 6.28125
                c2 = float(np.float32(np.round((TWO_PI - c1) * 2 ** 22) / 2 ** 22))
                c3 = float(np.float32(TWO_PI - c1 - c2))
                ROUND = 1.5 * 2 ** 23
                dve.wait_ge(*W("diff_in", "all", at="load"))
                step(dve.tensor_copy(d_ang, d_pos))
                step(dve.tensor_scalar(d_ang, d_ang, C["invfreq"], None, ALU.mult))
                step(dve.tensor_scalar(d_n, d_ang, 1.0 / TWO_PI, ROUND, ALU.mult, ALU.add))
                step(dve.tensor_scalar(d_n, d_n, ROUND, None, ALU.subtract))
                for cc in (c1, c2, c3):
                    step(dve.scalar_tensor_tensor(d_ang, d_n, -cc, d_ang, ALU.mult, ALU.add))
                step(dve.tensor_scalar(d_ang, d_ang, math.pi - 1e-6, -(math.pi - 1e-6), ALU.min, ALU.max))
                dve.tensor_scalar(d_n, d_ang, 0.5, None, ALU.mult).then_inc(*T_at("diff_tables", "angles"))
                dve.wait_ge(*W("diff_sines", 0, at="load"))
                step(dve.tensor_tensor(d_cos, d_n, d_n, ALU.mult))
                step(dve.tensor_scalar(d_cos, d_cos, -2.0, 1.0, ALU.mult, ALU.add))
                for n in range(2):
                    step(dve.tensor_tensor(d_lam[:, 2 * n, :], d_lam[:, 2 * n, :], d_lam[:, 2 * n + 1, :], ALU.mult))
                    ins = dve.tensor_reduce(d_ls[:, n:n + 1], d_lam[:, 2 * n, :], AX.X, ALU.add)
                ins.then_inc(*T_at("diff_tables", "dots"))
                dve.wait_ge(*W("diff_lam", 0, at="load"))
                step(dve.tensor_tensor(d_ls[:, 4:5], d_ls[:, 3:4], d_ls[:, 2:3], ALU.subtract))
                step(dve.tensor_scalar(d_ls[:, 5:6], d_ls[:, 4:5], LAM_INIT, None, ALU.subtract))

            def diff():
                stage[0] = "mix1"
                U = 2 * B_HEADS
                for u in range(U + 1):
                    if u < U:
                        keys = P * (u % 2 + 1)
                        dve.wait_ge(*W("product", ("scores", u)))
                        for x in range(2):
                            s = psum[4 * (u % 2) + x]
                            ins = dve.tensor_tensor(s[:, keys - P:keys], s[:, keys - P:keys], C["causal"], ALU.add)
                        step(ins)
                        for x in range(2):
                            ins = dve.tensor_reduce(d_st[u % 2][:, x:x + 1], psum[4 * (u % 2) + x][:, 0:keys], AX.X, ALU.max, negate=True)
                        ins.then_inc(*T("mix_v", ("max", u)))
                    if u:
                        v = u - 1
                        stt, p = d_st[v % 2], d_p[v % 3]
                        keys = P * (v % 2 + 1)
                        dve.wait_ge(*W("mix_a", ("exp", v)))
                        step(dve.reciprocal(stt[:, 4:6], stt[:, 2:4]))
                        step(dve.tensor_scalar(stt[:, 5:6], stt[:, 5:6], d_ls[:, 5:6], None, ALU.mult))
                        step(dve.tensor_scalar(p[:, 1, 0:keys], p[:, 1, 0:keys], stt[:, 5:6], None, ALU.mult))
                        dve.scalar_tensor_tensor(p[:, 0, 0:keys], p[:, 0, 0:keys], stt[:, 4:5], p[:, 1, 0:keys], ALU.mult, ALU.add)\
                            .then_inc(*T("mix_v", ("probs", v)))
                dve.wait_ge(*W("mix_a", "orms"))
                dve.reciprocal(inv8, rms8).then_inc(*T("mix_v", "oinverse"))
                for n in range(5):
                    if n < 4:
                        x = d_q[:, 2 * n:2 * n + 2, :].rearrange("p a t -> p (a t)")
                        dve.wait_ge(*W("product", ("obcast", n)))
                        dve.scalar_tensor_tensor(x, x, V["b_o_norm"], psum[n][:, :], ALU.mult, ALU.mult).then_inc(*T("mix_v", ("onormed", n)))
                    if n:
                        k = n - 1
                        dve.wait_ge(*W("mix_a", ("upper", k)))
                        for h in range(2 * k, 2 * k + 2):
                            dve.tensor_tensor(h_lo[:, h, 0:T1], d_q[:, h, :], h_hi[:, h, 0:T1].bitcast(F32), ALU.subtract).then_inc(*T("h_ready", h))

            def in_evac(name, l):
                def f(c, n):
                    bank = psum[bank_of(name, c, n)]
                    if c in (3, 5):
                        at = 0 if c == 3 else P
                        return dve.tensor_copy(g_v[:, :, at:at + P], bank[:, :].rearrange("p (t n) -> p t n", t=4))
                    return dve.tensor_copy(g_v[:, 2 * n:2 * n + 2, 256:512], bank[:, :].rearrange("p (t n) -> p t n", t=2))
                return f

            def y_evac(name, n_tok):
                def f(c, n):
                    return dve.tensor_copy(Y[:, 2 * c + n, 0:n_tok], psum[bank_of(name, c, n)][:, 0:n_tok])
                return f

            def attention(l):
                stage[0] = f"mix2.{l}"
                dve.wait_ge(*W("bias_in", l, at="load"))
                us = units(l)
                for u in range(len(us) + 3):
                    if u < len(us):
                        s, pair, qb = us[u]
                        k0, k1 = keys_of(s)
                        dve.wait_ge(*W("product", ("scores", u)))
                        if s == 0 and pair >= 3:
                            for x in range(2):
                                sc = psum[4 * (u % 2) + x][:, 0:T1]
                                ins = dve.tensor_tensor(sc, sc, g_bias[:, qb, 2 * pair + x - 6, :], ALU.add)
                            step(ins)
                        for x in range(2):
                            ins = dve.tensor_reduce(g_st[u % 2][:, x:x + 1], psum[4 * (u % 2) + x][:, 0:k1 - k0], AX.X, ALU.max, negate=True)
                        ins.then_inc(*T("mix_v", ("max", u)))
                    if 1 <= u <= len(us):
                        v = u - 1
                        k0, k1 = keys_of(us[v][0])
                        stt = g_st[v % 2]
                        dve.wait_ge(*W("mix_a", ("exp", v)))
                        step(dve.reciprocal(stt[:, 4:6], stt[:, 2:4]))
                        for x in range(2):
                            p = g_p[v % 3][:, x, 0:k1 - k0]
                            ins = dve.tensor_scalar(p, p, stt[:, 4 + x:5 + x], None, ALU.mult)
                        ins.then_inc(*T("mix_v", ("probs", v)))
                    if u >= 3:
                        v = u - 3
                        s, pair, qb = us[v]
                        cut = slice(T1 * s + P * qb, T1 * s + P * qb + P)
                        dve.wait_ge(*W("mix_a", ("upper", v)))
                        dve.tensor_tensor(h_lo[:, pair, cut], psum[6 + v % 2][:, 0:P], h_hi[:, pair, cut].bitcast(F32), ALU.subtract)\
                            .then_inc(*T("h_ready", v))

            def turn_out():
                stage[0] = "store"
                for t in range(2):
                    for q in range(2):
                        dve.wait_ge(*W("product", (t, q)))
                        ins = dve.tensor_copy(xo[:, t, 512 * q:512 * q + 512], psum[2 * t + q][:, :])
                    ins.then_inc(*T("out_tile", t))

            for s in range(SLOTS):
                dve.sem_inc(sem(f"raw_done{s}"), 1)
            for name, start in START.items():
                dve.sem_inc(sem(name), start)
            dve.memset(epsc, EPS)
            dve.memset(epsq, EPS * HD)
            dve.memset(epso, EPS / (1.0 - LAM_INIT) ** 2)
            dve.memset(onec, 1.0)
            dve.memset(zeroc, 0.0)
            dve.memset(cact, 0.0)
            dve.memset(ones, 1.0).then_inc(*T_at("ones_set", 0))
            turn_in()

            def start():
                angles()
                dve.wait_ge(*W("product", ("turned", ADA_START - 1)))
                mods_first(0, 2 * ADA_START, psum[4], 0)
                split_lo(0, SLOT)

            dve.wait_ge(*W("small_in", "all", at="load"))
            norm("norm0.0", T1, part1(0, 0), start)
            linear("mlstm", mlstm_evac, False)
            mlstm()
            linear("mlstm_out", residual("mlstm_out", 0, 0), True)
            norm("norm0.1", T1, part1(0, 1))
            moe(0)
            norm("norm1.0", T1, part1(1, 0))
            linear("diff", diff_evac, True, head_pipe("diff"))
            diff()
            linear("diff_out", residual("diff_out", 1, 0), True)
            norm("norm1.1", T1, part1(1, 1))
            moe(1)
            for l in range(DEPTH):
                both = l < DEPTH - 1
                n = T2 if both else T1
                norm(f"normffn{l}a", T2, part2(l, 0, 1))
                ffn(l, 0, True)
                post(f"post{l}.0", T2, l, 0)
                norm(f"normin{l}", T2, part2(l, 1, 1))
                linear(f"in{l}", in_evac(f"in{l}", l), True, head_pipe(f"in{l}"))
                attention(l)
                linear(f"attn_out{l}", y_evac(f"attn_out{l}", n), True)
                post(f"post{l}.1", n, l, 1)
                norm(f"normffn{l}b", n, part2(l, 2, both))
                ffn(l, 1, both)
                post(f"postffn{l}b", n, l, 2)
            turn_out()
    return log


def pack_columns(x):
    col = lambda v: np.asarray(v, np.float32).reshape(-1, P).T
    twice = lambda v: np.concatenate([np.asarray(v).reshape(-1, HD)] * 2, axis=1).T
    rows = lambda v: np.repeat(np.asarray(v).reshape(1, -1), P, axis=0)
    both = np.stack([np.asarray(x["c_2"]).reshape(KT, P), np.asarray(x["c_ctx_2"]).reshape(KT, P)], axis=1)
    parts = {"c1": col(x["c"]), "c2": both.reshape(2 * KT, P).T, "norm1": col(x["norm1"]), "norm2": col(x["norm2"]),
             "b_ada": col(x["b_ada"]), "a_h_norm": col(x["a_h_norm"]), "b_q_norm": twice(x["b_q_norm"]),
             "b_k_norm": twice(x["b_k_norm"]), "b_o_norm": col(x["b_o_norm"]), "b_ada_2": col(x["b_ada_2"]),
             "norm_g_2": col(x["norm_g_2"]), "qk_g_2": twice(x["qk_g_2"]), "conv_w_2": col(x["conv_w_2"]),
             "b_if": rows(x["a_b_if"]), "router_bias": rows(x["router_bias"])}
    return np.concatenate([parts[k] for k in COLS], axis=1)


def rpb_rows(rpb):
    out = np.full((DEPTH, 4, 64, 6, 4, 64), INVALID, np.float32)
    for r in range(4):
        for c in range(64):
            first = min(max(c - 8, 0), 48)
            for kr in range(4):
                out[:, r, c, :, kr, first:first + 16] = rpb[:, :, kr - r + 7, first - c + 15:first - c + 31]
    return out.reshape(DEPTH, 4, 64, 6, T1)


DIRECT = ["x", "ctx_2", "positions", "a_w_in", "a_w_out", "b_w_in", "b_w_out", "w_router",
          "b_lam_q1", "b_lam_k1", "b_lam_q2", "b_lam_k2", "moe_w_gu", "moe_w_down", "w_in_2", "w_o_2",
          "ffn_wi_2", "ffn_wo_2"]


def mod_weights(x):
    return {"w_ada_first": np.ascontiguousarray(x["w_ada"][0]),
            "w_mods": np.concatenate([x["w_ada"][1], x["w_ada_2"][0], x["w_ada_2"][1]], axis=1)}


def kernel(**inputs):
    import concourse.bacc as bacc
    from concourse.bass_utils import run_bass_kernel_spmd

    x = {k: np.asarray(v) for k, v in inputs.items()}
    arrays = {k: np.ascontiguousarray(x[k]) for k in DIRECT}
    arrays["consts"], arrays["consts2"] = host_consts()
    arrays["columns"] = np.ascontiguousarray(pack_columns(x))
    arrays["rpb_rows"] = rpb_rows(x["rpb_2"])
    arrays.update(mod_weights(x))

    def program(notes):
        nc = bacc.Bacc("TRN2", target_bir_lowering=False, num_devices=1)
        args = {k: nc.dram_tensor(f"in_{k}", a.shape, mybir.dt.from_np(a.dtype), kind="ExternalInput").ap()
                for k, a in arrays.items()}
        out = nc.dram_tensor("out_0", (1, T1, D), F32, kind="ExternalOutput").ap()
        return nc, build(nc, args, out, notes)

    _, notes = program(None)
    nc, _ = program(notes)
    r = run_bass_kernel_spmd(nc, [{f"in_{k}": a for k, a in arrays.items()}], core_ids=[0])
    return r.results[0]["out_0"]
```
